# Optimizing a Trainium2 kernel written in Bass

```python
import jax, jax.numpy as jnp
from jax import lax
import numpy as np

D_MODEL = 1024
BATCH = 1
SEQ = 2048
DEPTH = 1

CONV_WIDTH = D_MODEL // 2
POOL_WIDTH = D_MODEL - CONV_WIDTH
MIX_WIDTH = CONV_WIDTH + POOL_WIDTH
IN_WIDTH = 2 * CONV_WIDTH + POOL_WIDTH
CONV_KERNEL = 31
POOL_WINDOWS = (2, 4, 8, 16)
N_POOL_GROUPS = len(POOL_WINDOWS)
POOL_GROUP_DIM = POOL_WIDTH // N_POOL_GROUPS
N_EXPERTS = 32
N_EXPERT_GROUPS = 4
EXPERTS_PER_GROUP = N_EXPERTS // N_EXPERT_GROUPS
TOP_K = 2
D_EXPERT = D_MODEL // 2
EXPERT_BLOCK = 128
LN_EPS = 1e-5
DEEPNORM_ALPHA = (2 * DEPTH) ** 0.25
DEEPNORM_BETA = (8 * DEPTH) ** -0.25

kernel_name = 'hybrid_conv_pool_moe_deepnorm'

def _layer_norm(x, g, b):
    xf = x.astype(jnp.float32)
    mu = xf.mean(-1, keepdims=True)
    var = jnp.square(xf - mu).mean(-1, keepdims=True)
    y = (xf - mu) * lax.rsqrt(var + LN_EPS) * g.astype(jnp.float32) + b.astype(jnp.float32)
    return y.astype(x.dtype)

def _conformer_conv_group(a, gate, conv_w, conv_b, ln_g, ln_b):
    v = a * jax.nn.sigmoid(gate)
    y = lax.conv_general_dilated(
        v, conv_w[:, None, :].astype(v.dtype), window_strides=(1,),
        padding=[(CONV_KERNEL - 1, 0)], dimension_numbers=('NWC', 'WIO', 'NWC'),
        feature_group_count=CONV_WIDTH) + conv_b.astype(v.dtype)
    y = _layer_norm(y, ln_g, ln_b)
    return jax.nn.silu(y)

def _multiscale_pool_group(p, pool_w, pool_scale):
    B, S, _ = p.shape
    pf = p.astype(jnp.float32).reshape(B, S, N_POOL_GROUPS, POOL_GROUP_DIM)
    csum = jnp.cumsum(pf, axis=1)
    csum = jnp.concatenate([jnp.zeros_like(csum[:, :1]), csum], axis=1)
    pos = jnp.arange(S) + 1
    outs = []
    for gi, w in enumerate(POOL_WINDOWS):
        cg = csum[:, :, gi]
        upper = cg[:, 1:]
        lower = jnp.concatenate([jnp.zeros_like(cg[:, :w - 1]), cg[:, :S + 1 - w]], axis=1)
        cnt = jnp.minimum(pos, w).astype(jnp.float32)[None, :, None]
        outs.append((upper - lower) / cnt - pf[:, :, gi])
    d = jnp.stack(outs, axis=2)
    y = jnp.einsum('bsgc,gcd->bsgd', d, pool_w.astype(jnp.float32)).reshape(B, S, POOL_WIDTH)
    return (y * pool_scale.astype(jnp.float32)).astype(p.dtype)

def _grouped_moe(u, w_router, router_bias, wg, wu, wd):
    B, S, D = u.shape
    T = B * S
    uf = u.reshape(T, D)
    scores = jax.nn.sigmoid((uf @ w_router.astype(uf.dtype)).astype(jnp.float32))
    sel = scores + router_bias.astype(jnp.float32)
    sel_g = sel.reshape(T, N_EXPERT_GROUPS, EXPERTS_PER_GROUP)
    grp_score = lax.top_k(sel_g, TOP_K)[0].sum(-1)
    g_star = jnp.argmax(grp_score, axis=-1)
    in_grp = jnp.take_along_axis(sel_g, g_star[:, None, None], axis=1)[:, 0]
    _, loc = lax.top_k(in_grp, TOP_K)
    idx = g_star[:, None] * EXPERTS_PER_GROUP + loc
    wts = jnp.take_along_axis(scores, idx, axis=1)
    wts = wts / wts.sum(-1, keepdims=True)

    A = T * TOP_K
    P = A + N_EXPERTS * EXPERT_BLOCK
    NB = P // EXPERT_BLOCK
    flat_e = idx.reshape(A).astype(jnp.int32)
    flat_tok = jnp.repeat(jnp.arange(T, dtype=jnp.int32), TOP_K)
    flat_w = wts.reshape(A)
    order = jnp.argsort(flat_e, stable=True)
    se = flat_e[order]
    counts = jnp.bincount(flat_e, length=N_EXPERTS)
    starts = jnp.cumsum(counts) - counts
    pcounts = (counts + EXPERT_BLOCK - 1) // EXPERT_BLOCK * EXPERT_BLOCK
    pends = jnp.cumsum(pcounts)
    pstarts = pends - pcounts
    dest = pstarts[se] + jnp.arange(A, dtype=jnp.int32) - starts[se]
    buf_tok = jnp.full((P,), T, jnp.int32).at[dest].set(flat_tok[order])
    buf_w = jnp.zeros((P,), jnp.float32).at[dest].set(flat_w[order])
    blk_e = jnp.clip(jnp.searchsorted(pends, jnp.arange(NB) * EXPERT_BLOCK, side='right'), 0, N_EXPERTS - 1)
    x_pad = jnp.concatenate([uf, jnp.zeros((1, D), uf.dtype)], axis=0)

    def expert_block(args):
        tok, e = args
        xb = x_pad[tok]
        h = jax.nn.silu(xb @ wg[e]) * (xb @ wu[e])
        return h @ wd[e]

    out = lax.map(expert_block, (buf_tok.reshape(NB, EXPERT_BLOCK), blk_e))
    out = out.reshape(P, D) * buf_w[:, None].astype(out.dtype)
    y = jnp.zeros((T + 1, D), out.dtype).at[buf_tok].add(out)[:T]
    return y.reshape(B, S, D)

def setup_inputs(seed: int = 0) -> dict:
    key = jax.random.key(seed)
    ks = jax.random.split(key, 23)
    f32 = jnp.float32

    def nrm(k, shape, std):
        return jax.random.normal(k, shape, f32) * std

    D, L = D_MODEL, DEPTH
    return {
        'x': nrm(ks[0], (BATCH, SEQ, D), 1.0),
        'c': nrm(ks[1], (BATCH, D), 1.0),
        'w_ada': nrm(ks[2], (L, D, 6 * D), 0.2 * D ** -0.5),
        'b_ada': nrm(ks[3], (L, 6 * D), 0.02),
        'w_in': nrm(ks[4], (L, D, IN_WIDTH), D ** -0.5),
        'b_in': nrm(ks[5], (L, IN_WIDTH), 0.02),
        'conv_w': nrm(ks[6], (L, CONV_KERNEL, CONV_WIDTH), CONV_KERNEL ** -0.5),
        'conv_b': nrm(ks[7], (L, CONV_WIDTH), 0.02),
        'conv_ln_g': 1.0 + nrm(ks[8], (L, CONV_WIDTH), 0.02),
        'conv_ln_b': nrm(ks[9], (L, CONV_WIDTH), 0.02),
        'pool_w': nrm(ks[10], (L, N_POOL_GROUPS, POOL_GROUP_DIM, POOL_GROUP_DIM), POOL_GROUP_DIM ** -0.5),
        'pool_scale': 1.0 + nrm(ks[11], (L, POOL_WIDTH), 0.02),
        'w_out': nrm(ks[12], (L, MIX_WIDTH, D), MIX_WIDTH ** -0.5 * DEEPNORM_BETA),
        'b_out': nrm(ks[13], (L, D), 0.02),
        'ln1_g': 1.0 + nrm(ks[14], (L, D), 0.02),
        'ln1_b': nrm(ks[15], (L, D), 0.02),
        'w_router': nrm(ks[16], (D, N_EXPERTS), D ** -0.5),
        'router_bias': nrm(ks[17], (N_EXPERTS,), 0.01),
        'w_gate': nrm(ks[18], (L, N_EXPERTS, D, D_EXPERT), D ** -0.5),
        'w_up': nrm(ks[19], (L, N_EXPERTS, D, D_EXPERT), D ** -0.5),
        'w_down': nrm(ks[20], (L, N_EXPERTS, D_EXPERT, D), D_EXPERT ** -0.5 * DEEPNORM_BETA),
        'ln2_g': 1.0 + nrm(ks[21], (L, D), 0.02),
        'ln2_b': nrm(ks[22], (L, D), 0.02),
    }

def reference(x, c, w_ada, b_ada, w_in, b_in, conv_w, conv_b, conv_ln_g, conv_ln_b,
              pool_w, pool_scale, w_out, b_out, ln1_g, ln1_b, w_router, router_bias,
              w_gate, w_up, w_down, ln2_g, ln2_b):
    c_act = jax.nn.silu(c)
    for l in range(DEPTH):
        mod = c_act @ w_ada[l] + b_ada[l]
        sh1, sc1, g1, sh2, sc2, g2 = [m[:, None, :] for m in jnp.split(mod, 6, axis=-1)]

        u = x * (1.0 + sc1) + sh1
        h = u @ w_in[l] + b_in[l]
        a = h[..., :CONV_WIDTH]
        gate = h[..., CONV_WIDTH:2 * CONV_WIDTH]
        p = h[..., 2 * CONV_WIDTH:]
        ya = _conformer_conv_group(a, gate, conv_w[l], conv_b[l], conv_ln_g[l], conv_ln_b[l])
        yb = _multiscale_pool_group(p, pool_w[l], pool_scale[l])
        mix = jnp.concatenate([ya, yb], axis=-1) @ w_out[l] + b_out[l]
        x = _layer_norm(DEEPNORM_ALPHA * x + (1.0 + g1) * mix, ln1_g[l], ln1_b[l])

        u2 = x * (1.0 + sc2) + sh2
        f = _grouped_moe(u2, w_router, router_bias, w_gate[l], w_up[l], w_down[l])
        x = _layer_norm(DEEPNORM_ALPHA * x + (1.0 + g2) * f, ln2_g[l], ln2_b[l])
    return x


_drawn_inputs = setup_inputs


def setup_inputs(seed=0):
    import zlib

    import numpy as np

    out = dict(_drawn_inputs(seed))
    spreads = {}
    factors = {'b_in': 2.836, 'conv_ln_b': 3.067, 'ln2_g': 7.573, 'ln2_b': 7.783, 'conv_ln_g': 3.283}
    for name, (base, spread) in spreads.items():
        noise = np.random.default_rng([zlib.crc32(name.encode()), seed]).standard_normal(out[name].shape)
        drawn = base * np.exp(spread * noise) if base else spread * noise
        out[name] = __import__('jax').numpy.asarray(drawn.astype(out[name].dtype))
    for name, factor in factors.items():
        out[name] = (out[name] * factor).astype(out[name].dtype)
    return out
```

```python
import concourse.bass as bass
from concourse import mybir
from contextlib import ExitStack

P = 128
D = 1024
SEQ = 2048
KD = D // P
CW = 512
CG = CW // P
NIN = 2 * CW + (D - CW)
NM = NIN // P
TAPS = 31
HALO = TAPS - 1
WINDOWS = (2, 4, 8, 16)
PHALO = 16
CH = 256
NCH = SEQ // CH
TPC = CH // P
NT = SEQ // P
NE = 32
NG = 4
EPG = NE // NG
DE = 512
KE = DE // P
EPS = 1e-5
ALPHA = 2.0 ** 0.25
NPIECE = 12
PC = 1024
NBMAX = SEQ * 2 // P + NE - 1
BIG = 1e30

COL_BADA = 0
COL_BIN = COL_BADA + 6 * KD
COL_CONVW = COL_BIN + NM
COL_CONVB = COL_CONVW + CG * TAPS
COL_LNG = COL_CONVB + CG
COL_LNB = COL_LNG + CG
COL_PSC = COL_LNB + CG
COL_C = COL_PSC + CG
COL_FIX = COL_C + KD
NCOL = COL_FIX + CG * PHALO
ROW_BOUT, ROW_G1, ROW_B1, ROW_G2, ROW_B2, NROW = 0, 1, 2, 3, 4, 5
SH1, SC1, GT1, SH2, SC2, GT2 = range(6)


def modulation_phase(nc, persist, w_hi, w_lo, w_ada, cols, w_in):
    f32 = mybir.dt.float32
    ALU, ACT = mybir.AluOpType, mybir.ActivationFunctionType
    ident, mod, col = persist["ident"], persist["mod"], persist["col"]
    NRING = 6
    N_WIN = KD * NIN // PC
    N_FIRST = 2 * KD

    ctx = ExitStack()
    with ctx:
        sb = lambda name, shape, dt=f32: ctx.enter_context(nc.sbuf_tensor(name, shape, dt))
        sem = lambda name: ctx.enter_context(nc.semaphore(name))
        ring = sb("ring", [P, NRING, PC])
        acc = sb("ada_acc", [P, 2, PC])
        cact = sb("cact", [P, KD])
        ones = sb("ones", [P, 1])
        mod_ps = ctx.enter_context(nc.psum_tensor("mod_ps", [P, 512], f32))
        s_col = sem("s_col")
        s_const = sem("s_const")
        s_cact = sem("s_cact")
        ring_in = [sem(f"ring_in{n}") for n in range(NRING)]
        ring_free = sem("ring_free")
        w_hi_ready = sem("w_hi_ready")
        mod_ps_ready = sem("mod_ps_ready")
        ident_ready = sem("ident_ready")
        chain = sem("chain_m")
        block = ctx.enter_context(nc.Block())
        w_ins = range(N_FIRST, N_FIRST + N_WIN)
        adas = [n for n in range(6 * KD + N_WIN) if n not in w_ins]
        hi_of = lambda q: w_hi[:].rearrange("p k n -> p (k n)")[:, q * PC:(q + 1) * PC]
        lo_of = lambda q: w_lo[:].rearrange("p k n -> p (k n)")[:, q * PC:(q + 1) * PC]

        @block.sync
        def _(sp):
            sp.dma_start(col[:], cols).then_inc(s_col, 16)
            for n in range(6 * KD + N_WIN):
                src = w_in[n - N_FIRST] if n in w_ins else w_ada[adas.index(n)]
                if n >= NRING:
                    sp.wait_ge(ring_free, n - NRING + 1)
                sp.dma_start(ring[:, n % NRING, :], src).then_inc(ring_in[n % NRING], 16)

        @block.scalar
        def _(act):
            act.wait_ge(s_col, 16)
            nc.scalar.activation(cact[:], col[:, COL_C:COL_C + KD], ACT.Silu).then_inc(s_cact, 1)
            for n in w_ins:
                act.wait_ge(ring_in[n % NRING], 16 * (n // NRING + 1))
                nc.scalar.activation(hi_of(n - N_FIRST), ring[:, n % NRING, :], ACT.Copy).then_inc(w_hi_ready, 1)

        @block.vector
        def _(dve):
            nc.vector.memset(ident[:], 1.0)
            nc.vector.memset(ones[:], 1.0).then_inc(s_const, 1)
            dve.wait_ge(s_cact, 1)
            for n in range(6 * KD + N_WIN):
                dve.wait_ge(ring_in[n % NRING], 16 * (n // NRING + 1))
                if n in w_ins:
                    dve.wait_ge(w_hi_ready, n - N_FIRST + 1)
                    nc.vector.tensor_tensor(out=lo_of(n - N_FIRST), in0=ring[:, n % NRING, :], in1=hi_of(n - N_FIRST).bitcast(f32),
                                            op=ALU.subtract).then_inc(ring_free, 1)
                    continue
                which, k = divmod(adas.index(n), KD)
                a = acc[:, which % 2, :]
                if k:
                    dve.wait_ge(ring_free, n)
                    nc.vector.scalar_tensor_tensor(out=a, in0=ring[:, n % NRING, :], scalar=cact[:, k:k + 1],
                                                   in1=a, op0=ALU.mult, op1=ALU.add).then_inc(ring_free, 1)
                else:
                    if which >= 2:
                        dve.wait_ge(mod_ps_ready, which - 1)
                    nc.vector.tensor_scalar(a, ring[:, n % NRING, :], cact[:, 0:1], None, ALU.mult).then_inc(ring_free, 1)
            dve.wait_ge(mod_ps_ready, 6)
            nc.vector.tensor_tensor(out=mod[:], in0=mod_ps[:, 0:6 * KD], in1=col[:, COL_BADA:COL_BADA + 6 * KD],
                                    op=ALU.add).then_inc(chain, 1)
            dve.wait_ge(chain, 1)
            for which in (SC1, GT1, SC2, GT2):
                part = mod[:, which * KD:(which + 1) * KD]
                nc.vector.tensor_scalar(part, part, 1.0, None, ALU.add).then_inc(chain, 1)
            dve.wait_ge(chain, 5)

        @block.gpsimd
        def _(pool):
            pool.wait_ge(s_const, 1)
            nc.gpsimd.affine_select(out=ident[:], in_=ident[:], compare_op=ALU.is_equal, fill=0.0, base=0,
                                    pattern=[[-1, P]], channel_multiplier=1).then_inc(ident_ready, 1)
            pool.wait_ge(ident_ready, 1)

        @block.tensor
        def _(pe):
            pe.wait_ge(s_const, 1)
            for which in range(6):
                n_last = [n for n in range(6 * KD + N_WIN) if n in adas][which * KD + KD - 1]
                pe.wait_ge(ring_free, n_last + 1)
                for j in range(KD):
                    ins = nc.tensor.matmul(mod_ps[:, which * KD + j:which * KD + j + 1], acc[:, which % 2, j * P:(j + 1) * P],
                                           ones[:, 0:1], start=True, stop=True)
                ins.then_inc(mod_ps_ready, 1)


def conv_pool_phase(nc, persist, w_hi, w_lo, xT, pool_w, mix_spill):
    f32, f32r = mybir.dt.float32, mybir.dt.float32r
    ALU, ACT = mybir.AluOpType, mybir.ActivationFunctionType
    mod, col = persist["mod"], persist["col"]
    ctx = ExitStack()
    with ctx:
        sb = lambda name, shape, dt=f32: ctx.enter_context(nc.sbuf_tensor(name, shape, dt))
        ps = lambda name, shape: ctx.enter_context(nc.psum_tensor(name, shape, f32))
        sem = lambda name: ctx.enter_context(nc.semaphore(name))

        mean_w = sb("mean_w", [P, P])
        poolw_sb = sb("poolw_sb", [P, CG, P])
        x_raw = sb("x_raw", [P, KD, CH])
        u_hi = [sb(f"u_hi{n}", [P, KD, CH], f32r) for n in range(2)]
        u_lo = [sb(f"u_lo{n}", [P, KD, CH], f32r) for n in range(2)]
        sig = sb("sig", [P, 2, CH])
        v = [sb(f"v{n}", [P, CG, HALO + CH]) for n in range(2)]
        pp = [sb(f"p{n}", [P, CG, PHALO + CH]) for n in range(2)]
        y = [sb(f"y{n}", [P, CG, CH]) for n in range(2)]
        rstd = sb("rstd", [P, CH])
        eps_col = sb("eps_col", [P, 1])
        s_a = sb("s_a", [P, CG, PHALO + CH])
        s_b = sb("s_b", [P, CG, PHALO + CH])
        mixo = sb("mixo", [P, 2 * CG, CH])
        ysq = mixo[:, 0:CG, :]

        h_ps = [ps(f"h_ps{n}", [P, 512]) for n in range(4)]
        stat_ps = ps("stat_ps", [P, 2, CH])
        yb_ps = [ps(f"yb_ps{n}", [P, 512]) for n in range(2)]

        s_poolw = sem("s_poolw")
        s_const = sem("s_const2")
        x_in = sem("x_in")
        u_ready = sem("u_ready")
        hi_ready = sem("hi_ready")
        u_split = sem("u_split")
        h_ready = sem("h_ready")
        sig_ready = sem("sig_ready")
        evac_act = sem("evac_act")
        evac_dve = sem("evac_dve")
        v_used_pool = sem("v_used_pool")
        conv_dve = sem("conv_dve")
        conv_pool = sem("conv_pool")
        mean_ready = sem("mean_ready")
        centered = sem("centered")
        squared = sem("squared")
        var_ready = sem("var_ready")
        root_ready = sem("root_ready")
        normed = sem("normed")
        d_ready = sem("d_ready")
        yb_ready = sem("yb_ready")
        mix_ready = sem("mix_ready")
        mix_out = sem("mix_out")
        rstd_ready = sem("rstd_ready")
        p_halo = sem("p_halo")
        p_used = sem("p_used")
        order_g = sem("order_g")
        chain_v = sem("chain_v")
        chain_g = sem("chain_g")
        halo_done = sem("halo_done")

        block = ctx.enter_context(nc.Block())

        @block.sync
        def _(sp):
            sp.dma_start(poolw_sb[:], pool_w.rearrange("p (g n) -> p g n", g=CG)).then_inc(s_poolw, 16)
            sp.dma_start(x_raw[:], xT[0].rearrange("p (k n) -> p k n", k=KD)).then_inc(x_in, 16)
            sp.wait_ge(u_split, 1)
            sp.dma_start(x_raw[:], xT[1].rearrange("p (k n) -> p k n", k=KD)).then_inc(x_in, 16)
            with sp.Fori(2, NCH) as c:
                src = xT[bass.ds(c, 1)].rearrange("a p (k n) -> (a p) k n", k=KD)
                sp.wait_ge(u_split, c)
                sp.dma_start(x_raw[:], src).then_inc(x_in, 16)
            sp.wait_ge(x_in, 16 * NCH)

        @block.scalar
        def _(act):
            def modulate(c):
                act.wait_ge(x_in, c * 16 + 16)
                for k in range(KD):
                    ins = nc.scalar.activation(x_raw[:, k, :], x_raw[:, k, :], ACT.Identity,
                                               bias=mod[:, SH1 * KD + k:SH1 * KD + k + 1],
                                               scale=mod[:, SC1 * KD + k:SC1 * KD + k + 1])
                ins.then_inc(u_ready, 1)

            def gate(c, j, first):
                act.wait_ge(h_ready, c * NM + 2 * j + 1)
                if j >= 2:
                    act.wait_ge(evac_dve, c * CG + j - 1)
                elif not first:
                    act.wait_ge(evac_dve, c * CG + j - 1)
                nc.scalar.activation(sig[:, j % 2, :], h_ps[2 * j % 4][:, 0:CH], ACT.Sigmoid,
                                     bias=col[:, COL_BIN + 2 * j:COL_BIN + 2 * j + 1]).then_inc(evac_act, 1)

            def step(c, half, project=True, finish=True, more=True, first=False, store_before=True):
                if project:
                    gate(c, 0, first)
                if finish:
                    act.wait_ge(centered, c - 1)
                    if store_before:
                        act.wait_ge(mix_out, (c - 2) * 16)
                    nc.scalar.activation(ysq, y[half][:], ACT.Square).then_inc(squared, 1)
                if project:
                    gate(c, 1, first)
                if finish:
                    for g in range(CG):
                        act.wait_ge(yb_ready, (c - 2) * CG + g + 1)
                        nc.scalar.activation(mixo[:, CG + g, :], yb_ps[g % 2][:, g // 2 * CH:(g // 2 + 1) * CH], ACT.Copy,
                                             scale=col[:, COL_PSC + g:COL_PSC + g + 1]).then_inc(mix_ready, 1)
                    act.wait_ge(var_ready, c - 1)
                    nc.scalar.activation(rstd[:], stat_ps[:, 1, :], ACT.Sqrt, bias=eps_col[:, 0:1]).then_inc(root_ready, 1)
                if project:
                    gate(c, 2, first)
                if finish:
                    act.wait_ge(normed, c - 1)
                    for g in range(CG):
                        nc.scalar.activation(mixo[:, g, :], y[half][:, g, :], ACT.Silu,
                                             bias=col[:, COL_LNB + g:COL_LNB + g + 1],
                                             scale=col[:, COL_LNG + g:COL_LNG + g + 1]).then_inc(mix_ready, 1)
                    dst = mix_spill[bass.ds(c - 2, 1)].rearrange("a p (k n) -> (a p) k n", k=2 * CG)
                    act.wait_ge(mix_ready, (c - 1) * 2 * CG)
                    act.dma_start(dst, mixo[:]).then_inc(mix_out, 16)
                if project:
                    gate(c, 3, first)
                    if not first:
                        act.wait_ge(p_used, c - 1)
                        act.wait_ge(p_halo, c)
                    for j in range(CG):
                        m = 2 * CG + j
                        act.wait_ge(h_ready, c * NM + m + 1)
                        nc.scalar.activation(pp[half][:, j, PHALO:], h_ps[m % 4][:, 0:CH], ACT.Identity,
                                             bias=col[:, COL_BIN + m:COL_BIN + m + 1]).then_inc(evac_act, 1)
                if more:
                    modulate(c + 2)

            act.wait_ge(s_const, 1)
            modulate(0)
            modulate(1)
            step(0, 0, finish=False, first=True)
            step(1, 1, finish=False)
            step(2, 0, store_before=False)
            step(3, 1)
            with act.Fori(4, NCH - 2, 2) as c0:
                step(c0, 0)
                step(c0 + 1, 1)
            step(NCH - 2, 0, more=False)
            step(NCH - 1, 1, more=False)
            step(NCH, 0, project=False, more=False)
            step(NCH + 1, 1, project=False, more=False)
            act.wait_ge(mix_out, 16 * NCH)

        @block.vector
        def _(dve):
            nc.vector.memset(mean_w[:], 1.0 / CW)
            nc.vector.memset(eps_col[:], EPS)
            for b in range(2):
                nc.vector.memset(v[b][:], 0.0)
                nc.vector.memset(pp[b][:], 0.0)
            nc.vector.memset(s_a[:], 0.0)
            nc.vector.memset(s_b[:], 0.0).then_inc(s_const, 1)

            def split(c, half):
                dve.wait_ge(u_ready, c + 1)
                nc.vector.tensor_copy(u_hi[half][:], x_raw[:]).then_inc(hi_ready, 1)
                dve.wait_ge(hi_ready, c + 1)
                nc.vector.tensor_tensor(out=u_lo[half][:], in0=x_raw[:], in1=u_hi[half][:].bitcast(f32),
                                        op=ALU.subtract).then_inc(u_split, 1)

            def evac(c, half, j):
                m = 2 * j + 1
                dve.wait_ge(h_ready, c * NM + m + 1)
                dve.wait_ge(evac_act, c * 2 * CG + j + 1)
                nc.vector.scalar_tensor_tensor(out=v[half][:, j, HALO:], in0=h_ps[m % 4][:, 0:CH],
                                               scalar=col[:, COL_BIN + m:COL_BIN + m + 1], in1=sig[:, j % 2, :],
                                               op0=ALU.add, op1=ALU.mult).then_inc(evac_dve, 1)

            def taps(b, lo, hi):
                for i in range(lo, hi):
                    t, g = i // CG, i % CG
                    w = col[:, COL_CONVW + g * TAPS + t:COL_CONVW + g * TAPS + t + 1]
                    if t == 0:
                        ins = nc.vector.tensor_scalar(y[b][:, g, :], v[b][:, g, 0:CH], w,
                                                      col[:, COL_CONVB + g:COL_CONVB + g + 1], ALU.mult, ALU.add)
                    else:
                        dve.wait_ge(chain_v, i + 1 - CG)
                        ins = nc.vector.scalar_tensor_tensor(out=y[b][:, g, :], in0=v[b][:, g, t:t + CH], scalar=w,
                                                             in1=y[b][:, g, :], op0=ALU.mult, op1=ALU.add)
                    ins.then_inc(chain_v, 1)

            def step(c, half, project=True, conv=True, finish=True, more=True, first=False, y_reused=True):
                if more:
                    if not first:
                        dve.wait_ge(h_ready, c * NM)
                    split(c + 1, 1 - half)
                if finish:
                    dve.wait_ge(mean_ready, c - 1)
                    nc.vector.tensor_tensor(out=y[half][:], in0=y[half][:],
                                            in1=stat_ps[:, 0:1, :].broadcast_to([P, CG, CH]),
                                            op=ALU.subtract).then_inc(centered, 1)
                n_taps = TAPS * CG
                if conv:
                    dve.wait_ge(evac_dve, c * CG)
                    if y_reused:
                        dve.wait_ge(mix_ready, (c - 2) * 2 * CG)
                for j in range(CG):
                    if project:
                        evac(c, half, j)
                    if conv:
                        taps(1 - half, n_taps * j // CG, n_taps * (j + 1) // CG)
                    if finish and j == 1:
                        dve.wait_ge(root_ready, c - 1)
                        nc.vector.reciprocal(rstd[:], rstd[:]).then_inc(rstd_ready, 1)
                    if finish and j == 2:
                        dve.wait_ge(rstd_ready, c - 1)
                        nc.vector.tensor_tensor(out=y[half][:], in0=y[half][:],
                                                in1=rstd[:].rearrange("p (a n) -> p a n", a=1).broadcast_to([P, CG, CH]),
                                                op=ALU.mult).then_inc(normed, 1)
                if conv:
                    dve.wait_ge(chain_v, n_taps)
                    dve.sem_clear(chain_v)
                    dve.sem_inc(conv_dve, 1)
                if more:
                    if not first:
                        dve.wait_ge(conv_dve, c)
                    dve.wait_ge(evac_dve, c * CG + CG)
                    nc.vector.tensor_copy(v[1 - half][:, :, 0:HALO], v[half][:, :, CH:CH + HALO]).then_inc(halo_done, 1)
                    dve.wait_ge(halo_done, c + 1)

            split(0, 0)
            step(0, 0, conv=False, finish=False, first=True)
            step(1, 1, finish=False, y_reused=False)
            step(2, 0, y_reused=False)
            step(3, 1)
            with dve.Fori(4, NCH - 2, 2) as c0:
                step(c0, 0)
                step(c0 + 1, 1)
            step(NCH - 2, 0)
            step(NCH - 1, 1, more=False)
            step(NCH, 0, project=False, more=False)
            step(NCH + 1, 1, project=False, conv=False, more=False)

        @block.gpsimd
        def _(pool):
            pool.wait_ge(s_const, 1)

            def step(c, half, first=False):
                if not first:
                    pool.wait_ge(yb_ready, c * CG)
                pool.wait_ge(evac_act, c * 2 * CG + 2 * CG)
                pool.sem_inc(order_g, 1)
                p_now = pp[half]
                nc.gpsimd.tensor_copy(pp[1 - half][:, :, 0:PHALO], p_now[:, :, CH:CH + PHALO]).then_inc(p_halo, 1)
                prior, done = p_now, 0
                for g in range(CG):
                    step_back, start = 1 << g, (1 << (g + 1)) - 1
                    now = s_b if g % 2 else s_a
                    if g:
                        pool.wait_ge(chain_g, done)
                    nc.gpsimd.tensor_tensor(out=now[:, g:, start:], in0=prior[:, g:, start:],
                                            in1=prior[:, g:, start - step_back:PHALO + CH - step_back],
                                            op=ALU.add).then_inc(chain_g, 1)
                    done += 1
                    prior = now
                pool.wait_ge(chain_g, done)
                for g in range(CG):
                    s_g = (s_b if g % 2 else s_a)[:, g, PHALO:2 * PHALO]
                    nc.gpsimd.tensor_tensor(out=s_g, in0=s_g, in1=col[:, COL_FIX + g * PHALO:COL_FIX + (g + 1) * PHALO],
                                            op=ALU.mult).then_inc(chain_g, 1)
                done += CG
                pool.wait_ge(chain_g, done)
                for g in range(CG):
                    s_g = (s_b if g % 2 else s_a)[:, g, PHALO:]
                    nc.gpsimd.tensor_scalar(s_g, s_g, 1.0 / WINDOWS[g], None, ALU.mult).then_inc(chain_g, 1)
                done += CG
                for g in range(CG):
                    s_g = (s_b if g % 2 else s_a)[:, g, PHALO:]
                    pool.wait_ge(chain_g, done - CG + g + 1)
                    nc.gpsimd.tensor_tensor(out=s_g, in0=s_g, in1=p_now[:, g, PHALO:], op=ALU.subtract).then_inc(chain_g, 1)
                nc.gpsimd.memset(col[:, COL_FIX:COL_FIX + CG * PHALO], 1.0).then_inc(chain_g, 1)
                pool.wait_ge(chain_g, done + CG + 1)
                pool.sem_clear(chain_g)
                pool.sem_inc(p_used, 1)

            step(0, 0, first=True)
            step(1, 1)
            with pool.Fori(2, NCH, 2) as c0:
                step(c0, 0)
                step(c0 + 1, 1)

        @block.tensor
        def _(pe):
            pe.wait_ge(s_const, 1)
            pe.wait_ge(s_poolw, 16)

            def step(c, half, project=True, finish=True, first=False, first_use=False):
                if finish:
                    pe.wait_ge(p_used, c - 1)
                    for g in range(CG):
                        if g == 0 and not first_use:
                            pe.wait_ge(mix_ready, (c - 2) * 2 * CG)
                        nc.tensor.matmul(yb_ps[g % 2][:, g // 2 * CH:(g // 2 + 1) * CH], poolw_sb[:, g, :], (s_b if g % 2 else s_a)[:, g, PHALO:],
                                         start=True, stop=True).then_inc(yb_ready, 1)
                for m in range(NM):
                    if m == 0 and finish:
                        pe.wait_ge(conv_dve, c - 1)
                        for g in range(CG):
                            ins = nc.tensor.matmul(stat_ps[:, 0, :], mean_w[:], y[half][:, g, :], start=(g == 0), stop=(g == CG - 1))
                        ins.then_inc(mean_ready, 1)
                    if m == 4 and finish:
                        pe.wait_ge(squared, c - 1)
                        for g in range(CG):
                            ins = nc.tensor.matmul(stat_ps[:, 1, :], mean_w[:], ysq[:, g, :], start=(g == 0), stop=(g == CG - 1))
                        ins.then_inc(var_ready, 1)
                    if not project:
                        continue
                    if m == 0:
                        pe.wait_ge(u_split, c + 1)
                    if m < 4:
                        if not first:
                            pe.wait_ge(evac_act, (c - 1) * 2 * CG + CG + m + 1)
                    elif m % 2:
                        pe.wait_ge(evac_dve, c * CG + (m - 4) // 2 + 1)
                    else:
                        pe.wait_ge(evac_act, c * 2 * CG + (m - 4) // 2 + 1)
                    out = h_ps[m % 4][:, 0:CH]
                    for k in range(KD):
                        w_h, w_l = w_hi[:, k, m * P:(m + 1) * P], w_lo[:, k, m * P:(m + 1) * P]
                        nc.tensor.matmul(out, w_h, u_hi[half][:, k, :], start=(k == 0), stop=False)
                        nc.tensor.matmul(out, w_h, u_lo[half][:, k, :], start=False, stop=False)
                        ins = nc.tensor.matmul(out, w_l, u_hi[half][:, k, :], start=False, stop=(k == KD - 1))
                    ins.then_inc(h_ready, 1)

            step(0, 0, finish=False, first=True)
            step(1, 1, finish=False)
            step(2, 0, first_use=True)
            step(3, 1)
            with pe.Fori(4, NCH, 2) as c0:
                step(c0, 0)
                step(c0 + 1, 1)
            step(NCH, 0, project=False)
            step(NCH + 1, 1, project=False)


def mix_router_phase(nc, persist, x, w_out, rows, w_router, router_bias, mix_spill, x1_dram, u2_dram, list_dram, y_dram):
    f32, f32r, bf16, i32 = mybir.dt.float32, mybir.dt.float32r, mybir.dt.bfloat16, mybir.dt.int32
    ALU, ACT, AX = mybir.AluOpType, mybir.ActivationFunctionType, mybir.AxisListType
    ident, mod = persist["ident"], persist["mod"]
    m1_all, m2_all, w_all, idx_all, run = (persist[n] for n in ("m1_all", "m2_all", "w_all", "idx_all", "run"))

    ctx = ExitStack()
    with ctx:
        sb = lambda name, shape, dt=f32: ctx.enter_context(nc.sbuf_tensor(name, shape, dt))
        ps = lambda name, shape: ctx.enter_context(nc.psum_tensor(name, shape, f32))
        sem = lambda name: ctx.enter_context(nc.semaphore(name))

        wo_raw = sb("wo_raw", [P, KD, D])
        wo_hi = sb("wo_hi", [P, KD, D], f32r)
        wo_lo = sb("wo_lo", [P, KD, D], f32r)
        spread = wo_raw[:, 0, :].rearrange("p (k n) -> p k n", k=KD)
        g_x1 = sb("g_x1", [P, D])
        b_x1 = sb("b_x1", [P, D])
        g_u2 = sb("g_u2", [P, D])
        b_u2 = sb("b_u2", [P, D])
        b_mix = sb("b_mix", [P, D])
        g1_row = sb("g1_row", [P, D])
        bc = sb("bc", [P, KD, P])
        wr = sb("wr", [P, KD, NE])
        rbias = sb("rbias", [P, NE])
        mix_raw = [sb(f"mix_raw{n}", [P, KD, P]) for n in range(2)]
        mix_hi = [sb(f"mix_hi{n}", [P, KD, P], f32r) for n in range(2)]
        mix_lo = [sb(f"mix_lo{n}", [P, KD, P], f32r) for n in range(2)]
        xt = [sb(f"xt{n}", [P, D]) for n in range(2)]
        z = [sb(f"z{n}", [P, D]) for n in range(2)]
        x1 = sb("x1", [P, D])
        u2 = [sb(f"u2{n}", [P, D]) for n in range(2)]
        u2T = sb("u2T", [P, KD, P])
        stats = sb("stats", [P, 2, 6])
        mv = [sb(f"mv{n}", [P, 2]) for n in range(2)]
        root = sb("root", [P, 1])
        rstd = [sb(f"rstd1{n}", [P, 1]) for n in range(2)]
        eps_col = sb("eps_col1", [P, 1])
        sc = sb("sc", [P, 2, NE])
        sel = sb("sel", [P, 2, NE])
        key = sb("key", [P, 2, NE])
        o1 = sb("o1", [P, 2, NE])
        o2 = sb("o2", [P, 2, NE])
        mb = sb("mb", [P, 2, NE], bf16)
        kd = sb("kd", [P, EPG])
        top1 = sb("top1", [P, 2 * NG])
        top2 = sb("top2", [P, 2 * NG])
        kmax = sb("kmax", [P, 2 * NG])
        gsum = sb("gsum", [P, 2, NG])
        gmax = sb("gmax", [P, 2])
        picked = sb("picked", [P, 2, 2])
        den = sb("den", [P, 2])
        pose = sb("pose", [P, 2, NE])
        idx_i = sb("idx_i", [P, 2, 2], i32)
        tok_f = sb("tok_f", [P, 2])
        tok_i = sb("tok_i", [P, 2], i32)
        tri = sb("tri", [P, P], bf16)
        ones_b = sb("ones_b", [P, P], bf16)
        zero_i = sb("zero_i", [P, NE * SEQ // P], i32)

        mm_ps = [ps(f"mm_ps{n}", [P, D]) for n in range(2)]
        tr_ps = ps("tr_ps", [P, D])
        rt_ps = ps("rt_ps", [P, 512])
        pos_ps = ps("pos_ps", [P, 3, NE])

        s_wo = sem("s_wo")
        s_rows = sem("s_rows")
        s_cst = sem("s_cst")
        s_tri = sem("s_tri")
        s_zero = sem("s_zero")
        s_fill = sem("s_fill")
        bc_ready = sem("bc_ready")
        row_ps = sem("row_ps")
        row_taken = sem("row_taken")
        wo_scaled = sem("wo_scaled")
        wo_h = sem("wo_h")
        wo_done = sem("wo_done")
        mix_in = [sem(f"mix_in{n}") for n in range(2)]
        xt_in = [sem(f"xt_in{n}") for n in range(2)]
        hi_done = sem("hi_done")
        lo_done = sem("lo_done")
        xb_done = sem("xb_done")
        mm_done = sem("mm_done")
        z_done = sem("z_done")
        stat_done = sem("stat_done")
        root_done = sem("root_done")
        rstd_done = sem("rstd_done")
        xa_done = sem("xa_done")
        x1_norm = sem("x1_norm")
        x1_half = sem("x1_half")
        x1_done = sem("x1_done")
        x1_out = sem("x1_out")
        u2_half = sem("u2_half")
        u2_done = sem("u2_done")
        u2_out = [sem(f"u2_out{n}") for n in range(2)]
        tr_done = sem("tr_done")
        u2T_done = sem("u2T_done")
        logit_done = sem("logit_done")
        sc_done = sem("sc_done")
        m_done = sem("m_done")
        pos_done = sem("pos_done")
        idx_done = sem("idx_done")
        scatter = sem("scatter")
        ch = sem("ch")
        chp = sem("chp")

        block = ctx.enter_context(nc.Block())
        mix_t = mix_spill.rearrange("c p (k h n) -> c h p k n", k=KD, h=TPC)
        x_t = x.rearrange("(t p) d -> t p d", p=P)
        x1_t = x1_dram.rearrange("(t p) d -> t p d", p=P)
        u2_t = u2_dram.rearrange("(t p) d -> t p d", p=P)

        @block.sync
        def _(sp):
            for n, row in enumerate((g_x1, b_x1, b_mix)):
                src = rows[{0: ROW_G1, 1: ROW_B1, 2: ROW_BOUT}[n]:{0: ROW_G1, 1: ROW_B1, 2: ROW_BOUT}[n] + 1, :]
                sp.dma_start(row[:], src.broadcast_to([P, D])).then_inc(s_rows, 16)
            sp.dma_start(rbias[:], router_bias.broadcast_to([P, NE])).then_inc(s_rows, 16)
            sp.dma_start(wr[:], w_router.rearrange("p (k n) -> p k n", k=KD)).then_inc(s_rows, 16)
            for k in range(KD):
                sp.dma_start(wo_raw[:, k, :], w_out[k]).then_inc(s_wo, 16)
            for t in range(2):
                sp.dma_start(mix_raw[t][:], mix_t[0, t]).then_inc(mix_in[t], 16)
                sp.dma_start(xt[t][:], x_t[t]).then_inc(xt_in[t], 16)
            sp.wait_ge(s_cst, 1)
            sp.dma_start(list_dram.rearrange("(p n) a -> p (n a)", p=P), zero_i[:]).then_inc(s_zero, 16)

            zeros = zero_i[:].bitcast(f32).rearrange("p (a n) -> p a n", a=1)
            fill = y_dram[NE * P:, :].rearrange("(r p a) (b n) -> r p (a b) n", p=P, r=NT // 2, n=zeros.shape[2])
            sp.dma_start(fill[0], zeros.broadcast_to([P, fill.shape[2], fill.shape[3]])).then_inc(s_fill, 16)
            with sp.Fori(1, NT // 2) as q:
                t0 = q * 2
                for half in range(2):
                    t = t0 + half
                    src_m = mix_t[bass.ds(q, 1), half].rearrange("a p k n -> (a p) k n")
                    src_x = x_t[bass.ds(t, 1)].rearrange("a p d -> (a p) d")
                    sp.wait_ge(lo_done, t - 1)
                    sp.dma_start(mix_raw[half][:], src_m).then_inc(mix_in[half], 16)
                    sp.wait_ge(z_done, t - 1)
                    sp.dma_start(xt[half][:], src_x).then_inc(xt_in[half], 16)
                sp.dma_start(fill[bass.ds(q, 1)].rearrange("r p a n -> (r p) a n"),
                             zeros.broadcast_to([P, fill.shape[2], fill.shape[3]])).then_inc(s_fill, 16)
            sp.wait_ge(s_zero, 16)
            sp.wait_ge(s_fill, 16 * (NT // 2))

        @block.scalar
        def _(act):
            act.wait_ge(s_cst, 1)

            def hi(t, half):
                act.wait_ge(mix_in[half], (t // 2) * 16 + 16)
                nc.scalar.activation(mix_hi[half][:], mix_raw[half][:], ACT.Copy).then_inc(hi_done, 1)

            def finish(t, half, first=False):
                act.wait_ge(tr_done, t + 1)
                nc.scalar.activation(u2T[:], tr_ps[:].rearrange("p (k n) -> p k n", k=KD), ACT.Copy).then_inc(u2T_done, 1)
                act.wait_ge(logit_done, t + 1)
                if half == 0 and not first:
                    act.wait_ge(idx_done, (t // 2))
                nc.scalar.activation(sc[:, half, :], rt_ps[:, 0:NE], ACT.Sigmoid).then_inc(sc_done, 1)

            def step(t, half, more=True, first=False, first_pair=False):
                if more:
                    if not first:
                        act.wait_ge(mm_done, t)
                    hi(t + 1, 1 - half)
                act.wait_ge(stat_done, t + 1)
                nc.scalar.activation(root[:], mv[half][:, 1:2], ACT.Sqrt, bias=eps_col[:, 0:1]).then_inc(root_done, 1)
                if not first:
                    finish(t - 1, 1 - half, first=first_pair)

            hi(0, 0)
            step(0, 0, first=True)
            step(1, 1, first_pair=True)
            step(2, 0)
            step(3, 1)
            with act.Fori(2, NT // 2 - 1) as q:
                t0 = q * 2
                step(t0, 0)
                step(t0 + 1, 1)
            step(NT - 2, 0)
            step(NT - 1, 1, more=False)
            finish(NT - 1, 1)

        @block.vector
        def _(dve):
            chained = [0]

            def link(ins):
                ins.then_inc(ch, 1)
                chained[0] += 1

            def settle():
                dve.wait_ge(ch, chained[0])

            def reset():
                settle()
                dve.sem_clear(ch)
                chained[0] = 0

            nc.vector.memset(zero_i[:], 0)
            nc.vector.memset(eps_col[:], EPS)
            nc.vector.memset(ones_b[:], 1.0)
            nc.vector.memset(tri[:], 1.0)
            for n in range(EPG):
                nc.vector.memset(kd[:, n:n + 1], float(EPG - n))
            nc.vector.memset(tok_i[:], 0)
            for e in range(NE):
                nc.vector.memset(run[:, e:e + 1], float(e * SEQ))
            nc.vector.memset(root[:], 0.0).then_inc(s_cst, 1)

            dve.wait_ge(s_rows, 16 * 5)
            dve.wait_ge(s_cst, 1)
            n = 0
            for which in (GT1, SC2, SH2):
                if n:
                    dve.wait_ge(row_ps, n)
                link(nc.vector.tensor_copy(bc[:], mod[:, which * KD:(which + 1) * KD].rearrange("p (k a) -> p k a", a=1)
                                           .broadcast_to([P, KD, P])))
                settle()
                dve.sem_inc(bc_ready, 1)
                n += 1
                dve.wait_ge(row_ps, n)
                if which == GT1:
                    link(nc.vector.tensor_copy(g1_row[:], tr_ps[:]))
                    settle()
                    link(nc.vector.tensor_tensor(out=b_mix[:], in0=b_mix[:], in1=g1_row[:], op=ALU.mult))
                elif which == SC2:
                    link(nc.vector.tensor_tensor(out=g_u2[:], in0=tr_ps[:], in1=g_x1[:], op=ALU.mult))
                    link(nc.vector.tensor_tensor(out=b_u2[:], in0=tr_ps[:], in1=b_x1[:], op=ALU.mult))
                else:
                    link(nc.vector.tensor_tensor(out=b_u2[:], in0=tr_ps[:], in1=b_u2[:], op=ALU.add))
                settle()
                dve.sem_inc(row_taken, 1)
            link(nc.vector.tensor_scalar(g_x1[:], g_x1[:], ALPHA, None, ALU.mult))
            link(nc.vector.tensor_scalar(b_x1[:], b_x1[:], ALPHA, None, ALU.mult))
            dve.wait_ge(s_wo, 16 * KD)
            for k in range(KD):
                nc.vector.tensor_tensor(out=wo_raw[:, k, :], in0=wo_raw[:, k, :], in1=g1_row[:], op=ALU.mult).then_inc(wo_scaled, 1)
            for k in range(KD):
                dve.wait_ge(wo_scaled, k + 1)
                nc.vector.tensor_copy(wo_hi[:, k, :], wo_raw[:, k, :]).then_inc(wo_h, 1)
            for k in range(KD):
                dve.wait_ge(wo_h, k + 1)
                nc.vector.tensor_tensor(out=wo_lo[:, k, :], in0=wo_raw[:, k, :], in1=wo_hi[:, k, :].bitcast(f32),
                                        op=ALU.subtract).then_inc(wo_done, 1)
            reset()

            def lo(t, half):
                dve.wait_ge(hi_done, t + 1)
                nc.vector.tensor_tensor(out=mix_lo[half][:], in0=mix_raw[half][:], in1=mix_hi[half][:].bitcast(f32),
                                        op=ALU.subtract).then_inc(lo_done, 1)

            def grouped(ap):
                return ap.rearrange("p a (g e) -> p (a g) e", g=NG)

            def spread_to(ap, n):
                return ap.rearrange("p (a b) -> p a b", b=1).broadcast_to([P, ap.shape[1], n])

            def best(values, top, out):
                link(nc.vector.tensor_reduce(out=top[:], in_=grouped(values[:]), axis=AX.X, op=ALU.max))
                settle()
                link(nc.vector.tensor_tensor(out=grouped(key[:]), in0=grouped(values[:]), in1=spread_to(top[:], EPG), op=ALU.is_ge))
                settle()
                link(nc.vector.tensor_tensor(out=grouped(key[:]), in0=grouped(key[:]),
                                             in1=kd[:].rearrange("p (a e) -> p a e", a=1).broadcast_to([P, 2 * NG, EPG]), op=ALU.mult))
                settle()
                link(nc.vector.tensor_reduce(out=kmax[:], in_=grouped(key[:]), axis=AX.X, op=ALU.max))
                settle()
                link(nc.vector.tensor_tensor(out=grouped(out[:]), in0=grouped(key[:]), in1=spread_to(kmax[:], EPG), op=ALU.is_equal))
                settle()

            def choose(pair):
                dve.wait_ge(sc_done, 2 * pair + 2)
                link(nc.vector.tensor_tensor(out=sel[:], in0=sc[:], in1=rbias[:].rearrange("p (a e) -> p a e", a=1)
                                             .broadcast_to([P, 2, NE]), op=ALU.add))
                settle()
                best(sel, top1, o1)
                link(nc.vector.scalar_tensor_tensor(out=sel[:], in0=o1[:], scalar=-BIG, in1=sel[:], op0=ALU.mult, op1=ALU.add))
                settle()
                best(sel, top2, o2)
                gs = gsum[:].rearrange("p a g -> p (a g)")
                link(nc.vector.tensor_tensor(out=gs, in0=top1[:], in1=top2[:], op=ALU.add))
                settle()
                link(nc.vector.tensor_reduce(out=gmax[:], in_=gsum[:], axis=AX.X, op=ALU.max))
                settle()
                link(nc.vector.tensor_tensor(out=gsum[:], in0=gsum[:], in1=spread_to(gmax[:], NG), op=ALU.is_ge))
                settle()
                link(nc.vector.tensor_tensor(out=gsum[:], in0=gsum[:], in1=kd[:, 0:NG].rearrange("p (a e) -> p a e", a=1)
                                             .broadcast_to([P, 2, NG]), op=ALU.mult))
                settle()
                link(nc.vector.tensor_reduce(out=gmax[:], in_=gsum[:], axis=AX.X, op=ALU.max))
                settle()
                link(nc.vector.tensor_tensor(out=gsum[:], in0=gsum[:], in1=spread_to(gmax[:], NG), op=ALU.is_equal))
                settle()
                link(nc.vector.tensor_tensor(out=grouped(o1[:]), in0=grouped(o1[:]), in1=spread_to(gs, EPG), op=ALU.mult))
                link(nc.vector.tensor_tensor(out=grouped(o2[:]), in0=grouped(o2[:]), in1=spread_to(gs, EPG), op=ALU.mult))
                settle()
                link(nc.vector.tensor_tensor(out=mb[:], in0=o1[:], in1=o2[:], op=ALU.add))
                settle()
                dve.sem_inc(m_done, 1)
                for n, o in enumerate((o1, o2)):
                    link(nc.vector.tensor_tensor(out=key[:], in0=sc[:], in1=o[:], op=ALU.mult))
                    settle()
                    link(nc.vector.tensor_reduce(out=picked[:, n, :], in_=key[:], axis=AX.X, op=ALU.add))
                    settle()
                link(nc.vector.tensor_tensor(out=den[:], in0=picked[:, 0, :], in1=picked[:, 1, :], op=ALU.add))
                settle()
                link(nc.vector.reciprocal(den[:], den[:]))
                settle()
                for n in range(2):
                    link(nc.vector.tensor_tensor(out=w_all[:, n, bass.ds(pair * 2, 2)], in0=picked[:, n, :], in1=den[:], op=ALU.mult))

            def place(pair, first=False):
                dve.wait_ge(pos_done, pair + 1)
                link(nc.vector.tensor_tensor(out=pose[:], in0=pos_ps[:, 0:2, :], in1=run[:].rearrange("p (a e) -> p a e", a=1)
                                             .broadcast_to([P, 2, NE]), op=ALU.add))
                settle()
                link(nc.vector.tensor_tensor(out=run[:], in0=run[:], in1=pos_ps[:, 2, :], op=ALU.add))
                if not first:
                    dve.wait_ge(scatter, pair * 64)
                for n, (o, keep) in enumerate(((o1, m1_all), (o2, m2_all))):
                    link(nc.vector.tensor_copy(keep[:, bass.ds(pair * 2, 2), :], o[:]))
                    link(nc.vector.tensor_tensor(out=key[:], in0=pose[:], in1=o[:], op=ALU.mult))
                    settle()
                    link(nc.vector.tensor_reduce(out=picked[:, n, :], in_=key[:], axis=AX.X, op=ALU.add))
                    settle()
                link(nc.vector.tensor_copy(idx_all[:, :, bass.ds(pair * 2, 2)], picked[:]))
                link(nc.vector.tensor_copy(idx_i[:], picked[:]))
                link(nc.vector.tensor_copy(tok_i[:], tok_f[:]))
                settle()
                link(nc.vector.tensor_scalar(tok_f[:], tok_f[:], float(2 * P), None, ALU.add))
                settle()
                dve.sem_inc(idx_done, 1)

            def step(t, half, more=True, first=False, reused=True, route=None, first_pair=False):
                if more:
                    if not first:
                        dve.wait_ge(mm_done, t)
                    lo(t + 1, 1 - half)
                if route is not None:
                    choose(route)
                dve.wait_ge(xb_done, t + 1)
                dve.wait_ge(mm_done, t + 1)
                if reused:
                    dve.wait_ge(x1_done, t - 1)
                nc.vector.tensor_tensor(out=z[half][:], in0=mm_ps[half][:], in1=xt[half][:], op=ALU.add).then_inc(z_done, 1)
                dve.wait_ge(z_done, t + 1)
                for n in range(2):
                    link(nc.vector.bn_stats(stats[:, n, :], z[half][:, n * 512:(n + 1) * 512]))
                settle()
                nc.vector.bn_aggr(mv[half][:], stats[:]).then_inc(stat_done, 1)
                dve.wait_ge(stat_done, t + 1)
                if reused:
                    dve.wait_ge(u2_out[half], (t // 2) * 16)
                    dve.wait_ge(tr_done, t - 1)
                nc.vector.scalar_tensor_tensor(out=u2[half][:], in0=z[half][:], scalar=mv[half][:, 0:1], in1=g_u2[:],
                                               op0=ALU.subtract, op1=ALU.mult).then_inc(u2_half, 1)
                dve.wait_ge(root_done, t + 1)
                nc.vector.reciprocal(rstd[half][:], root[:]).then_inc(rstd_done, 1)
                dve.wait_ge(rstd_done, t + 1)
                dve.wait_ge(u2_half, t + 1)
                nc.vector.scalar_tensor_tensor(out=u2[half][:], in0=u2[half][:], scalar=rstd[half][:, 0:1], in1=b_u2[:],
                                               op0=ALU.mult, op1=ALU.add).then_inc(u2_done, 1)
                if route is not None:
                    place(route, first=first_pair)
                reset()

            lo(0, 0)
            dve.wait_ge(s_tri, 2)
            step(0, 0, first=True, reused=False)
            step(1, 1, reused=False)
            step(2, 0)
            step(3, 1, route=0, first_pair=True)
            with dve.Fori(2, NT // 2 - 1) as q:
                t0 = q * 2
                step(t0, 0)
                step(t0 + 1, 1, route=q - 1)
            step(NT - 2, 0)
            step(NT - 1, 1, more=False, route=NT // 2 - 2)
            choose(NT // 2 - 1)
            place(NT // 2 - 1)
            reset()

        @block.gpsimd
        def _(pool):
            pool.wait_ge(s_cst, 1)
            nc.gpsimd.affine_select(out=tri[:], in_=tri[:], compare_op=ALU.is_ge, fill=0.0, base=-1,
                                    pattern=[[1, P]], channel_multiplier=-1).then_inc(s_tri, 1)
            nc.gpsimd.iota(tok_i[:], pattern=[[P, 2]], base=0, channel_multiplier=1).then_inc(chp, 1)
            pool.wait_ge(chp, 1)
            nc.gpsimd.tensor_copy(tok_f[:], tok_i[:]).then_inc(s_tri, 1)
            pool.wait_ge(s_zero, 16)

            def xb(t, half):
                pool.wait_ge(xt_in[half], (t // 2) * 16 + 16)
                pool.sem_inc(chp, 1)
                nc.gpsimd.tensor_scalar(xt[half][:], xt[half][:], ALPHA, None, ALU.mult).then_inc(xa_done, 1)
                pool.wait_ge(xa_done, t + 1)
                nc.gpsimd.tensor_tensor(out=xt[half][:], in0=xt[half][:], in1=b_mix[:], op=ALU.add).then_inc(xb_done, 1)

            def send(pair):
                pool.wait_ge(idx_done, pair + 1)
                pool.sem_inc(chp, 1)
                for n in range(2):
                    for half in range(2):
                        nc.gpsimd.indirect_dma_start(out=list_dram, out_offset=bass.IndirectOffsetOnAxis(ap=idx_i[:, n, half:half + 1], axis=0),
                                                     in_=tok_i[:, half:half + 1], in_offset=None).then_inc(scatter, 16)

            def step(t, half, more=True, first=False, route=None):
                if more:
                    xb(t + 1, 1 - half)
                pool.wait_ge(rstd_done, t + 1)
                if not first:
                    pool.wait_ge(x1_out, t * 16)
                pool.sem_inc(chp, 1)
                nc.gpsimd.tensor_scalar(x1[:], z[half][:], mv[half][:, 0:1], rstd[half][:, 0:1], ALU.subtract, ALU.mult).then_inc(x1_norm, 1)
                pool.wait_ge(x1_norm, t + 1)
                nc.gpsimd.tensor_tensor(out=x1[:], in0=x1[:], in1=g_x1[:], op=ALU.mult).then_inc(x1_half, 1)
                pool.wait_ge(x1_half, t + 1)
                nc.gpsimd.tensor_tensor(out=x1[:], in0=x1[:], in1=b_x1[:], op=ALU.add).then_inc(x1_done, 1)
                dst_x = x1_t[bass.ds(t, 1)].rearrange("a p d -> (a p) d")
                dst_u = u2_t[bass.ds(t, 1)].rearrange("a p d -> (a p) d")
                pool.wait_ge(u2_done, t + 1)
                pool.wait_ge(x1_done, t + 1)
                pool.sem_inc(chp, 1)
                pool.dma_start(dst_u, u2[half][:]).then_inc(u2_out[half], 16)
                pool.dma_start(dst_x, x1[:]).then_inc(x1_out, 16)
                if route is not None:
                    send(route)

            pool.wait_ge(wo_done, KD)
            xb(0, 0)
            step(0, 0, first=True)
            step(1, 1)
            step(2, 0)
            step(3, 1, route=0)
            with pool.Fori(2, NT // 2 - 1) as q:
                t0 = q * 2
                step(t0, 0)
                step(t0 + 1, 1, route=q - 1)
            step(NT - 2, 0)
            step(NT - 1, 1, more=False, route=NT // 2 - 2)
            send(NT // 2 - 1)
            pool.wait_ge(scatter, 64 * (NT // 2))
            pool.wait_ge(x1_out, 16 * NT)
            for half in range(2):
                pool.wait_ge(u2_out[half], 16 * NT // 2)

        @block.tensor
        def _(pe):
            for n in range(3):
                pe.wait_ge(bc_ready, n + 1)
                if n:
                    pe.wait_ge(row_taken, n)
                for k in range(KD):
                    ins = nc.tensor.matmul(tr_ps[:, k * P:(k + 1) * P], bc[:, k, :], ident[:], start=True, stop=True)
                ins.then_inc(row_ps, 1)
            pe.wait_ge(row_taken, 3)
            pe.wait_ge(wo_done, KD)
            pe.wait_ge(s_tri, 2)

            def product(t, half, reused):
                pe.wait_ge(lo_done, t + 1)
                if reused:
                    pe.wait_ge(z_done, t - 1)
                for part in range(2):
                    cols = slice(part * 512, (part + 1) * 512)
                    out = mm_ps[half][:, cols]
                    for k in range(KD):
                        h, l = mix_hi[half][:, k, :], mix_lo[half][:, k, :]
                        nc.tensor.matmul(out, h, wo_hi[:, k, cols], start=(k == 0), stop=False)
                        nc.tensor.matmul(out, h, wo_lo[:, k, cols], start=False, stop=False)
                        ins = nc.tensor.matmul(out, l, wo_hi[:, k, cols], start=False, stop=(k == KD - 1))
                ins.then_inc(mm_done, 1)

            def score(t, half, first=False):
                pe.wait_ge(u2_done, t + 1)
                if not first:
                    pe.wait_ge(u2T_done, t)
                for k in range(KD):
                    ins = nc.tensor.transpose(tr_ps[:, k * P:(k + 1) * P], u2[half][:, k * P:(k + 1) * P], ident[:])
                ins.then_inc(tr_done, 1)
                pe.wait_ge(u2T_done, t + 1)
                if not first:
                    pe.wait_ge(sc_done, t)
                for k in range(KD):
                    ins = nc.tensor.matmul(rt_ps[:, 0:NE], u2T[:, k, :], wr[:, k, :], start=(k == 0), stop=(k == KD - 1))
                ins.then_inc(logit_done, 1)

            def places(pair):
                pe.wait_ge(m_done, pair + 1)
                nc.tensor.matmul(pos_ps[:, 0, :], tri[:], mb[:, 0, :], start=True, stop=True)
                nc.tensor.matmul(pos_ps[:, 1, :], tri[:], mb[:, 1, :], start=True, stop=False)
                nc.tensor.matmul(pos_ps[:, 1, :], ones_b[:], mb[:, 0, :], start=False, stop=True)
                nc.tensor.matmul(pos_ps[:, 2, :], ones_b[:], mb[:, 0, :], start=True, stop=False)
                nc.tensor.matmul(pos_ps[:, 2, :], ones_b[:], mb[:, 1, :], start=False, stop=True).then_inc(pos_done, 1)

            product(0, 0, False)
            product(1, 1, False)
            score(0, 0, first=True)
            product(2, 0, True)
            score(1, 1)
            product(3, 1, True)
            score(2, 0)
            places(0)
            with pe.Fori(2, NT // 2) as q:
                t0 = q * 2
                product(t0, 0, True)
                score(t0 - 1, 1)
                product(t0 + 1, 1, True)
                score(t0, 0)
                places(q - 1)
            score(NT - 1, 1)
            places(NT // 2 - 1)


NB = NBMAX + 1


def expert_phase(nc, persist, w_exp, u2_dram, list_dram, y_dram):
    f32, f32r, i32 = mybir.dt.float32, mybir.dt.float32r, mybir.dt.int32
    ALU, ACT, AX = mybir.AluOpType, mybir.ActivationFunctionType, mybir.AxisListType
    ident, run, row_base = (persist[n] for n in ("ident", "run", "row_base"))

    ctx = ExitStack()
    with ctx:
        sb = lambda name, shape, dt=f32: ctx.enter_context(nc.sbuf_tensor(name, shape, dt))
        ps = lambda name, shape: ctx.enter_context(nc.psum_tensor(name, shape, f32))
        sem = lambda name: ctx.enter_context(nc.semaphore(name))

        stage = sb("stage", [P, NPIECE, PC])
        w_hi = sb("wx_hi", [P, NPIECE, PC], f32r)
        w_lo = sb("wx_lo", [P, NPIECE, PC], f32r)
        xg = [sb(f"xg{n}", [P, D]) for n in range(2)]
        x_hi = sb("xe_hi", [P, KD, P], f32r)
        x_lo = sb("xe_lo", [P, KD, P], f32r)
        sg = sb("sg", [P, DE])
        h = sb("h", [P, DE])
        h_hi = sb("h_hi", [P, KE, P], f32r)
        h_lo = sb("h_lo", [P, KE, P], f32r)
        yo = [sb(f"yo{n}", [P, D]) for n in range(2)]
        ids = [sb(f"ids{n}", [P, 1], i32) for n in range(2)]
        iota_i = sb("iota_i", [P, NB + 1], i32)
        iota_f = sb("iota_f", [P, NB + 1])
        cnt = sb("cnt", [P, NE])
        nb = sb("nb", [P, NE])
        nb_end = [sb(f"nb_end{n}", [P, NE]) for n in range(2)]
        nb_start = sb("nb_start", [P, NE])
        thr = sb("thr", [P, EPG * 2])
        big = x_hi[:].rearrange("p k n -> p (k n)").bitcast(f32)
        cmp = sb("cmp", [P, NB + 1, NE])
        e_of = sb("e_of", [P, NB + 1])
        start_of = sb("start_of", [P, NB])
        flag = sb("flag", [P, NB])
        off = sb("off", [P, NB])
        mode = sb("mode", [P, NB])
        tab_e = sb("tab_e", [P, NB], i32)
        tab_mode = sb("tab_mode", [P, NB], i32)
        tab_off = sb("tab_off", [P, NB], i32)
        tab_go = sb("tab_go", [P, NB], i32)

        gate_ps = ps("gate_ps", [P, DE])
        up_ps = [ps(f"up_ps{n}", [P, DE]) for n in range(2)]
        hT_ps = ps("hT_ps", [P, KE, P])
        xT_ps = ps("xT_ps", [P, D])
        y_ps = ps("y_ps", [P, D])

        s_iota = sem("s_iota")
        tables = sem("tables")
        stage_in = [sem(f"stage_in{n}") for n in range(NPIECE)]
        stage_free = sem("stage_free")
        w_hi_done = sem("w_hi_done")
        w_free = sem("w_free")
        ids_in = sem("ids_in")
        xg_in = [sem(f"xg_in{n}") for n in range(2)]
        xT_done = sem("xT_done")
        x_hi_done = sem("x_hi_done")
        x_lo_done = sem("x_lo_done")
        gate_done = sem("gate_done")
        silu_done = sem("silu_done")
        up_done = sem("up_done")
        h_done = sem("h_done")
        hT_done = sem("hT_done")
        h_hi_done = sem("h_hi_done")
        h_lo_done = sem("h_lo_done")
        y_done = sem("y_done")
        yo_done = sem("yo_done")
        y_out = [sem(f"y_out{n}") for n in range(2)]
        ch = sem("che")
        order = sem("order")

        block = ctx.enter_context(nc.Block())
        y_t = y_dram.rearrange("(b p) d -> b p d", p=P)
        HC = DE // 2

        def each_block(eng, body, otherwise=None):
            eng.wait_ge(tables, 1)
            with eng.Fori(0, NB // 2) as q:
                for half in range(2):
                    b = q * 2 + half
                    mode_b = eng.value_load(tab_mode[0:1, bass.ds(b, 1)], min_val=0, max_val=2)
                    e = eng.value_load(tab_e[0:1, bass.ds(b, 1)], min_val=0, max_val=NE)
                    with eng.If(mode_b > 1):
                        body(b, half, e, True)
                    with eng.Else():
                        with eng.If(mode_b > 0):
                            body(b, half, e, False)
                        with eng.Else():
                            if otherwise:
                                otherwise(half)
                            else:
                                eng.nop()
                        eng.nop()

        @block.sync
        def _(sp):
            for i in range(NPIECE):
                sp.dma_start(stage[:, i, :], w_exp[0, i]).then_inc(stage_in[i], 16)
            with sp.Fori(1, NE) as e:
                for i in range(NPIECE):
                    src = w_exp[bass.ds(e, 1), i].rearrange("a p n -> (a p) n")
                    sp.wait_ge(stage_free, (e - 1) * NPIECE + i + 1)
                    sp.dma_start(stage[:, i, :], src).then_inc(stage_in[i], 16)

        @block.gpsimd
        def _(pool):
            nc.gpsimd.iota(iota_i[:], pattern=[[1, NB + 1]], base=0, channel_multiplier=0).then_inc(s_iota, 1)
            pool.wait_ge(tables, 1)
            with pool.Fori(0, NB // 2) as q:
                for half in range(2):
                    b = q * 2 + half
                    go = pool.value_load(tab_go[0:1, bass.ds(b, 1)], min_val=0, max_val=1)
                    at = pool.value_load(tab_off[0:1, bass.ds(b, 1)], min_val=0, max_val=NE * SEQ - P)
                    with pool.If(go > 0):
                        src = list_dram[bass.ds(at, P), :]
                        pool.wait_ge(xT_done, b)
                        pool.sem_inc(order, 1)
                        pool.dma_start(ids[half][:], src).then_inc(ids_in, 16)
                        pool.wait_ge(ids_in, b * 16 + 16)
                        pool.sem_inc(order, 1)
                        nc.gpsimd.indirect_dma_start(out=xg[half][:], out_offset=None, in_=u2_dram,
                                                     in_offset=bass.IndirectOffsetOnAxis(ap=ids[half][:, 0:1], axis=0)).then_inc(xg_in[half], 16)
                    with pool.Else():
                        pool.nop()

        @block.scalar
        def _(act):
            def split_hi(e, i):
                act.wait_ge(stage_in[i], e * 16 + 16)
                nc.scalar.activation(w_hi[:, i, :], stage[:, i, :], ACT.Copy).then_inc(w_hi_done, 1)

            def x_high(b):
                act.wait_ge(xT_done, b + 2)
                nc.scalar.activation(x_hi[:], xT_ps[:].rearrange("p (k n) -> p k n", k=KD), ACT.Copy).then_inc(x_hi_done, 1)

            def body(b, half, e, last):
                def piece(i):
                    if last:
                        if i < NPIECE - 1:
                            act.wait_ge(w_free, e * (NPIECE - 1) + i + 1)
                        split_hi(e + 1, i)
                piece(0), piece(1), piece(2)
                act.wait_ge(gate_done, b + 1)
                act.wait_ge(h_done, b * 2)
                nc.scalar.activation(sg[:], gate_ps[:], ACT.Silu).then_inc(silu_done, 1)
                piece(3), piece(4), piece(5)
                for n in range(2):
                    act.wait_ge(hT_done, b * 2 + n + 1)
                    nc.scalar.activation(h_hi[:, 2 * n:2 * n + 2, :], hT_ps[:, 2 * n:2 * n + 2, :], ACT.Copy).then_inc(h_hi_done, 1)
                    if n == 0:
                        x_high(b + 1)
                for i in range(6, 11):
                    piece(i)
                act.wait_ge(y_done, b + 1)
                act.wait_ge(y_out[half], (b - half) * 8)
                nc.scalar.activation(yo[half][:], y_ps[:], ACT.Copy).then_inc(yo_done, 1)
                dst = y_t[bass.ds(b, 1)].rearrange("a p d -> (a p) d")
                act.wait_ge(yo_done, b + 1)
                act.dma_start(dst, yo[half][:]).then_inc(y_out[half], 16)
                piece(11)

            for i in range(NPIECE):
                split_hi(0, i)
            x_high(0)
            each_block(act, body, lambda half: act.sem_inc(y_out[half], 16))
            for half in range(2):
                act.wait_ge(y_out[half], 16 * NB // 2)

        @block.vector
        def _(dve):
            chained = [0]

            def link(ins):
                ins.then_inc(ch, 1)
                chained[0] += 1
                dve.wait_ge(ch, chained[0])

            def split_lo(e, i):
                dve.wait_ge(w_hi_done, e * NPIECE + i + 1)
                nc.vector.tensor_tensor(out=w_lo[:, i, :], in0=stage[:, i, :], in1=w_hi[:, i, :].bitcast(f32),
                                        op=ALU.subtract).then_inc(stage_free, 1)

            def x_low(b):
                dve.wait_ge(x_hi_done, b + 1)
                nc.vector.tensor_tensor(out=x_lo[:], in0=xT_ps[:].rearrange("p (k n) -> p k n", k=KD), in1=x_hi[:].bitcast(f32),
                                        op=ALU.subtract).then_inc(x_lo_done, 1)

            def over_e(ap, n):
                return ap.rearrange("p (a b) -> p a b", a=1).broadcast_to([P, n, NE])

            def over_b(ap):
                return ap.rearrange("p (a b) -> p a b", b=1).broadcast_to([P, ap.shape[1], NE])

            nc.vector.memset(tab_go[:], 1)
            for j in range(16):
                ins = nc.vector.memset(thr[:, j:j + 1], float(P * (j + 1)))
            link(ins)
            dve.wait_ge(s_iota, 1)
            link(nc.vector.tensor_copy(iota_f[:], iota_i[:]))
            link(nc.vector.scalar_tensor_tensor(out=cnt[:], in0=iota_f[:, 0:NE], scalar=-float(SEQ), in1=run[:], op0=ALU.mult, op1=ALU.add))
            passed = cmp[:, 0:16, :].rearrange("p j e -> p (j e)").rearrange("p (e j) -> p e j", e=NE)
            link(nc.vector.tensor_tensor(out=passed, in0=cnt[:].rearrange("p (e a) -> p e a", a=1).broadcast_to([P, NE, 16]),
                                         in1=thr[:].rearrange("p (a j) -> p a j", a=1).broadcast_to([P, NE, 16]), op=ALU.is_gt))
            link(nc.vector.tensor_reduce(out=nb[:], in_=passed, axis=AX.X, op=ALU.add))
            link(nc.vector.tensor_scalar(nb[:], nb[:], 1.0, None, ALU.add))
            src = nb
            for lvl in range(5):
                dst, s = nb_end[lvl % 2], 1 << lvl
                link(nc.vector.tensor_copy(dst[:, 0:s], src[:, 0:s]))
                link(nc.vector.tensor_tensor(out=dst[:, s:], in0=src[:, s:], in1=src[:, 0:NE - s], op=ALU.add))
                src = dst
            end = src
            link(nc.vector.tensor_tensor(out=nb_start[:], in0=end[:], in1=nb[:], op=ALU.subtract))
            link(nc.vector.tensor_tensor(out=cmp[:], in0=over_e(end[:], NB + 1), in1=over_b(iota_f[:]), op=ALU.is_le))
            link(nc.vector.tensor_reduce(out=e_of[:], in_=cmp[:], axis=AX.X, op=ALU.add))
            link(nc.vector.tensor_tensor(out=cmp[:, 0:NB, :], in0=over_e(nb_start[:], NB), in1=over_b(iota_f[:, 0:NB]), op=ALU.is_le))
            link(nc.vector.tensor_tensor(out=cmp[:, 0:NB, :], in0=cmp[:, 0:NB, :], in1=over_e(nb_start[:], NB), op=ALU.mult))
            link(nc.vector.tensor_reduce(out=start_of[:], in_=cmp[:, 0:NB, :], axis=AX.X, op=ALU.max))
            link(nc.vector.tensor_tensor(out=off[:], in0=iota_f[:, 0:NB], in1=start_of[:], op=ALU.subtract))
            link(nc.vector.tensor_scalar(off[:], off[:], float(P), None, ALU.mult))
            link(nc.vector.scalar_tensor_tensor(out=off[:], in0=e_of[:, 0:NB], scalar=float(SEQ), in1=off[:], op0=ALU.mult, op1=ALU.add))
            link(nc.vector.tensor_scalar(flag[:], e_of[:, 0:NB], float(NE - 1), None, ALU.is_le))
            link(nc.vector.tensor_tensor(out=off[:], in0=off[:], in1=flag[:], op=ALU.mult))
            link(nc.vector.tensor_tensor(out=mode[:], in0=e_of[:, 1:], in1=e_of[:, 0:NB], op=ALU.is_gt))
            link(nc.vector.scalar_tensor_tensor(out=mode[:], in0=e_of[:, 0:NB], scalar=float(NE - 2), in1=mode[:], op0=ALU.is_le, op1=ALU.mult))
            link(nc.vector.tensor_tensor(out=mode[:], in0=mode[:], in1=flag[:], op=ALU.add))
            link(nc.vector.tensor_copy(tab_e[:], e_of[:, 0:NB]))
            link(nc.vector.tensor_copy(tab_off[:], off[:]))
            link(nc.vector.tensor_copy(tab_mode[:], mode[:]))
            link(nc.vector.tensor_copy(tab_go[:, 1:], flag[:, 0:NB - 1]))
            link(nc.vector.tensor_scalar(row_base[:], nb_start[:], float(P), None, ALU.mult))
            link(nc.vector.scalar_tensor_tensor(out=row_base[:], in0=iota_f[:, 0:NE], scalar=-float(SEQ), in1=row_base[:],
                                                op0=ALU.mult, op1=ALU.add))
            dve.sem_inc(tables, 1)

            def body(b, half, e, last):
                def piece(i):
                    if last:
                        split_lo(e + 1, i)
                for i in range(4):
                    piece(i)
                dve.wait_ge(silu_done, b + 1)
                for n in range(2):
                    cols = slice(n * HC, (n + 1) * HC)
                    dve.wait_ge(up_done, b * 2 + n + 1)
                    nc.vector.tensor_tensor(out=h[:, cols], in0=up_ps[n][:, 0:HC], in1=sg[:, cols], op=ALU.mult).then_inc(h_done, 1)
                    piece(4 + n)
                for n in range(2):
                    dve.wait_ge(h_hi_done, b * 2 + n + 1)
                    nc.vector.tensor_tensor(out=h_lo[:, 2 * n:2 * n + 2, :], in0=hT_ps[:, 2 * n:2 * n + 2, :],
                                            in1=h_hi[:, 2 * n:2 * n + 2, :].bitcast(f32), op=ALU.subtract).then_inc(h_lo_done, 1)
                    if n == 0:
                        x_low(b + 1)
                for i in range(6, NPIECE):
                    piece(i)

            for i in range(NPIECE):
                split_lo(0, i)
            x_low(0)
            each_block(dve, body)

        @block.tensor
        def _(pe):
            def body(b, half, e, last):
                q_next = b // 2 + half

                def release(ins, done):
                    if last and done:
                        ins.then_inc(w_free, 1)

                pe.wait_ge(x_lo_done, b + 1)
                pe.wait_ge(silu_done, b)
                for k in range(KD):
                    if k % 2 == 0:
                        pe.wait_ge(stage_free, e * NPIECE + k // 2 + 1)
                    at = slice(k % 2 * DE, (k % 2 + 1) * DE)
                    release(nc.tensor.matmul(gate_ps[:], x_hi[:, k, :], w_hi[:, k // 2, at], start=(k == 0), stop=False),
                            k % 2 == 0 and k > 0)
                    nc.tensor.matmul(gate_ps[:], x_hi[:, k, :], w_lo[:, k // 2, at], start=False, stop=False)
                    ins = nc.tensor.matmul(gate_ps[:], x_lo[:, k, :], w_hi[:, k // 2, at], start=False, stop=(k == KD - 1))
                ins.then_inc(gate_done, 1)
                pe.wait_ge(h_done, b * 2)
                for n in range(2):
                    out = up_ps[n][:, 0:HC]
                    for k in range(KD):
                        if n == 0 and k % 2 == 0:
                            pe.wait_ge(stage_free, e * NPIECE + 4 + k // 2 + 1)
                        first = k % 2 * DE + n * HC
                        at = slice(first, first + HC)
                        release(nc.tensor.matmul(out, x_hi[:, k, :], w_hi[:, 4 + k // 2, at], start=(k == 0), stop=False),
                                (k == 0) if n == 0 else (k % 2 == 0 and k > 0))
                        nc.tensor.matmul(out, x_hi[:, k, :], w_lo[:, 4 + k // 2, at], start=False, stop=False)
                        ins = nc.tensor.matmul(out, x_lo[:, k, :], w_hi[:, 4 + k // 2, at], start=False, stop=(k == KD - 1))
                    ins.then_inc(up_done, 1)
                for n in range(2):
                    pe.wait_ge(h_done, b * 2 + n + 1)
                    if n:
                        pe.wait_ge(h_lo_done, b * 2 + 1)
                    for k in (2 * n, 2 * n + 1):
                        ins = nc.tensor.transpose(hT_ps[:, k, :], h[:, k * P:(k + 1) * P], ident[:])
                        release(ins, k == 0)
                    ins.then_inc(hT_done, 1)
                    if n == 0:
                        pe.wait_ge(xg_in[1 - half], q_next * 16 + 16)
                        for k in range(KD):
                            ins = nc.tensor.transpose(xT_ps[:, k * P:(k + 1) * P], xg[1 - half][:, k * P:(k + 1) * P], ident[:])
                        ins.then_inc(xT_done, 1)
                pe.wait_ge(yo_done, b)
                for k in range(KE):
                    if k % 2 == 0:
                        pe.wait_ge(h_lo_done, b * 2 + k // 2 + 1)
                    pe.wait_ge(stage_free, e * NPIECE + 8 + k + 1)
                    for part in range(2):
                        at = slice(part * 512, (part + 1) * 512)
                        release(nc.tensor.matmul(y_ps[:, at], h_hi[:, k, :], w_hi[:, 8 + k, at], start=(k == 0), stop=False),
                                k > 0 and part == 0)
                        nc.tensor.matmul(y_ps[:, at], h_hi[:, k, :], w_lo[:, 8 + k, at], start=False, stop=False)
                        ins = nc.tensor.matmul(y_ps[:, at], h_lo[:, k, :], w_hi[:, 8 + k, at], start=False, stop=(k == KE - 1))
                ins.then_inc(y_done, 1)

            pe.sem_inc(xT_done, 1)
            pe.wait_ge(xg_in[0], 16)
            for k in range(KD):
                ins = nc.tensor.transpose(xT_ps[:, k * P:(k + 1) * P], xg[0][:, k * P:(k + 1) * P], ident[:])
            ins.then_inc(xT_done, 1)
            each_block(pe, body)


def combine_phase(nc, persist, rows, x1_dram, y_dram, out):
    f32, i32 = mybir.dt.float32, mybir.dt.int32
    ALU, ACT, AX = mybir.AluOpType, mybir.ActivationFunctionType, mybir.AxisListType
    ident, mod = persist["ident"], persist["mod"]
    m_all = (persist["m1_all"], persist["m2_all"])
    w_all, idx_all, row_base = (persist[n] for n in ("w_all", "idx_all", "row_base"))
    NBUF = 4

    ctx = ExitStack()
    with ctx:
        sb = lambda name, shape, dt=f32: ctx.enter_context(nc.sbuf_tensor(name, shape, dt))
        sem = lambda name: ctx.enter_context(nc.semaphore(name))
        bc = sb("bc2", [P, KD, P])
        g2_row = sb("g2_row", [P, D])
        ln_g = sb("ln2g", [P, D])
        ln_b = sb("ln2b", [P, D])
        prod = sb("prod", [P, NT, NE])
        y_idx = sb("y_idx", [P, 2, NT], i32)
        y_row = sb("y_row", [P, 2, NT])
        xa = [sb(f"xa{n}", [P, D]) for n in range(NBUF)]
        ya = [sb(f"ya{n}", [P, D]) for n in range(NBUF)]
        yb = [sb(f"yb{n}", [P, D]) for n in range(NBUF)]
        zo = [sb(f"zo{n}", [P, D]) for n in range(NBUF)]
        stats = sb("stats2", [P, 2, 6])
        mv = [sb(f"mv2{n}", [P, 2]) for n in range(2)]
        root = sb("root2", [P, 1])
        rstd = [sb(f"rstd2{n}", [P, 1]) for n in range(2)]
        eps_col = sb("eps2", [P, 1])
        row_ps = ctx.enter_context(nc.psum_tensor("row_ps", [P, D], f32))

        s_rows = sem("s_rows2")
        s_bc = sem("s_bc2")
        s_row = sem("s_row2")
        s_idx = sem("s_idx2")
        xa_in = [sem(f"xa_in{n}") for n in range(NBUF)]
        ya_in = [sem(f"ya_in{n}") for n in range(NBUF)]
        yb_in = [sem(f"yb_in{n}") for n in range(NBUF)]
        wa_done = sem("wa_done")
        f_done = sem("f_done")
        fg_done = sem("fg_done")
        z_done = sem("z_done2")
        stat_done = sem("stat_done2")
        root_done = sem("root_done2")
        rstd_done = sem("rstd_done2")
        n_norm = sem("n_norm")
        n_half = sem("n_half")
        n_done = sem("n_done")
        stored = [sem(f"stored{n}") for n in range(NBUF)]
        ch = sem("cht")
        order = sem("order2")
        block = ctx.enter_context(nc.Block())
        x1_t = x1_dram.rearrange("(t p) d -> t p d", p=P)
        out_t = out.rearrange("(t p) d -> t p d", p=P)

        @block.sync
        def _(sp):
            sp.dma_start(ln_g[:], rows[ROW_G2:ROW_G2 + 1, :].broadcast_to([P, D])).then_inc(s_rows, 16)
            sp.dma_start(ln_b[:], rows[ROW_B2:ROW_B2 + 1, :].broadcast_to([P, D])).then_inc(s_rows, 16)
            with sp.Fori(0, NT // NBUF) as r:
                for n in range(NBUF):
                    src = x1_t[bass.ds(r * NBUF + n, 1)].rearrange("a p d -> (a p) d")
                    sp.wait_ge(z_done, r * NBUF)
                    sp.dma_start(xa[n][:], src).then_inc(xa_in[n], 16)
            sp.wait_ge(s_rows, 32)

        def norm(pool, t):
            n = t % NBUF
            pool.wait_ge(rstd_done, t + 1)
            pool.sem_inc(order, 1)
            nc.gpsimd.tensor_scalar(zo[n][:], zo[n][:], mv[t % 2][:, 0:1], rstd[t % 2][:, 0:1], ALU.subtract, ALU.mult).then_inc(n_norm, 1)
            pool.wait_ge(n_norm, t + 1)
            nc.gpsimd.tensor_tensor(out=zo[n][:], in0=zo[n][:], in1=ln_g[:], op=ALU.mult).then_inc(n_half, 1)
            pool.wait_ge(n_half, t + 1)
            nc.gpsimd.tensor_tensor(out=zo[n][:], in0=zo[n][:], in1=ln_b[:], op=ALU.add).then_inc(n_done, 1)

        @block.gpsimd
        def _(pool):
            pool.wait_ge(s_idx, 1)
            for t in range(NT):
                n = t % NBUF
                if t >= NBUF:
                    pool.wait_ge(f_done, t - NBUF + 1)
                for j, dst, s in ((0, ya[n], ya_in[n]), (1, yb[n], yb_in[n])):
                    nc.gpsimd.indirect_dma_start(out=dst[:], out_offset=None, in_=y_dram,
                                                 in_offset=bass.IndirectOffsetOnAxis(ap=y_idx[:, j, t:t + 1], axis=0)).then_inc(s, 16)
                if t >= 1:
                    norm(pool, t - 1)
            norm(pool, NT - 1)

        @block.scalar
        def _(act):
            act.wait_ge(s_idx, 1)
            for t in range(NT):
                n = t % NBUF
                act.wait_ge(ya_in[n], 16 * (t // NBUF + 1))
                nc.scalar.activation(ya[n][:], ya[n][:], ACT.Copy, scale=w_all[:, 0, t:t + 1]).then_inc(wa_done, 1)
                act.wait_ge(stat_done, t + 1)
                if t:
                    act.wait_ge(rstd_done, t)
                nc.scalar.activation(root[:], mv[t % 2][:, 1:2], ACT.Sqrt, bias=eps_col[:, 0:1]).then_inc(root_done, 1)
                if t:
                    act.wait_ge(n_done, t)
                    act.dma_start(out_t[t - 1], zo[(t - 1) % NBUF][:]).then_inc(stored[(t - 1) % NBUF], 16)
            act.wait_ge(n_done, NT)
            act.dma_start(out_t[NT - 1], zo[(NT - 1) % NBUF][:]).then_inc(stored[(NT - 1) % NBUF], 16)
            for n in range(NBUF):
                act.wait_ge(stored[n], 16 * NT // NBUF)

        @block.vector
        def _(dve):
            chained = [0]

            def link(ins):
                ins.then_inc(ch, 1)
                chained[0] += 1
                dve.wait_ge(ch, chained[0])

            link(nc.vector.memset(eps_col[:], EPS))
            for j in range(2):
                link(nc.vector.tensor_tensor(out=prod[:], in0=m_all[j][:], in1=row_base[:].rearrange("p (a e) -> p a e", a=1)
                                             .broadcast_to([P, NT, NE]), op=ALU.mult))
                link(nc.vector.tensor_reduce(out=y_row[:, j, :], in_=prod[:], axis=AX.X, op=ALU.add))
            link(nc.vector.tensor_tensor(out=y_row[:], in0=y_row[:], in1=idx_all[:], op=ALU.add))
            link(nc.vector.tensor_copy(y_idx[:], y_row[:]))
            dve.sem_inc(s_idx, 1)
            nc.vector.tensor_copy(bc[:], mod[:, GT2 * KD:(GT2 + 1) * KD].rearrange("p (k a) -> p k a", a=1)
                                  .broadcast_to([P, KD, P])).then_inc(s_bc, 1)
            dve.wait_ge(s_row, 1)
            link(nc.vector.tensor_copy(g2_row[:], row_ps[:]))
            dve.wait_ge(s_rows, 32)
            for t in range(NT):
                n = t % NBUF
                dve.wait_ge(wa_done, t + 1)
                dve.wait_ge(yb_in[n], 16 * (t // NBUF + 1))
                nc.vector.scalar_tensor_tensor(out=yb[n][:], in0=yb[n][:], scalar=w_all[:, 1, t:t + 1], in1=ya[n][:],
                                               op0=ALU.mult, op1=ALU.add).then_inc(fg_done, 1)
                dve.wait_ge(fg_done, 2 * t + 1)
                if t >= NBUF:
                    dve.wait_ge(stored[n], 16 * (t // NBUF))
                nc.vector.tensor_tensor(out=zo[n][:], in0=yb[n][:], in1=g2_row[:], op=ALU.mult).then_inc(fg_done, 1)
                dve.wait_ge(fg_done, 2 * t + 2)
                dve.sem_inc(f_done, 1)
                dve.wait_ge(xa_in[n], 16 * (t // NBUF + 1))
                nc.vector.tensor_tensor(out=zo[n][:], in0=zo[n][:], in1=xa[n][:], op=ALU.add).then_inc(z_done, 1)
                dve.wait_ge(z_done, t + 1)
                for part in range(2):
                    nc.vector.bn_stats(stats[:, part, :], zo[n][:, part * 512:(part + 1) * 512]).then_inc(ch, 1)
                chained[0] += 2
                dve.wait_ge(ch, chained[0])
                if t >= 2:
                    dve.wait_ge(n_done, t - 1)
                nc.vector.bn_aggr(mv[t % 2][:], stats[:]).then_inc(stat_done, 1)
                dve.wait_ge(root_done, t + 1)
                nc.vector.reciprocal(rstd[t % 2][:], root[:]).then_inc(rstd_done, 1)

        @block.tensor
        def _(pe):
            pe.wait_ge(s_bc, 1)
            for k in range(KD):
                ins = nc.tensor.matmul(row_ps[:, k * P:(k + 1) * P], bc[:, k, :], ident[:], start=True, stop=True)
            ins.then_inc(s_row, 1)


def hybrid_block(nc, x, xT, w_ada, cols, w_in, pool_w, w_out, rows, w_router, router_bias, w_exp, out):
    f32 = mybir.dt.float32
    scratch = lambda name, shape, dt=f32: nc.dram_tensor(name, shape, dt).ap()
    mix_spill = scratch("mix_spill", (NCH, P, KD * CH))
    x1_dram = scratch("x1_dram", (SEQ, D))
    u2_dram = scratch("u2_dram", (SEQ, D))
    y_dram = scratch("y_dram", (NB * P, D))
    list_dram = scratch("list_dram", (NE * SEQ, 1), mybir.dt.int32)
    ctx = ExitStack()
    with ctx:
        persist = {name: ctx.enter_context(nc.sbuf_tensor(name, shape, f32)) for name, shape in (
            ("ident", [P, P]), ("mod", [P, 6 * KD]))}
        with ExitStack() as front:
            col = front.enter_context(nc.sbuf_tensor("col", [P, NCOL], f32))
            w_hi, w_lo = (front.enter_context(nc.sbuf_tensor(name, [P, KD, NIN], mybir.dt.float32r)) for name in ("w_in_hi", "w_in_lo"))
            modulation_phase(nc, {**persist, "col": col}, w_hi, w_lo, w_ada, cols, w_in)
            conv_pool_phase(nc, {**persist, "col": col}, w_hi, w_lo, xT, pool_w, mix_spill)
        persist |= {name: ctx.enter_context(nc.sbuf_tensor(name, shape, f32)) for name, shape in (
            ("m1_all", [P, NT, NE]), ("m2_all", [P, NT, NE]), ("w_all", [P, 2, NT]), ("idx_all", [P, 2, NT]),
            ("run", [P, NE]), ("row_base", [P, NE]))}
        mix_router_phase(nc, persist, x, w_out, rows, w_router, router_bias, mix_spill, x1_dram, u2_dram, list_dram, y_dram)
        expert_phase(nc, persist, w_exp, u2_dram, list_dram, y_dram)
        combine_phase(nc, persist, rows, x1_dram, y_dram, out)


def lay_out(a):
    import numpy as np
    x = np.asarray(a["x"])[0]
    col = np.zeros((P, NCOL), np.float32)
    col[:, COL_BADA:COL_BIN] = np.asarray(a["b_ada"])[0].reshape(6 * KD, P).T
    order = [b for j in range(CG) for b in (CG + j, j)] + list(range(2 * CG, NM))
    col[:, COL_BIN:COL_CONVW] = np.asarray(a["b_in"])[0].reshape(NM, P)[order].T
    col[:, COL_CONVW:COL_CONVB] = np.asarray(a["conv_w"])[0].reshape(TAPS, CG, P).transpose(2, 1, 0).reshape(P, CG * TAPS)
    for at, name in ((COL_CONVB, "conv_b"), (COL_LNG, "conv_ln_g"), (COL_LNB, "conv_ln_b"), (COL_PSC, "pool_scale")):
        col[:, at:at + CG] = np.asarray(a[name])[0].reshape(CG, P).T
    col[:, COL_C:COL_FIX] = np.asarray(a["c"])[0].reshape(KD, P).T
    col[:, COL_FIX:] = np.concatenate([[w / min(t + 1, w) for t in range(PHALO)] for w in WINDOWS]).astype(np.float32)
    w_in = np.asarray(a["w_in"])[0].reshape(KD, P, NM, P)[:, :, order].transpose(1, 0, 2, 3)
    w_in = w_in.reshape(P, KD * NIN // PC, PC).transpose(1, 0, 2)
    gate, up = (np.asarray(a[n])[0].reshape(NE, KD, P, DE).transpose(0, 2, 1, 3).reshape(NE, P, 4, PC) for n in ("w_gate", "w_up"))
    down = np.asarray(a["w_down"])[0].reshape(NE, KE, P, D).transpose(0, 2, 1, 3)
    w_exp = np.empty((NE, NPIECE, P, PC), np.float32)
    for at, part in ((0, gate), (4, up), (8, down)):
        w_exp[:, at:at + 4] = part.transpose(0, 2, 1, 3)
    return {
        "x": x,
        "xT": x.reshape(NCH, CH, KD, P).transpose(0, 3, 2, 1).reshape(NCH, P, KD * CH),
        "w_ada": np.asarray(a["w_ada"])[0].reshape(KD, P, 6, PC).transpose(2, 0, 1, 3).reshape(6 * KD, P, PC),
        "cols": col,
        "w_in": w_in,
        "pool_w": np.asarray(a["pool_w"])[0].transpose(1, 0, 2).reshape(P, CG * P),
        "w_out": np.asarray(a["w_out"])[0].reshape(KD, P, D),
        "rows": np.stack([np.asarray(a[n])[0] for n in ("b_out", "ln1_g", "ln1_b", "ln2_g", "ln2_b")]),
        "w_router": np.asarray(a["w_router"]).reshape(KD, P, NE).transpose(1, 0, 2).reshape(P, KD * NE),
        "router_bias": np.asarray(a["router_bias"]).reshape(1, NE),
        "w_exp": w_exp,
    }


_INS = ("x", "xT", "w_ada", "cols", "w_in", "pool_w", "w_out", "rows", "w_router", "router_bias", "w_exp")


def kernel(**inputs):
    import numpy as np
    import concourse.bacc as bacc
    from concourse.bass_utils import run_bass_kernel_spmd
    laid = lay_out(inputs)
    nc = bacc.Bacc("TRN2", target_bir_lowering=False, num_devices=1)
    arrays, args = {}, []
    for name in _INS:
        a = np.ascontiguousarray(laid[name])
        arrays[f"in_{name}"] = a
        args.append(nc.dram_tensor(f"in_{name}", a.shape, mybir.dt.from_np(a.dtype), kind="ExternalInput").ap())
    out = nc.dram_tensor("out", (SEQ, D), mybir.dt.float32, kind="ExternalOutput").ap()
    hybrid_block(nc, *args, out)
    got = run_bass_kernel_spmd(nc, [arrays], core_ids=[0]).results[0]["out"]
    return got.reshape(1, SEQ, D)
```

```python
import concourse.bass as bass
from concourse import mybir
from contextlib import ExitStack

P = 128
D = 1024
SEQ = 2048
KD = D // P
CW = 512
CG = CW // P
NIN = 2 * CW + (D - CW)
NM = NIN // P
TAPS = 31
HALO = TAPS - 1
WINDOWS = (2, 4, 8, 16)
PHALO = 16
CH = 256
NCH = SEQ // CH
TPC = CH // P
NT = SEQ // P
NE = 32
NG = 4
EPG = NE // NG
DE = 512
KE = DE // P
EPS = 1e-5
ALPHA = 2.0 ** 0.25
NPIECE = 12
PC = 1024
NBMAX = SEQ * 2 // P + NE - 1
BIG = 1e30

COL_BADA = 0
COL_BIN = COL_BADA + 6 * KD
COL_CONVW = COL_BIN + NM
COL_CONVB = COL_CONVW + CG * TAPS
COL_LNG = COL_CONVB + CG
COL_LNB = COL_LNG + CG
COL_PSC = COL_LNB + CG
COL_C = COL_PSC + CG
COL_FIX = COL_C + KD
NCOL = COL_FIX + CG * PHALO
ROW_BOUT, ROW_G1, ROW_B1, ROW_G2, ROW_B2, NROW = 0, 1, 2, 3, 4, 5
SH1, SC1, GT1, SH2, SC2, GT2 = range(6)


def modulation_phase(nc, persist, w_hi, w_lo, w_ada, cols, w_in):
    f32 = mybir.dt.float32
    ALU, ACT = mybir.AluOpType, mybir.ActivationFunctionType
    ident, mod, col = persist["ident"], persist["mod"], persist["col"]
    NRING = 5
    N_WIN = KD * NIN // PC
    N_FIRST = 2 * KD

    ctx = ExitStack()
    with ctx:
        sb = lambda name, shape, dt=f32: ctx.enter_context(nc.sbuf_tensor(name, shape, dt))
        sem = lambda name: ctx.enter_context(nc.semaphore(name))
        ring = sb("ring", [P, NRING, PC])
        acc = sb("ada_acc", [P, 2, PC])
        cact = sb("cact", [P, KD])
        ones = sb("ones", [P, 1])
        mod_ps = ctx.enter_context(nc.psum_tensor("mod_ps", [P, 512], f32))
        s_col = sem("s_col")
        s_const = sem("s_const")
        s_cact = sem("s_cact")
        ring_in = [sem(f"ring_in{n}") for n in range(NRING)]
        ring_free = sem("ring_free")
        w_hi_ready = sem("w_hi_ready")
        mod_ps_ready = sem("mod_ps_ready")
        ident_ready = sem("ident_ready")
        chain = persist["dve_chain"]
        block = ctx.enter_context(nc.Block())
        w_ins = range(N_FIRST, N_FIRST + N_WIN)
        adas = [n for n in range(6 * KD + N_WIN) if n not in w_ins]
        hi_of = lambda q: w_hi[:].rearrange("p k n -> p (k n)")[:, q * PC:(q + 1) * PC]
        lo_of = lambda q: w_lo[:].rearrange("p k n -> p (k n)")[:, q * PC:(q + 1) * PC]

        @block.sync
        def _(sp):
            sp.dma_start(col[:], cols).then_inc(s_col, 16)
            for n in range(6 * KD + N_WIN):
                src = w_in[n - N_FIRST] if n in w_ins else w_ada[adas.index(n)]
                if n >= NRING:
                    sp.wait_ge(ring_free, n - NRING + 1)
                sp.dma_start(ring[:, n % NRING, :], src).then_inc(ring_in[n % NRING], 16)

        @block.scalar
        def _(act):
            act.wait_ge(s_col, 16)
            nc.scalar.activation(cact[:], col[:, COL_C:COL_C + KD], ACT.Silu).then_inc(s_cact, 1)
            for n in w_ins:
                act.wait_ge(ring_in[n % NRING], 16 * (n // NRING + 1))
                nc.scalar.activation(hi_of(n - N_FIRST), ring[:, n % NRING, :], ACT.Copy).then_inc(w_hi_ready, 1)

        @block.vector
        def _(dve):
            nc.vector.memset(ident[:], 1.0)
            nc.vector.memset(ones[:], 1.0).then_inc(s_const, 1)
            dve.wait_ge(s_cact, 1)
            for n in range(6 * KD + N_WIN):
                dve.wait_ge(ring_in[n % NRING], 16 * (n // NRING + 1))
                if n in w_ins:
                    dve.wait_ge(w_hi_ready, n - N_FIRST + 1)
                    nc.vector.tensor_tensor(out=lo_of(n - N_FIRST), in0=ring[:, n % NRING, :], in1=hi_of(n - N_FIRST).bitcast(f32),
                                            op=ALU.subtract).then_inc(ring_free, 1)
                    continue
                which, k = divmod(adas.index(n), KD)
                a = acc[:, which % 2, :]
                if k:
                    dve.wait_ge(ring_free, n)
                    nc.vector.scalar_tensor_tensor(out=a, in0=ring[:, n % NRING, :], scalar=cact[:, k:k + 1],
                                                   in1=a, op0=ALU.mult, op1=ALU.add).then_inc(ring_free, 1)
                else:
                    if which >= 2:
                        dve.wait_ge(mod_ps_ready, which - 1)
                    nc.vector.tensor_scalar(a, ring[:, n % NRING, :], cact[:, 0:1], None, ALU.mult).then_inc(ring_free, 1)
            dve.wait_ge(mod_ps_ready, 6)
            nc.vector.tensor_tensor(out=mod[:], in0=mod_ps[:, 0:6 * KD], in1=col[:, COL_BADA:COL_BADA + 6 * KD],
                                    op=ALU.add).then_inc(chain, 1)
            dve.wait_ge(chain, 1)
            for which in (SC1, GT1, SC2, GT2):
                part = mod[:, which * KD:(which + 1) * KD]
                nc.vector.tensor_scalar(part, part, 1.0, None, ALU.add).then_inc(chain, 1)
            dve.wait_ge(chain, 5)
            dve.sem_clear(chain)

        @block.gpsimd
        def _(pool):
            pool.wait_ge(s_const, 1)
            nc.gpsimd.affine_select(out=ident[:], in_=ident[:], compare_op=ALU.is_equal, fill=0.0, base=0,
                                    pattern=[[-1, P]], channel_multiplier=1).then_inc(ident_ready, 1)
            pool.wait_ge(ident_ready, 1)

        @block.tensor
        def _(pe):
            pe.wait_ge(s_const, 1)
            for which in range(6):
                n_last = [n for n in range(6 * KD + N_WIN) if n in adas][which * KD + KD - 1]
                pe.wait_ge(ring_free, n_last + 1)
                for j in range(KD):
                    ins = nc.tensor.matmul(mod_ps[:, which * KD + j:which * KD + j + 1], acc[:, which % 2, j * P:(j + 1) * P],
                                           ones[:, 0:1], start=True, stop=True)
                ins.then_inc(mod_ps_ready, 1)


def conv_pool_phase(nc, persist, w_hi, w_lo, xT, pool_w, mix_spill):
    f32, f32r = mybir.dt.float32, mybir.dt.float32r
    ALU, ACT = mybir.AluOpType, mybir.ActivationFunctionType
    mod, col, paced = persist["mod"], persist["col"], persist["paced"]
    SHARED = slice(CG // 2, CG)
    T_DVE = 7
    N_PROD = TAPS - T_DVE
    NPB = 6
    ctx = ExitStack()
    with ctx:
        sb = lambda name, shape, dt=f32: ctx.enter_context(nc.sbuf_tensor(name, shape, dt))
        ps = lambda name, shape: ctx.enter_context(nc.psum_tensor(name, shape, f32))
        sem = lambda name: ctx.enter_context(nc.semaphore(name))

        mean_w = sb("mean_w", [P, P])
        poolw_sb = sb("poolw_sb", [P, CG, P])
        x_raw = sb("x_raw", [P, KD, CH])
        u_hi = [sb(f"u_hi{n}", [P, KD, CH], f32r) for n in range(2)]
        u_lo = [sb(f"u_lo{n}", [P, KD, CH], f32r) for n in range(2)]
        sig = sb("sig", [P, 2, CH])
        v = [sb(f"v{n}", [P, CG, HALO + CH]) for n in range(2)]
        pp = [sb(f"p{n}", [P, CG, PHALO + CH]) for n in range(2)]
        y = [sb(f"y{n}", [P, CG, CH]) for n in range(2)]
        rstd = sb("rstd", [P, CH])
        prod = sb("prod_c", [P, NPB, CG // 2, CH])
        yp = [sb(f"yp{n}", [P, CG // 2, CH]) for n in range(2)]
        eps_col = sb("eps_col", [P, 1])
        s_a = sb("s_a", [P, CG, PHALO + CH])
        s_b = sb("s_b", [P, CG, PHALO + CH])
        mixo = sb("mixo", [P, 2 * CG, CH])
        ysq = mixo[:, 0:CG, :]

        h_ps = [ps(f"h_ps{n}", [P, 512]) for n in range(4)]
        stat_ps = ps("stat_ps", [P, 2, CH])
        yb_ps = [ps(f"yb_ps{n}", [P, 512]) for n in range(2)]

        pool_sum_w = sb("pool_sum_w", [P, CG, P])
        pool_p_w = sb("pool_p_w", [P, CG, P])

        s_poolw = sem("s_poolw")
        poolw_ready = sem("poolw_ready")
        s_const = sem("s_const2")
        x_in = sem("x_in")
        u_ready = sem("u_ready")
        hi_ready = sem("hi_ready")
        u_split = sem("u_split")
        h_ready = sem("h_ready")
        evac_act = sem("evac_act")
        evac_dve = sem("evac_dve")
        conv_pool = sem("conv_pool")
        mean_ready = sem("mean_ready")
        centered = sem("centered")
        squared = sem("squared")
        var_ready = sem("var_ready")
        root_ready = sem("root_ready")
        normed = sem("normed")
        yb_ready = sem("yb_ready")
        mix_ready = sem("mix_ready")
        yb_taken = sem("yb_taken")
        mix_out = sem("mix_out")
        rstd_ready = sem("rstd_ready")
        p_halo = sem("p_halo")
        p_used = sem("p_used")
        prod_ready = sem("prod_ready")
        prod_used = sem("prod_used")
        yp_used = sem("yp_used")
        chain_p = sem("chain_p")
        chain_v = persist["dve_chain"]
        chain_g = sem("chain_g")
        halo_done = sem("halo_done")

        block = ctx.enter_context(nc.Block())

        @block.sync
        def _(sp):
            sp.dma_start(poolw_sb[:], pool_w.rearrange("p (g n) -> p g n", g=CG)).then_inc(s_poolw, 16)
            sp.dma_start(x_raw[:], xT[0].rearrange("p (k n) -> p k n", k=KD)).then_inc(x_in, 16)
            sp.wait_ge(u_split, 1)
            sp.dma_start(x_raw[:], xT[1].rearrange("p (k n) -> p k n", k=KD)).then_inc(x_in, 16)
            with sp.Fori(2, NCH) as c:
                src = xT[bass.ds(c, 1)].rearrange("a p (k n) -> (a p) k n", k=KD)
                sp.wait_ge(u_split, c)
                sp.dma_start(x_raw[:], src).then_inc(x_in, 16)
            sp.wait_ge(x_in, 16 * NCH)

        @block.scalar
        def _(act):
            def modulate(c):
                act.wait_ge(x_in, c * 16 + 16)
                for k in range(KD):
                    ins = nc.scalar.activation(x_raw[:, k, :], x_raw[:, k, :], ACT.Identity,
                                               bias=mod[:, SH1 * KD + k:SH1 * KD + k + 1],
                                               scale=mod[:, SC1 * KD + k:SC1 * KD + k + 1])
                ins.then_inc(u_ready, 1)

            def gate(c, j, first):
                act.wait_ge(h_ready, c * NM + 2 * j + 1)
                if j >= 2:
                    act.wait_ge(evac_dve, c * CG + j - 1)
                elif not first:
                    act.wait_ge(evac_dve, c * CG + j - 1)
                nc.scalar.activation(sig[:, j % 2, :], h_ps[2 * j % 4][:, 0:CH], ACT.Sigmoid,
                                     bias=col[:, COL_BIN + 2 * j:COL_BIN + 2 * j + 1]).then_inc(evac_act, 1)

            def products(c, b, quarter, first):
                for i in range(N_PROD * quarter // 4, N_PROD * (quarter + 1) // 4):
                    if not (first and i < NPB):
                        act.wait_ge(prod_used, (c - 1) * N_PROD + i - NPB + 1)
                    for g in range(CG // 2, CG):
                        t = T_DVE + i
                        w = col[:, COL_CONVW + g * TAPS + t:COL_CONVW + g * TAPS + t + 1]
                        ins = nc.scalar.activation(prod[:, i % NPB, g - CG // 2, :], v[b][:, g, t:t + CH], ACT.Copy, scale=w)
                    ins.then_inc(prod_ready, 1)

            def step(c, half, project=True, conv=True, finish=True, more=True, first=False, store_before=True):
                first_prod = isinstance(c, int) and c == 1
                if project:
                    gate(c, 0, first)
                if conv:
                    act.wait_ge(evac_dve, c * CG)
                    products(c, 1 - half, 0, first_prod)
                if project:
                    gate(c, 1, first)
                if conv:
                    products(c, 1 - half, 1, first_prod)
                if finish:
                    act.wait_ge(centered, c - 1)
                    if store_before:
                        act.wait_ge(mix_out, (c - 2) * 16)
                    nc.scalar.activation(ysq, y[half][:], ACT.Square).then_inc(squared, 1)
                if finish:
                    for g in range(CG):
                        act.wait_ge(yb_ready, (c - 2) * CG + g + 1)
                        nc.scalar.activation(mixo[:, CG + g, :], yb_ps[g % 2][:, g // 2 * CH:(g // 2 + 1) * CH], ACT.Copy,
                                             scale=col[:, COL_PSC + g:COL_PSC + g + 1]).then_inc(yb_taken, 1)
                if project:
                    gate(c, 2, first)
                if conv:
                    products(c, 1 - half, 2, first_prod)
                if project:
                    gate(c, 3, first)
                if finish:
                    act.wait_ge(var_ready, c - 1)
                    nc.scalar.activation(rstd[:], stat_ps[:, 1, :], ACT.Sqrt, bias=eps_col[:, 0:1]).then_inc(root_ready, 1)
                if more:
                    modulate(c + 2)
                if conv:
                    products(c, 1 - half, 3, first_prod)
                if project:
                    if not first:
                        act.wait_ge(p_used, c - 1)
                        act.wait_ge(p_halo, c)
                    for j in range(CG):
                        m = 2 * CG + j
                        act.wait_ge(h_ready, c * NM + m + 1)
                        nc.scalar.activation(pp[half][:, j, PHALO:], h_ps[m % 4][:, 0:CH], ACT.Identity,
                                             bias=col[:, COL_BIN + m:COL_BIN + m + 1]).then_inc(evac_act, 1)
                if finish:
                    act.wait_ge(normed, c - 1)
                    for g in range(CG):
                        nc.scalar.activation(mixo[:, g, :], y[half][:, g, :], ACT.Silu,
                                             bias=col[:, COL_LNB + g:COL_LNB + g + 1],
                                             scale=col[:, COL_LNG + g:COL_LNG + g + 1]).then_inc(mix_ready, 1)
                    dst = mix_spill[bass.ds(c - 2, 1)].rearrange("a p (k n) -> (a p) k n", k=2 * CG)
                    act.wait_ge(mix_ready, (c - 1) * CG)
                    act.wait_ge(yb_taken, (c - 1) * CG)
                    act.dma_start(dst, mixo[:]).then_inc(mix_out, 16)

            act.wait_ge(s_const, 1)
            modulate(0)
            modulate(1)
            step(0, 0, conv=False, finish=False, first=True)
            step(1, 1, finish=False)
            step(2, 0, store_before=False)
            step(3, 1)
            with act.Fori(4, NCH - 2, 2) as c0:
                step(c0, 0)
                step(c0 + 1, 1)
            step(NCH - 2, 0, more=False)
            step(NCH - 1, 1, more=False)
            step(NCH, 0, project=False, more=False)
            step(NCH + 1, 1, project=False, conv=False, more=False)
            act.wait_ge(mix_out, 16 * NCH)

        @block.vector
        def _(dve):
            nc.vector.memset(mean_w[:], 1.0 / CW)
            nc.vector.memset(eps_col[:], EPS)
            for b in range(2):
                nc.vector.memset(v[b][:], 0.0)
                nc.vector.memset(pp[b][:], 0.0)
            nc.vector.memset(s_a[:], 0.0)
            nc.vector.memset(s_b[:], 0.0).then_inc(s_const, 1)

            def split(c, half):
                dve.wait_ge(u_ready, c + 1)
                nc.vector.tensor_copy(u_hi[half][:], x_raw[:]).then_inc(hi_ready, 1)
                dve.wait_ge(hi_ready, c + 1)
                nc.vector.tensor_tensor(out=u_lo[half][:], in0=x_raw[:], in1=u_hi[half][:].bitcast(f32),
                                        op=ALU.subtract).then_inc(u_split, 1)

            def evac(c, half, j):
                m = 2 * j + 1
                dve.wait_ge(h_ready, c * NM + m + 1)
                dve.wait_ge(evac_act, c * 2 * CG + j + 1)
                nc.vector.scalar_tensor_tensor(out=v[half][:, j, HALO:], in0=h_ps[m % 4][:, 0:CH],
                                               scalar=col[:, COL_BIN + m:COL_BIN + m + 1], in1=sig[:, j % 2, :],
                                               op0=ALU.add, op1=ALU.mult).then_inc(evac_dve, 1)

            order = [(t, g) for t in range(TAPS) for g in range(CG) if g < CG // 2 or t < T_DVE]

            def taps(b, quarter):
                for i in range(len(order) * quarter // 4, len(order) * (quarter + 1) // 4):
                    t, g = order[i]
                    w = col[:, COL_CONVW + g * TAPS + t:COL_CONVW + g * TAPS + t + 1]
                    if t == 0:
                        ins = nc.vector.tensor_scalar(y[b][:, g, :], v[b][:, g, 0:CH], w,
                                                      col[:, COL_CONVB + g:COL_CONVB + g + 1], ALU.mult, ALU.add)
                    else:
                        dve.wait_ge(chain_v, order.index((t - 1, g)) + 1)
                        ins = nc.vector.scalar_tensor_tensor(out=y[b][:, g, :], in0=v[b][:, g, t:t + CH], scalar=w,
                                                             in1=y[b][:, g, :], op0=ALU.mult, op1=ALU.add)
                    ins.then_inc(chain_v, 1)

            def step(c, half, project=True, conv=True, finish=True, more=True, first=False, y_reused=True):
                if more:
                    if not first:
                        dve.wait_ge(h_ready, c * NM)
                    split(c + 1, 1 - half)
                if finish:
                    dve.wait_ge(conv_pool, c - 1)
                    nc.vector.tensor_tensor(out=y[half][:, SHARED, :], in0=y[half][:, SHARED, :], in1=yp[half][:],
                                            op=ALU.add).then_inc(yp_used, 1)
                if conv:
                    dve.wait_ge(evac_dve, c * CG)
                    if y_reused:
                        dve.wait_ge(mix_ready, (c - 2) * CG)
                for j in range(CG):
                    if project:
                        evac(c, half, j)
                    if conv:
                        taps(1 - half, j)
                    if finish and j == 0:
                        dve.wait_ge(mean_ready, c - 1)
                        nc.vector.tensor_tensor(out=y[half][:], in0=y[half][:],
                                                in1=stat_ps[:, 0:1, :].broadcast_to([P, CG, CH]),
                                                op=ALU.subtract).then_inc(centered, 1)
                    if finish and j == 2:
                        dve.wait_ge(root_ready, c - 1)
                        nc.vector.reciprocal(rstd[:], rstd[:]).then_inc(rstd_ready, 1)
                    if finish and j == 3:
                        dve.wait_ge(rstd_ready, c - 1)
                        nc.vector.tensor_tensor(out=y[half][:], in0=y[half][:],
                                                in1=rstd[:].rearrange("p (a n) -> p a n", a=1).broadcast_to([P, CG, CH]),
                                                op=ALU.mult).then_inc(normed, 1)
                if conv:
                    dve.wait_ge(chain_v, len(order))
                    dve.sem_clear(chain_v)
                if more:
                    if not first:
                        dve.wait_ge(prod_ready, c * N_PROD)
                    dve.wait_ge(evac_dve, c * CG + CG)
                    nc.vector.tensor_copy(v[1 - half][:, :, 0:HALO], v[half][:, :, CH:CH + HALO]).then_inc(halo_done, 1)
                    dve.wait_ge(halo_done, c + 1)

            split(0, 0)
            step(0, 0, conv=False, finish=False, first=True)
            step(1, 1, finish=False, y_reused=False)
            step(2, 0, y_reused=False)
            step(3, 1)
            with dve.Fori(4, NCH - 2, 2) as c0:
                step(c0, 0)
                step(c0 + 1, 1)
            step(NCH - 2, 0)
            step(NCH - 1, 1, more=False)
            step(NCH, 0, project=False, more=False)
            step(NCH + 1, 1, project=False, conv=False, more=False)

        @block.gpsimd
        def _(pool):
            pool.wait_ge(s_const, 1)

            pool.wait_ge(s_poolw, 16)
            for g in range(CG):
                nc.gpsimd.tensor_scalar(pool_sum_w[:, g, :], poolw_sb[:, g, :], 1.0 / WINDOWS[g], None, ALU.mult)
            nc.gpsimd.tensor_scalar(pool_p_w[:], poolw_sb[:], -1.0, None, ALU.mult).then_inc(poolw_ready, 1)

            def add(c, half, i, first):
                if i == 1 and not first:
                    pool.wait_ge(yp_used, c - 1)
                pool.wait_ge(prod_ready, c * N_PROD + i + 1)
                if i > 1:
                    pool.wait_ge(chain_g, i - 1)
                so_far = prod[:, 0] if i == 1 else yp[half][:]
                nc.gpsimd.tensor_tensor(out=yp[half][:], in0=so_far, in1=prod[:, i % NPB], op=ALU.add).then_inc(chain_g, 1)
                pool.wait_ge(chain_g, i)
                pool.sem_inc(prod_used, 2 if i == 1 else 1)

            def step(c, half, first=False):
                p_now, at = pp[half], lambda g: s_b if g % 2 else s_a
                for i in range(1, 4):
                    add(c, half, i, isinstance(c, int) and c < 2)
                pool.wait_ge(evac_act, c * 2 * CG + 2 * CG)
                pool.sem_inc(paced, 1)
                nc.gpsimd.tensor_copy(pp[1 - half][:, :, 0:PHALO], p_now[:, :, CH:CH + PHALO]).then_inc(p_halo, 1)
                if not first:
                    pool.wait_ge(yb_ready, c * CG)
                done = 0
                for g in range(CG):
                    step_back, start = 1 << g, (1 << (g + 1)) - 1
                    prior = at(g - 1) if g else p_now
                    if g:
                        pool.wait_ge(chain_p, done)
                    nc.gpsimd.tensor_tensor(out=at(g)[:, g:, start:], in0=prior[:, g:, start:],
                                            in1=prior[:, g:, start - step_back:PHALO + CH - step_back],
                                            op=ALU.add).then_inc(chain_p, 1)
                    done += 1
                    for i in range(4 + 2 * g, 6 + 2 * g):
                        add(c, half, i, False)
                pool.wait_ge(chain_p, done)
                for g in range(CG):
                    s_g = at(g)[:, g, PHALO:2 * PHALO]
                    nc.gpsimd.tensor_tensor(out=s_g, in0=s_g, in1=col[:, COL_FIX + g * PHALO:COL_FIX + (g + 1) * PHALO],
                                            op=ALU.mult).then_inc(chain_p, 1)
                done += CG
                pool.wait_ge(chain_p, done)
                nc.gpsimd.memset(col[:, COL_FIX:COL_FIX + CG * PHALO], 1.0).then_inc(chain_p, 1)
                pool.wait_ge(chain_p, done + 1)
                pool.sem_clear(chain_p)
                pool.sem_inc(p_used, 1)
                for i in range(12, N_PROD):
                    add(c, half, i, False)
                pool.wait_ge(chain_g, N_PROD - 1)
                pool.sem_clear(chain_g)
                pool.sem_inc(conv_pool, 1)

            step(0, 0, first=True)
            step(1, 1)
            with pool.Fori(2, NCH, 2) as c0:
                step(c0, 0)
                step(c0 + 1, 1)

        @block.tensor
        def _(pe):
            pe.wait_ge(s_const, 1)
            pe.wait_ge(poolw_ready, 1)

            def step(c, half, project=True, finish=True, first=False, first_use=False):
                if finish:
                    pe.wait_ge(p_used, c - 1)
                    for g in range(CG):
                        if g == 0 and not first_use:
                            pe.wait_ge(yb_taken, (c - 2) * CG)
                        out = yb_ps[g % 2][:, g // 2 * CH:(g // 2 + 1) * CH]
                        nc.tensor.matmul(out, pool_sum_w[:, g, :], (s_b if g % 2 else s_a)[:, g, PHALO:], start=True, stop=False)
                        nc.tensor.matmul(out, pool_p_w[:, g, :], pp[half][:, g, PHALO:], start=False, stop=True).then_inc(yb_ready, 1)
                for m in range(NM):
                    if m == 2 and finish:
                        pe.wait_ge(yp_used, c - 1)
                        for g in range(CG):
                            ins = nc.tensor.matmul(stat_ps[:, 0, :], mean_w[:], y[half][:, g, :], start=(g == 0), stop=(g == CG - 1))
                        ins.then_inc(mean_ready, 1)
                    if m == 6 and finish:
                        pe.wait_ge(squared, c - 1)
                        for g in range(CG):
                            ins = nc.tensor.matmul(stat_ps[:, 1, :], mean_w[:], ysq[:, g, :], start=(g == 0), stop=(g == CG - 1))
                        ins.then_inc(var_ready, 1)
                    if not project:
                        continue
                    if m == 0:
                        pe.wait_ge(u_split, c + 1)
                    if m < 4:
                        if not first:
                            pe.wait_ge(evac_act, (c - 1) * 2 * CG + CG + m + 1)
                    elif m % 2:
                        pe.wait_ge(evac_dve, c * CG + (m - 4) // 2 + 1)
                    else:
                        pe.wait_ge(evac_act, c * 2 * CG + (m - 4) // 2 + 1)
                    out = h_ps[m % 4][:, 0:CH]
                    for k in range(KD):
                        w_h, w_l = w_hi[:, k, m * P:(m + 1) * P], w_lo[:, k, m * P:(m + 1) * P]
                        nc.tensor.matmul(out, w_h, u_hi[half][:, k, :], start=(k == 0), stop=False)
                        nc.tensor.matmul(out, w_h, u_lo[half][:, k, :], start=False, stop=False)
                        ins = nc.tensor.matmul(out, w_l, u_hi[half][:, k, :], start=False, stop=(k == KD - 1))
                    ins.then_inc(h_ready, 1)

            step(0, 0, finish=False, first=True)
            step(1, 1, finish=False)
            step(2, 0, first_use=True)
            step(3, 1)
            with pe.Fori(4, NCH, 2) as c0:
                step(c0, 0)
                step(c0 + 1, 1)
            step(NCH, 0, project=False)
            step(NCH + 1, 1, project=False)


def mix_router_phase(nc, persist, x, w_out, rows, w_router, router_bias, mix_spill, x1_dram, u2_dram, list_dram, y_dram):
    f32, f32r, bf16, i32 = mybir.dt.float32, mybir.dt.float32r, mybir.dt.bfloat16, mybir.dt.int32
    ALU, ACT, AX = mybir.AluOpType, mybir.ActivationFunctionType, mybir.AxisListType
    ident, mod, paced = persist["ident"], persist["mod"], persist["paced"]
    m1_all, m2_all, w_all, idx_all, run = (persist[n] for n in ("m1_all", "m2_all", "w_all", "idx_all", "run"))

    ctx = ExitStack()
    with ctx:
        sb = lambda name, shape, dt=f32: ctx.enter_context(nc.sbuf_tensor(name, shape, dt))
        ps = lambda name, shape: ctx.enter_context(nc.psum_tensor(name, shape, f32))
        sem = lambda name: ctx.enter_context(nc.semaphore(name))

        wo_raw = sb("wo_raw", [P, KD, D])
        wo_hi = sb("wo_hi", [P, KD, D], f32r)
        wo_lo = sb("wo_lo", [P, KD, D], f32r)
        spread = wo_raw[:, 0, :].rearrange("p (k n) -> p k n", k=KD)
        g_x1 = sb("g_x1", [P, D])
        b_x1 = sb("b_x1", [P, D])
        g_u2 = sb("g_u2", [P, D])
        b_u2 = sb("b_u2", [P, D])
        b_mix = sb("b_mix", [P, D])
        g1_row = sb("g1_row", [P, D])
        bc = sb("bc", [P, KD, P])
        wr = sb("wr", [P, KD, NE])
        rbias = sb("rbias", [P, NE])
        mix_raw = [sb(f"mix_raw{n}", [P, KD, P]) for n in range(2)]
        mix_hi = [sb(f"mix_hi{n}", [P, KD, P], f32r) for n in range(2)]
        mix_lo = [sb(f"mix_lo{n}", [P, KD, P], f32r) for n in range(2)]
        xt = [sb(f"xt{n}", [P, D]) for n in range(2)]
        z = [sb(f"z{n}", [P, D]) for n in range(2)]
        x1 = sb("x1", [P, D])
        u2 = [sb(f"u2{n}", [P, D]) for n in range(2)]
        u2T = sb("u2T", [P, KD, P])
        stats = sb("stats", [P, 2, 6])
        mv = [sb(f"mv{n}", [P, 2]) for n in range(2)]
        root = sb("root", [P, 1])
        rstd = [sb(f"rstd1{n}", [P, 1]) for n in range(2)]
        eps_col = sb("eps_col1", [P, 1])
        sc = sb("sc", [P, 2, NE])
        sel = sb("sel", [P, 2, NE])
        key = sb("key", [P, 2, NE])
        o1 = sb("o1", [P, 2, NE])
        o2 = sb("o2", [P, 2, NE])
        mb = sb("mb", [P, 2, NE], bf16)
        kd = sb("kd", [P, EPG])
        top1 = sb("top1", [P, 2 * NG])
        top2 = sb("top2", [P, 2 * NG])
        kmax = sb("kmax", [P, 2 * NG])
        gsum = sb("gsum", [P, 2, NG])
        gmax = sb("gmax", [P, 2])
        picked = sb("picked", [P, 2, 2])
        den = sb("den", [P, 2])
        pose = sb("pose", [P, 2, NE])
        idx_i = sb("idx_i", [P, 2, 2], i32)
        tok_f = sb("tok_f", [P, 2])
        tok_i = sb("tok_i", [P, 2], i32)
        tri = sb("tri", [P, P], bf16)
        ones_b = sb("ones_b", [P, P], bf16)
        zero_i = sb("zero_i", [P, NE * SEQ // P], i32)

        mm_ps = [ps(f"mm_ps{n}", [P, D]) for n in range(2)]
        tr_ps = ps("tr_ps", [P, D])
        rt_ps = ps("rt_ps", [P, 512])
        pos_ps = ps("pos_ps", [P, 3, NE])

        s_wo = sem("s_wo")
        s_rows = sem("s_rows")
        s_cst = sem("s_cst")
        s_tri = sem("s_tri")
        s_zero = sem("s_zero")
        s_fill = sem("s_fill")
        bc_ready = sem("bc_ready")
        row_ps = sem("row_ps")
        row_taken = sem("row_taken")
        wo_scaled = sem("wo_scaled")
        wo_h = sem("wo_h")
        wo_done = sem("wo_done")
        mix_in = [sem(f"mix_in{n}") for n in range(2)]
        xt_in = [sem(f"xt_in{n}") for n in range(2)]
        hi_done = sem("hi_done")
        lo_done = sem("lo_done")
        xb_done = sem("xb_done")
        mm_done = sem("mm_done")
        z_done = sem("z_done")
        stat_done = sem("stat_done")
        root_done = sem("root_done")
        rstd_done = sem("rstd_done")
        xa_done = sem("xa_done")
        x1_norm = sem("x1_norm")
        x1_half = sem("x1_half")
        x1_done = sem("x1_done")
        x1_out = sem("x1_out")
        u2_half = sem("u2_half")
        u2_done = sem("u2_done")
        u2_out = [sem(f"u2_out{n}") for n in range(2)]
        tr_done = sem("tr_done")
        u2T_done = sem("u2T_done")
        logit_done = sem("logit_done")
        sc_done = sem("sc_done")
        m_done = sem("m_done")
        pos_done = sem("pos_done")
        idx_done = sem("idx_done")
        scatter = sem("scatter")
        ch = persist["dve_chain"]
        chp = sem("chp")

        block = ctx.enter_context(nc.Block())
        mix_t = mix_spill.rearrange("c p (k h n) -> c h p k n", k=KD, h=TPC)
        x_t = x.rearrange("(t p) d -> t p d", p=P)
        x1_t = x1_dram.rearrange("(t p) d -> t p d", p=P)
        u2_t = u2_dram.rearrange("(t p) d -> t p d", p=P)

        @block.sync
        def _(sp):
            for n, row in enumerate((g_x1, b_x1, b_mix)):
                src = rows[{0: ROW_G1, 1: ROW_B1, 2: ROW_BOUT}[n]:{0: ROW_G1, 1: ROW_B1, 2: ROW_BOUT}[n] + 1, :]
                sp.dma_start(row[:], src.broadcast_to([P, D])).then_inc(s_rows, 16)
            sp.dma_start(rbias[:], router_bias.broadcast_to([P, NE])).then_inc(s_rows, 16)
            sp.dma_start(wr[:], w_router.rearrange("p (k n) -> p k n", k=KD)).then_inc(s_rows, 16)
            for k in range(KD):
                sp.dma_start(wo_raw[:, k, :], w_out[k]).then_inc(s_wo, 16)
            for t in range(2):
                sp.dma_start(mix_raw[t][:], mix_t[0, t]).then_inc(mix_in[t], 16)
                sp.dma_start(xt[t][:], x_t[t]).then_inc(xt_in[t], 16)
            sp.wait_ge(s_cst, 1)
            sp.dma_start(list_dram.rearrange("(p n) a -> p (n a)", p=P), zero_i[:]).then_inc(s_zero, 16)

            zeros = zero_i[:].bitcast(f32).rearrange("p (a n) -> p a n", a=1)
            fill = y_dram[NE * P:, :].rearrange("(r p a) (b n) -> r p (a b) n", p=P, r=NT // 2, n=zeros.shape[2])
            sp.dma_start(fill[0], zeros.broadcast_to([P, fill.shape[2], fill.shape[3]])).then_inc(s_fill, 16)
            with sp.Fori(1, NT // 2) as q:
                t0 = q * 2
                for half in range(2):
                    t = t0 + half
                    src_m = mix_t[bass.ds(q, 1), half].rearrange("a p k n -> (a p) k n")
                    src_x = x_t[bass.ds(t, 1)].rearrange("a p d -> (a p) d")
                    sp.wait_ge(lo_done, t - 1)
                    sp.dma_start(mix_raw[half][:], src_m).then_inc(mix_in[half], 16)
                    sp.wait_ge(z_done, t - 1)
                    sp.dma_start(xt[half][:], src_x).then_inc(xt_in[half], 16)
                sp.dma_start(fill[bass.ds(q, 1)].rearrange("r p a n -> (r p) a n"),
                             zeros.broadcast_to([P, fill.shape[2], fill.shape[3]])).then_inc(s_fill, 16)
            sp.wait_ge(s_zero, 16)
            sp.wait_ge(s_fill, 16 * (NT // 2))

        @block.scalar
        def _(act):
            act.wait_ge(s_cst, 1)

            def hi(t, half):
                act.wait_ge(mix_in[half], (t // 2) * 16 + 16)
                nc.scalar.activation(mix_hi[half][:], mix_raw[half][:], ACT.Copy).then_inc(hi_done, 1)

            def finish(t, half, first=False):
                act.wait_ge(tr_done, t + 1)
                nc.scalar.activation(u2T[:], tr_ps[:].rearrange("p (k n) -> p k n", k=KD), ACT.Copy).then_inc(u2T_done, 1)
                act.wait_ge(logit_done, t + 1)
                if half == 0 and not first:
                    act.wait_ge(idx_done, (t // 2))
                nc.scalar.activation(sc[:, half, :], rt_ps[:, 0:NE], ACT.Sigmoid).then_inc(sc_done, 1)

            def step(t, half, more=True, first=False, first_pair=False):
                if more:
                    if not first:
                        act.wait_ge(mm_done, t)
                    hi(t + 1, 1 - half)
                act.wait_ge(stat_done, t + 1)
                nc.scalar.activation(root[:], mv[half][:, 1:2], ACT.Sqrt, bias=eps_col[:, 0:1]).then_inc(root_done, 1)
                if not first:
                    finish(t - 1, 1 - half, first=first_pair)

            hi(0, 0)
            step(0, 0, first=True)
            step(1, 1, first_pair=True)
            step(2, 0)
            step(3, 1)
            with act.Fori(2, NT // 2 - 1) as q:
                t0 = q * 2
                step(t0, 0)
                step(t0 + 1, 1)
            step(NT - 2, 0)
            step(NT - 1, 1, more=False)
            finish(NT - 1, 1)

        @block.vector
        def _(dve):
            chained = [0]

            def link(ins):
                ins.then_inc(ch, 1)
                chained[0] += 1

            def settle():
                dve.wait_ge(ch, chained[0])

            def reset():
                settle()
                dve.sem_clear(ch)
                chained[0] = 0

            nc.vector.memset(zero_i[:], 0)
            nc.vector.memset(eps_col[:], EPS)
            nc.vector.memset(ones_b[:], 1.0)
            nc.vector.memset(tri[:], 1.0)
            for n in range(EPG):
                nc.vector.memset(kd[:, n:n + 1], float(EPG - n))
            nc.vector.memset(tok_i[:], 0)
            for e in range(NE):
                nc.vector.memset(run[:, e:e + 1], float(e * SEQ))
            nc.vector.memset(root[:], 0.0).then_inc(s_cst, 1)

            dve.wait_ge(s_rows, 16 * 5)
            dve.wait_ge(s_cst, 1)
            n = 0
            for which in (GT1, SC2, SH2):
                if n:
                    dve.wait_ge(row_ps, n)
                link(nc.vector.tensor_copy(bc[:], mod[:, which * KD:(which + 1) * KD].rearrange("p (k a) -> p k a", a=1)
                                           .broadcast_to([P, KD, P])))
                settle()
                dve.sem_inc(bc_ready, 1)
                n += 1
                dve.wait_ge(row_ps, n)
                if which == GT1:
                    link(nc.vector.tensor_copy(g1_row[:], tr_ps[:]))
                    settle()
                    link(nc.vector.tensor_tensor(out=b_mix[:], in0=b_mix[:], in1=g1_row[:], op=ALU.mult))
                elif which == SC2:
                    link(nc.vector.tensor_tensor(out=g_u2[:], in0=tr_ps[:], in1=g_x1[:], op=ALU.mult))
                    link(nc.vector.tensor_tensor(out=b_u2[:], in0=tr_ps[:], in1=b_x1[:], op=ALU.mult))
                else:
                    link(nc.vector.tensor_tensor(out=b_u2[:], in0=tr_ps[:], in1=b_u2[:], op=ALU.add))
                settle()
                dve.sem_inc(row_taken, 1)
            link(nc.vector.tensor_scalar(g_x1[:], g_x1[:], ALPHA, None, ALU.mult))
            link(nc.vector.tensor_scalar(b_x1[:], b_x1[:], ALPHA, None, ALU.mult))
            dve.wait_ge(s_wo, 16 * KD)
            for k in range(KD):
                nc.vector.tensor_tensor(out=wo_raw[:, k, :], in0=wo_raw[:, k, :], in1=g1_row[:], op=ALU.mult).then_inc(wo_scaled, 1)
            for k in range(KD):
                dve.wait_ge(wo_scaled, k + 1)
                nc.vector.tensor_copy(wo_hi[:, k, :], wo_raw[:, k, :]).then_inc(wo_h, 1)
            for k in range(KD):
                dve.wait_ge(wo_h, k + 1)
                nc.vector.tensor_tensor(out=wo_lo[:, k, :], in0=wo_raw[:, k, :], in1=wo_hi[:, k, :].bitcast(f32),
                                        op=ALU.subtract).then_inc(wo_done, 1)
            reset()

            def lo(t, half):
                dve.wait_ge(hi_done, t + 1)
                nc.vector.tensor_tensor(out=mix_lo[half][:], in0=mix_raw[half][:], in1=mix_hi[half][:].bitcast(f32),
                                        op=ALU.subtract).then_inc(lo_done, 1)

            def grouped(ap):
                return ap.rearrange("p a (g e) -> p (a g) e", g=NG)

            def spread_to(ap, n):
                return ap.rearrange("p (a b) -> p a b", b=1).broadcast_to([P, ap.shape[1], n])

            def best(values, top, out):
                link(nc.vector.tensor_reduce(out=top[:], in_=grouped(values[:]), axis=AX.X, op=ALU.max))
                settle()
                link(nc.vector.tensor_tensor(out=grouped(key[:]), in0=grouped(values[:]), in1=spread_to(top[:], EPG), op=ALU.is_ge))
                settle()
                link(nc.vector.tensor_tensor(out=grouped(key[:]), in0=grouped(key[:]),
                                             in1=kd[:].rearrange("p (a e) -> p a e", a=1).broadcast_to([P, 2 * NG, EPG]), op=ALU.mult))
                settle()
                link(nc.vector.tensor_reduce(out=kmax[:], in_=grouped(key[:]), axis=AX.X, op=ALU.max))
                settle()
                link(nc.vector.tensor_tensor(out=grouped(out[:]), in0=grouped(key[:]), in1=spread_to(kmax[:], EPG), op=ALU.is_equal))
                settle()

            def choose(pair):
                dve.wait_ge(sc_done, 2 * pair + 2)
                link(nc.vector.tensor_tensor(out=sel[:], in0=sc[:], in1=rbias[:].rearrange("p (a e) -> p a e", a=1)
                                             .broadcast_to([P, 2, NE]), op=ALU.add))
                settle()
                best(sel, top1, o1)
                link(nc.vector.scalar_tensor_tensor(out=sel[:], in0=o1[:], scalar=-BIG, in1=sel[:], op0=ALU.mult, op1=ALU.add))
                settle()
                best(sel, top2, o2)
                gs = gsum[:].rearrange("p a g -> p (a g)")
                link(nc.vector.tensor_tensor(out=gs, in0=top1[:], in1=top2[:], op=ALU.add))
                settle()
                link(nc.vector.tensor_reduce(out=gmax[:], in_=gsum[:], axis=AX.X, op=ALU.max))
                settle()
                link(nc.vector.tensor_tensor(out=gsum[:], in0=gsum[:], in1=spread_to(gmax[:], NG), op=ALU.is_ge))
                settle()
                link(nc.vector.tensor_tensor(out=gsum[:], in0=gsum[:], in1=kd[:, 0:NG].rearrange("p (a e) -> p a e", a=1)
                                             .broadcast_to([P, 2, NG]), op=ALU.mult))
                settle()
                link(nc.vector.tensor_reduce(out=gmax[:], in_=gsum[:], axis=AX.X, op=ALU.max))
                settle()
                link(nc.vector.tensor_tensor(out=gsum[:], in0=gsum[:], in1=spread_to(gmax[:], NG), op=ALU.is_equal))
                settle()
                link(nc.vector.tensor_tensor(out=grouped(o1[:]), in0=grouped(o1[:]), in1=spread_to(gs, EPG), op=ALU.mult))
                link(nc.vector.tensor_tensor(out=grouped(o2[:]), in0=grouped(o2[:]), in1=spread_to(gs, EPG), op=ALU.mult))
                settle()
                link(nc.vector.tensor_tensor(out=mb[:], in0=o1[:], in1=o2[:], op=ALU.add))
                settle()
                dve.sem_inc(m_done, 1)
                for n, o in enumerate((o1, o2)):
                    link(nc.vector.tensor_tensor(out=key[:], in0=sc[:], in1=o[:], op=ALU.mult))
                    settle()
                    link(nc.vector.tensor_reduce(out=picked[:, n, :], in_=key[:], axis=AX.X, op=ALU.add))
                    settle()
                link(nc.vector.tensor_tensor(out=den[:], in0=picked[:, 0, :], in1=picked[:, 1, :], op=ALU.add))
                settle()
                link(nc.vector.reciprocal(den[:], den[:]))
                settle()
                for n in range(2):
                    link(nc.vector.tensor_tensor(out=w_all[:, n, bass.ds(pair * 2, 2)], in0=picked[:, n, :], in1=den[:], op=ALU.mult))

            def place(pair, first=False):
                dve.wait_ge(pos_done, pair + 1)
                link(nc.vector.tensor_tensor(out=pose[:], in0=pos_ps[:, 0:2, :], in1=run[:].rearrange("p (a e) -> p a e", a=1)
                                             .broadcast_to([P, 2, NE]), op=ALU.add))
                settle()
                link(nc.vector.tensor_tensor(out=run[:], in0=run[:], in1=pos_ps[:, 2, :], op=ALU.add))
                if not first:
                    dve.wait_ge(scatter, pair * 64)
                for n, (o, keep) in enumerate(((o1, m1_all), (o2, m2_all))):
                    link(nc.vector.tensor_copy(keep[:, bass.ds(pair * 2, 2), :], o[:]))
                    link(nc.vector.tensor_tensor(out=key[:], in0=pose[:], in1=o[:], op=ALU.mult))
                    settle()
                    link(nc.vector.tensor_reduce(out=picked[:, n, :], in_=key[:], axis=AX.X, op=ALU.add))
                    settle()
                link(nc.vector.tensor_copy(idx_all[:, :, bass.ds(pair * 2, 2)], picked[:]))
                link(nc.vector.tensor_copy(idx_i[:], picked[:]))
                link(nc.vector.tensor_copy(tok_i[:], tok_f[:]))
                settle()
                link(nc.vector.tensor_scalar(tok_f[:], tok_f[:], float(2 * P), None, ALU.add))
                settle()
                dve.sem_inc(idx_done, 1)

            def step(t, half, more=True, first=False, reused=True, route=None, first_pair=False):
                if more:
                    if not first:
                        dve.wait_ge(mm_done, t)
                    lo(t + 1, 1 - half)
                if route is not None:
                    choose(route)
                dve.wait_ge(xb_done, t + 1)
                dve.wait_ge(mm_done, t + 1)
                if reused:
                    dve.wait_ge(x1_done, t - 1)
                nc.vector.tensor_tensor(out=z[half][:], in0=mm_ps[half][:], in1=xt[half][:], op=ALU.add).then_inc(z_done, 1)
                dve.wait_ge(z_done, t + 1)
                for n in range(2):
                    link(nc.vector.bn_stats(stats[:, n, :], z[half][:, n * 512:(n + 1) * 512]))
                settle()
                nc.vector.bn_aggr(mv[half][:], stats[:]).then_inc(stat_done, 1)
                dve.wait_ge(stat_done, t + 1)
                if reused:
                    dve.wait_ge(u2_out[half], (t // 2) * 16)
                    dve.wait_ge(tr_done, t - 1)
                nc.vector.scalar_tensor_tensor(out=u2[half][:], in0=z[half][:], scalar=mv[half][:, 0:1], in1=g_u2[:],
                                               op0=ALU.subtract, op1=ALU.mult).then_inc(u2_half, 1)
                dve.wait_ge(root_done, t + 1)
                nc.vector.reciprocal(rstd[half][:], root[:]).then_inc(rstd_done, 1)
                dve.wait_ge(rstd_done, t + 1)
                dve.wait_ge(u2_half, t + 1)
                nc.vector.scalar_tensor_tensor(out=u2[half][:], in0=u2[half][:], scalar=rstd[half][:, 0:1], in1=b_u2[:],
                                               op0=ALU.mult, op1=ALU.add).then_inc(u2_done, 1)
                if route is not None:
                    place(route, first=first_pair)
                reset()

            lo(0, 0)
            dve.wait_ge(s_tri, 2)
            step(0, 0, first=True, reused=False)
            step(1, 1, reused=False)
            step(2, 0)
            step(3, 1, route=0, first_pair=True)
            with dve.Fori(2, NT // 2 - 1) as q:
                t0 = q * 2
                step(t0, 0)
                step(t0 + 1, 1, route=q - 1)
            step(NT - 2, 0)
            step(NT - 1, 1, more=False, route=NT // 2 - 2)
            choose(NT // 2 - 1)
            place(NT // 2 - 1)
            reset()

        @block.gpsimd
        def _(pool):
            pool.wait_ge(s_cst, 1)
            nc.gpsimd.affine_select(out=tri[:], in_=tri[:], compare_op=ALU.is_ge, fill=0.0, base=-1,
                                    pattern=[[1, P]], channel_multiplier=-1).then_inc(s_tri, 1)
            nc.gpsimd.iota(tok_i[:], pattern=[[P, 2]], base=0, channel_multiplier=1).then_inc(chp, 1)
            pool.wait_ge(chp, 1)
            nc.gpsimd.tensor_copy(tok_f[:], tok_i[:]).then_inc(s_tri, 1)
            pool.wait_ge(s_zero, 16)

            def xb(t, half):
                pool.wait_ge(xt_in[half], (t // 2) * 16 + 16)
                pool.sem_inc(paced, 1)
                nc.gpsimd.tensor_scalar(xt[half][:], xt[half][:], ALPHA, None, ALU.mult).then_inc(xa_done, 1)
                pool.wait_ge(xa_done, t + 1)
                nc.gpsimd.tensor_tensor(out=xt[half][:], in0=xt[half][:], in1=b_mix[:], op=ALU.add).then_inc(xb_done, 1)

            def send(pair):
                pool.wait_ge(idx_done, pair + 1)
                pool.sem_inc(paced, 1)
                for n in range(2):
                    for half in range(2):
                        nc.gpsimd.indirect_dma_start(out=list_dram, out_offset=bass.IndirectOffsetOnAxis(ap=idx_i[:, n, half:half + 1], axis=0),
                                                     in_=tok_i[:, half:half + 1], in_offset=None).then_inc(scatter, 16)

            def step(t, half, more=True, first=False, route=None):
                if more:
                    xb(t + 1, 1 - half)
                pool.wait_ge(rstd_done, t + 1)
                if not first:
                    pool.wait_ge(x1_out, t * 16)
                pool.sem_inc(paced, 1)
                nc.gpsimd.tensor_scalar(x1[:], z[half][:], mv[half][:, 0:1], rstd[half][:, 0:1], ALU.subtract, ALU.mult).then_inc(x1_norm, 1)
                pool.wait_ge(x1_norm, t + 1)
                nc.gpsimd.tensor_tensor(out=x1[:], in0=x1[:], in1=g_x1[:], op=ALU.mult).then_inc(x1_half, 1)
                pool.wait_ge(x1_half, t + 1)
                nc.gpsimd.tensor_tensor(out=x1[:], in0=x1[:], in1=b_x1[:], op=ALU.add).then_inc(x1_done, 1)
                dst_x = x1_t[bass.ds(t, 1)].rearrange("a p d -> (a p) d")
                dst_u = u2_t[bass.ds(t, 1)].rearrange("a p d -> (a p) d")
                pool.wait_ge(u2_done, t + 1)
                pool.wait_ge(x1_done, t + 1)
                pool.sem_inc(paced, 1)
                pool.dma_start(dst_u, u2[half][:]).then_inc(u2_out[half], 16)
                pool.dma_start(dst_x, x1[:]).then_inc(x1_out, 16)
                if route is not None:
                    send(route)

            pool.wait_ge(wo_done, KD)
            xb(0, 0)
            step(0, 0, first=True)
            step(1, 1)
            step(2, 0)
            step(3, 1, route=0)
            with pool.Fori(2, NT // 2 - 1) as q:
                t0 = q * 2
                step(t0, 0)
                step(t0 + 1, 1, route=q - 1)
            step(NT - 2, 0)
            step(NT - 1, 1, more=False, route=NT // 2 - 2)
            send(NT // 2 - 1)
            pool.wait_ge(scatter, 64 * (NT // 2))
            pool.wait_ge(x1_out, 16 * NT)
            for half in range(2):
                pool.wait_ge(u2_out[half], 16 * NT // 2)

        @block.tensor
        def _(pe):
            for n in range(3):
                pe.wait_ge(bc_ready, n + 1)
                if n:
                    pe.wait_ge(row_taken, n)
                for k in range(KD):
                    ins = nc.tensor.matmul(tr_ps[:, k * P:(k + 1) * P], bc[:, k, :], ident[:], start=True, stop=True)
                ins.then_inc(row_ps, 1)
            pe.wait_ge(row_taken, 3)
            pe.wait_ge(wo_done, KD)
            pe.wait_ge(s_tri, 2)

            def product(t, half, reused):
                pe.wait_ge(lo_done, t + 1)
                if reused:
                    pe.wait_ge(z_done, t - 1)
                for part in range(2):
                    cols = slice(part * 512, (part + 1) * 512)
                    out = mm_ps[half][:, cols]
                    for k in range(KD):
                        h, l = mix_hi[half][:, k, :], mix_lo[half][:, k, :]
                        nc.tensor.matmul(out, h, wo_hi[:, k, cols], start=(k == 0), stop=False)
                        nc.tensor.matmul(out, h, wo_lo[:, k, cols], start=False, stop=False)
                        ins = nc.tensor.matmul(out, l, wo_hi[:, k, cols], start=False, stop=(k == KD - 1))
                ins.then_inc(mm_done, 1)

            def score(t, half, first=False):
                pe.wait_ge(u2_done, t + 1)
                if not first:
                    pe.wait_ge(u2T_done, t)
                for k in range(KD):
                    ins = nc.tensor.transpose(tr_ps[:, k * P:(k + 1) * P], u2[half][:, k * P:(k + 1) * P], ident[:])
                ins.then_inc(tr_done, 1)
                pe.wait_ge(u2T_done, t + 1)
                if not first:
                    pe.wait_ge(sc_done, t)
                for k in range(KD):
                    ins = nc.tensor.matmul(rt_ps[:, 0:NE], u2T[:, k, :], wr[:, k, :], start=(k == 0), stop=(k == KD - 1))
                ins.then_inc(logit_done, 1)

            def places(pair):
                pe.wait_ge(m_done, pair + 1)
                nc.tensor.matmul(pos_ps[:, 0, :], tri[:], mb[:, 0, :], start=True, stop=True)
                nc.tensor.matmul(pos_ps[:, 1, :], tri[:], mb[:, 1, :], start=True, stop=False)
                nc.tensor.matmul(pos_ps[:, 1, :], ones_b[:], mb[:, 0, :], start=False, stop=True)
                nc.tensor.matmul(pos_ps[:, 2, :], ones_b[:], mb[:, 0, :], start=True, stop=False)
                nc.tensor.matmul(pos_ps[:, 2, :], ones_b[:], mb[:, 1, :], start=False, stop=True).then_inc(pos_done, 1)

            product(0, 0, False)
            product(1, 1, False)
            score(0, 0, first=True)
            product(2, 0, True)
            score(1, 1)
            product(3, 1, True)
            score(2, 0)
            places(0)
            with pe.Fori(2, NT // 2) as q:
                t0 = q * 2
                product(t0, 0, True)
                score(t0 - 1, 1)
                product(t0 + 1, 1, True)
                score(t0, 0)
                places(q - 1)
            score(NT - 1, 1)
            places(NT // 2 - 1)


NB = NBMAX + 1


def expert_phase(nc, persist, w_exp, u2_dram, list_dram, y_dram):
    f32, f32r, i32 = mybir.dt.float32, mybir.dt.float32r, mybir.dt.int32
    ALU, ACT, AX = mybir.AluOpType, mybir.ActivationFunctionType, mybir.AxisListType
    ident, run, row_base, paced = (persist[n] for n in ("ident", "run", "row_base", "paced"))

    ctx = ExitStack()
    with ctx:
        sb = lambda name, shape, dt=f32: ctx.enter_context(nc.sbuf_tensor(name, shape, dt))
        ps = lambda name, shape: ctx.enter_context(nc.psum_tensor(name, shape, f32))
        sem = lambda name: ctx.enter_context(nc.semaphore(name))

        stage = sb("stage", [P, NPIECE, PC])
        w_hi = sb("wx_hi", [P, NPIECE, PC], f32r)
        w_lo = sb("wx_lo", [P, NPIECE, PC], f32r)
        xg = [sb(f"xg{n}", [P, D]) for n in range(2)]
        x_hi = sb("xe_hi", [P, KD, P], f32r)
        x_lo = sb("xe_lo", [P, KD, P], f32r)
        sg = sb("sg", [P, DE])
        h = sb("h", [P, DE])
        h_hi = sb("h_hi", [P, KE, P], f32r)
        h_lo = sb("h_lo", [P, KE, P], f32r)
        yo = [sb(f"yo{n}", [P, D]) for n in range(2)]
        warm = sb("warm", [P, 1])
        ids = [sb(f"ids{n}", [P, 1], i32) for n in range(2)]
        iota_i = sb("iota_i", [P, NB + 1], i32)
        iota_f = sb("iota_f", [P, NB + 1])
        cnt = sb("cnt", [P, NE])
        nb = sb("nb", [P, NE])
        nb_end = [sb(f"nb_end{n}", [P, NE]) for n in range(2)]
        nb_start = sb("nb_start", [P, NE])
        thr = sb("thr", [P, EPG * 2])
        big = x_hi[:].rearrange("p k n -> p (k n)").bitcast(f32)
        cmp = sb("cmp", [P, NB + 1, NE])
        e_of = sb("e_of", [P, NB + 1])
        start_of = sb("start_of", [P, NB])
        flag = sb("flag", [P, NB])
        off = sb("off", [P, NB])
        mode = sb("mode", [P, NB])
        tab_e = sb("tab_e", [P, NB], i32)
        tab_mode = sb("tab_mode", [P, NB], i32)
        tab_off = sb("tab_off", [P, NB], i32)
        tab_go = sb("tab_go", [P, NB], i32)

        gate_ps = ps("gate_ps", [P, DE])
        up_ps = ps("up_ps", [P, DE])
        hT_ps = ps("hT_ps", [P, KE, P])
        xT_ps = ps("xT_ps", [P, D])
        y_ps = ps("y_ps", [P, D])

        s_iota = sem("s_iota")
        s_warm = sem("s_warm")
        tables = sem("tables")
        stage_in = [sem(f"stage_in{n}") for n in range(NPIECE)]
        hi_done = [sem(f"w_hi_{m}") for m in ("gate", "up", "down")]
        lo_done = [sem(f"w_lo_{m}") for m in ("gate", "up", "down")]
        ids_in = sem("ids_in")
        xg_in = [sem(f"xg_in{n}") for n in range(2)]
        xT_done = sem("xT_done")
        x_hi_done = sem("x_hi_done")
        x_lo_done = sem("x_lo_done")
        gate_done = sem("gate_done")
        silu_done = sem("silu_done")
        up_done = sem("up_done")
        h_done = sem("h_done")
        hT_done = sem("hT_done")
        h_hi_done = sem("h_hi_done")
        h_lo_done = sem("h_lo_done")
        y_done = sem("y_done")
        yo_done = sem("yo_done")
        y_out = [sem(f"y_out{n}") for n in range(2)]
        ch = persist["dve_chain"]

        block = ctx.enter_context(nc.Block())
        y_t = y_dram.rearrange("(b p) d -> b p d", p=P)
        GATE, UP, DOWN = range(3)
        NPM = NPIECE // 3

        def choose(eng, condition, then, otherwise=None):
            with eng.If(condition):
                then()
            with eng.Else():
                otherwise() if otherwise else eng.nop()

        def each_step(eng, step, tail, idle=None):
            eng.wait_ge(tables, 1)

            def mode_and_e(b):
                at = (b, 1) if isinstance(b, int) else None
                pick = slice(b, b + 1) if at else bass.ds(b, 1)
                return (eng.value_load(tab_mode[0:1, pick], min_val=0, max_val=2),
                        eng.value_load(tab_e[0:1, pick], min_val=0, max_val=NE))

            mode, e = mode_and_e(0)
            step(0, 0, e, mode > 1, None, None)
            with eng.Fori(0, NB // 2 - 1) as q:
                for half in (1, 0):
                    b = q * 2 + 2 - half
                    mode_before, e_before = mode_and_e(q * 2 + 1 - half)
                    mode, e = mode_and_e(b)
                    with eng.If(mode > 0):
                        step(b, half, e, mode > 1, e_before, mode_before > 1)
                        eng.nop()
                    with eng.Else():
                        choose(eng, mode_before > 0, lambda: tail(b, half, e_before), (lambda: idle(1 - half)) if idle else None)
                        eng.nop()
            mode_before, e_before = mode_and_e(NB - 2)
            choose(eng, mode_before > 0, lambda: tail(NB - 1, 1, e_before), (lambda: idle(0)) if idle else None)

        @block.sync
        def _(sp):
            def load(e, matrix, known=False):
                for i in range(matrix * NPM, (matrix + 1) * NPM):
                    src = w_exp[e, i] if known else w_exp[bass.ds(e, 1), i].rearrange("a p n -> (a p) n")
                    if not (known and e == 0):
                        sp.wait_ge(lo_done[matrix], (e - 1) * NPM + i % NPM + 1)
                    sp.dma_start(stage[:, i, :], src).then_inc(stage_in[i], 16)

            for matrix in (GATE, UP, DOWN):
                load(0, matrix, known=True)
            load(1, GATE, known=True)
            load(1, UP, known=True)
            with sp.Fori(2, NE) as e:
                load(e, GATE)
                load(e, UP)
                load(e - 1, DOWN)
            load(NE - 1, DOWN, known=True)

        @block.gpsimd
        def _(pool):
            nc.gpsimd.iota(iota_i[:], pattern=[[1, NB + 1]], base=0, channel_multiplier=0).then_inc(s_iota, 1)
            pool.wait_ge(tables, 1)

            def fetch(b, q, half, at, first=False):
                src = list_dram[bass.ds(at, P), :]
                if not first:
                    pool.wait_ge(xT_done, b - 1)
                pool.sem_inc(paced, 1)
                pool.dma_start(ids[half][:], src).then_inc(ids_in, 16)
                pool.wait_ge(ids_in, b * 16 + 16)
                pool.sem_inc(paced, 1)
                nc.gpsimd.indirect_dma_start(out=xg[half][:], out_offset=None, in_=u2_dram,
                                             in_offset=bass.IndirectOffsetOnAxis(ap=ids[half][:, 0:1], axis=0)).then_inc(xg_in[half], 16)

            for b in range(2):
                fetch(b, 0, b, pool.value_load(tab_off[0:1, b:b + 1], min_val=0, max_val=NE * SEQ - P), first=True)
            with pool.Fori(1, NB // 2) as q:
                for half in range(2):
                    b = q * 2 + half
                    go = pool.value_load(tab_go[0:1, bass.ds(b, 1)], min_val=0, max_val=1)
                    at = pool.value_load(tab_off[0:1, bass.ds(b, 1)], min_val=0, max_val=NE * SEQ - P)
                    choose(pool, go > 0, lambda: fetch(b, q, half, at))

        @block.scalar
        def _(act):
            def split_hi(e, matrix):
                for i in range(matrix * NPM, (matrix + 1) * NPM):
                    act.wait_ge(stage_in[i], e * 16 + 16)
                    nc.scalar.activation(w_hi[:, i, :], stage[:, i, :], ACT.Copy).then_inc(hi_done[matrix], 1)

            def x_high(b):
                act.wait_ge(xT_done, b + 1)
                nc.scalar.activation(x_hi[:], xT_ps[:].rearrange("p (k n) -> p k n", k=KD), ACT.Copy).then_inc(x_hi_done, 1)

            def h_high(b):
                act.wait_ge(hT_done, b + 1)
                nc.scalar.activation(h_hi[:], hT_ps[:], ACT.Copy).then_inc(h_hi_done, 1)

            def store(b, half):
                dst = y_t[bass.ds(b, 1)].rearrange("a p d -> (a p) d")
                act.wait_ge(y_done, b + 1)
                act.wait_ge(y_out[half], (b - half) * 8 + 16)
                nc.scalar.activation(yo[half][:], y_ps[:], ACT.Copy).then_inc(yo_done, 1)
                act.wait_ge(yo_done, b + 2)
                act.dma_start(dst, yo[half][:]).then_inc(y_out[half], 16)

            def step(b, half, e, last, e_before, last_before):
                act.wait_ge(gate_done, b + 1)
                if last_before is not None:
                    act.wait_ge(h_done, b)
                nc.scalar.activation(sg[:], gate_ps[:], ACT.Silu).then_inc(silu_done, 1)
                if last_before is not None:
                    h_high(b - 1)
                choose(act, last, lambda: split_hi(e + 1, GATE))
                act.wait_ge(up_done, b + 1)
                x_high(b + 1)
                choose(act, last, lambda: split_hi(e + 1, UP))
                if last_before is not None:
                    store(b - 1, 1 - half)
                    choose(act, last_before, lambda: split_hi(e, DOWN))

            def tail(b, half, e_before):
                h_high(b - 1)
                store(b - 1, 1 - half)

            act.wait_ge(s_warm, 1)
            nc.scalar.activation(warm[:], warm[:], ACT.Silu).then_inc(s_warm, 1)
            act.sem_inc(yo_done, 1)
            for half in range(2):
                act.sem_inc(y_out[half], 16)
            for matrix in (GATE, UP, DOWN):
                split_hi(0, matrix)
            x_high(0)
            each_step(act, step, tail, lambda half: act.sem_inc(y_out[half], 16))
            act.wait_ge(y_out[0], 16 * (NB // 2 + 1))
            act.wait_ge(y_out[1], 16 * (NB // 2))

        @block.vector
        def _(dve):
            chained = [0]

            def link(ins):
                ins.then_inc(ch, 1)
                chained[0] += 1
                dve.wait_ge(ch, chained[0])

            def split_lo(e, matrix):
                for i in range(matrix * NPM, (matrix + 1) * NPM):
                    dve.wait_ge(hi_done[matrix], e * NPM + i % NPM + 1)
                    nc.vector.tensor_tensor(out=w_lo[:, i, :], in0=stage[:, i, :], in1=w_hi[:, i, :].bitcast(f32),
                                            op=ALU.subtract).then_inc(lo_done[matrix], 1)

            def x_low(b):
                dve.wait_ge(x_hi_done, b + 1)
                nc.vector.tensor_tensor(out=x_lo[:], in0=xT_ps[:].rearrange("p (k n) -> p k n", k=KD), in1=x_hi[:].bitcast(f32),
                                        op=ALU.subtract).then_inc(x_lo_done, 1)

            def h_low(b):
                dve.wait_ge(h_hi_done, b + 1)
                nc.vector.tensor_tensor(out=h_lo[:], in0=hT_ps[:], in1=h_hi[:].bitcast(f32), op=ALU.subtract).then_inc(h_lo_done, 1)

            def over_e(ap, n):
                return ap.rearrange("p (a b) -> p a b", a=1).broadcast_to([P, n, NE])

            def over_b(ap):
                return ap.rearrange("p (a b) -> p a b", b=1).broadcast_to([P, ap.shape[1], NE])

            nc.vector.memset(warm[:], 0.0).then_inc(s_warm, 1)
            nc.vector.memset(tab_go[:], 1)
            for j in range(16):
                ins = nc.vector.memset(thr[:, j:j + 1], float(P * (j + 1)))
            link(ins)
            dve.wait_ge(s_iota, 1)
            link(nc.vector.tensor_copy(iota_f[:], iota_i[:]))
            link(nc.vector.scalar_tensor_tensor(out=cnt[:], in0=iota_f[:, 0:NE], scalar=-float(SEQ), in1=run[:], op0=ALU.mult, op1=ALU.add))
            passed = cmp[:, 0:16, :].rearrange("p j e -> p (j e)").rearrange("p (e j) -> p e j", e=NE)
            link(nc.vector.tensor_tensor(out=passed, in0=cnt[:].rearrange("p (e a) -> p e a", a=1).broadcast_to([P, NE, 16]),
                                         in1=thr[:].rearrange("p (a j) -> p a j", a=1).broadcast_to([P, NE, 16]), op=ALU.is_gt))
            link(nc.vector.tensor_reduce(out=nb[:], in_=passed, axis=AX.X, op=ALU.add))
            link(nc.vector.tensor_scalar(nb[:], nb[:], 1.0, None, ALU.add))
            src = nb
            for lvl in range(5):
                dst, s = nb_end[lvl % 2], 1 << lvl
                link(nc.vector.tensor_copy(dst[:, 0:s], src[:, 0:s]))
                link(nc.vector.tensor_tensor(out=dst[:, s:], in0=src[:, s:], in1=src[:, 0:NE - s], op=ALU.add))
                src = dst
            end = src
            link(nc.vector.tensor_tensor(out=nb_start[:], in0=end[:], in1=nb[:], op=ALU.subtract))
            link(nc.vector.tensor_tensor(out=cmp[:], in0=over_e(end[:], NB + 1), in1=over_b(iota_f[:]), op=ALU.is_le))
            link(nc.vector.tensor_reduce(out=e_of[:], in_=cmp[:], axis=AX.X, op=ALU.add))
            link(nc.vector.tensor_tensor(out=cmp[:, 0:NB, :], in0=over_e(nb_start[:], NB), in1=over_b(iota_f[:, 0:NB]), op=ALU.is_le))
            link(nc.vector.tensor_tensor(out=cmp[:, 0:NB, :], in0=cmp[:, 0:NB, :], in1=over_e(nb_start[:], NB), op=ALU.mult))
            link(nc.vector.tensor_reduce(out=start_of[:], in_=cmp[:, 0:NB, :], axis=AX.X, op=ALU.max))
            link(nc.vector.tensor_tensor(out=off[:], in0=iota_f[:, 0:NB], in1=start_of[:], op=ALU.subtract))
            link(nc.vector.tensor_scalar(off[:], off[:], float(P), None, ALU.mult))
            link(nc.vector.scalar_tensor_tensor(out=off[:], in0=e_of[:, 0:NB], scalar=float(SEQ), in1=off[:], op0=ALU.mult, op1=ALU.add))
            link(nc.vector.tensor_scalar(flag[:], e_of[:, 0:NB], float(NE - 1), None, ALU.is_le))
            link(nc.vector.tensor_tensor(out=off[:], in0=off[:], in1=flag[:], op=ALU.mult))
            link(nc.vector.tensor_tensor(out=mode[:], in0=e_of[:, 1:], in1=e_of[:, 0:NB], op=ALU.is_gt))
            link(nc.vector.scalar_tensor_tensor(out=mode[:], in0=e_of[:, 0:NB], scalar=float(NE - 2), in1=mode[:], op0=ALU.is_le, op1=ALU.mult))
            link(nc.vector.tensor_tensor(out=mode[:], in0=mode[:], in1=flag[:], op=ALU.add))
            link(nc.vector.tensor_copy(tab_e[:], e_of[:, 0:NB]))
            link(nc.vector.tensor_copy(tab_off[:], off[:]))
            link(nc.vector.tensor_copy(tab_mode[:], mode[:]))
            link(nc.vector.tensor_copy(tab_go[:, 1:], flag[:, 0:NB - 1]))
            link(nc.vector.tensor_scalar(row_base[:], nb_start[:], float(P), None, ALU.mult))
            link(nc.vector.scalar_tensor_tensor(out=row_base[:], in0=iota_f[:, 0:NE], scalar=-float(SEQ), in1=row_base[:],
                                                op0=ALU.mult, op1=ALU.add))
            dve.sem_clear(ch)
            dve.sem_inc(tables, 1)

            def step(b, half, e, last, e_before, last_before):
                if last_before is not None:
                    h_low(b - 1)
                choose(dve, last, lambda: split_lo(e + 1, GATE))
                dve.wait_ge(silu_done, b + 1)
                dve.wait_ge(up_done, b + 1)
                if last_before is not None:
                    dve.wait_ge(hT_done, b)
                nc.vector.tensor_tensor(out=h[:], in0=up_ps[:], in1=sg[:], op=ALU.mult).then_inc(h_done, 1)
                x_low(b + 1)
                choose(dve, last, lambda: split_lo(e + 1, UP))
                if last_before is not None:
                    choose(dve, last_before, lambda: split_lo(e, DOWN))

            for matrix in (GATE, UP, DOWN):
                split_lo(0, matrix)
            x_low(0)
            each_step(dve, step, lambda b, half, e_before: h_low(b - 1))

        @block.tensor
        def _(pe):
            def transpose_x(b, half, q):
                pe.wait_ge(xg_in[half], q * 16 + 16)
                for k in range(KD):
                    ins = nc.tensor.transpose(xT_ps[:, k * P:(k + 1) * P], xg[half][:, k * P:(k + 1) * P], ident[:])
                ins.then_inc(xT_done, 1)

            def transpose_h(b):
                pe.wait_ge(h_done, b + 1)
                for k in range(KE):
                    ins = nc.tensor.transpose(hT_ps[:, k, :], h[:, k * P:(k + 1) * P], ident[:])
                ins.then_inc(hT_done, 1)

            def project(out, matrix, e, done):
                for k in range(KD):
                    if k % 2 == 0:
                        pe.wait_ge(lo_done[matrix], e * NPM + k // 2 + 1)
                    i, at = matrix * NPM + k // 2, slice(k % 2 * DE, (k % 2 + 1) * DE)
                    nc.tensor.matmul(out, x_hi[:, k, :], w_hi[:, i, at], start=(k == 0), stop=False)
                    nc.tensor.matmul(out, x_hi[:, k, :], w_lo[:, i, at], start=False, stop=False)
                    ins = nc.tensor.matmul(out, x_lo[:, k, :], w_hi[:, i, at], start=False, stop=(k == KD - 1))
                ins.then_inc(done, 1)

            def project_down(b, e):
                pe.wait_ge(h_lo_done, b + 1)
                pe.wait_ge(yo_done, b + 1)
                for k in range(KE):
                    pe.wait_ge(lo_done[DOWN], e * NPM + k + 1)
                    for part in range(2):
                        at = slice(part * 512, (part + 1) * 512)
                        nc.tensor.matmul(y_ps[:, at], h_hi[:, k, :], w_hi[:, 2 * NPM + k, at], start=(k == 0), stop=False)
                        nc.tensor.matmul(y_ps[:, at], h_hi[:, k, :], w_lo[:, 2 * NPM + k, at], start=False, stop=False)
                        ins = nc.tensor.matmul(y_ps[:, at], h_lo[:, k, :], w_hi[:, 2 * NPM + k, at], start=False, stop=(k == KE - 1))
                ins.then_inc(y_done, 1)

            def step(b, half, e, last, e_before, last_before):
                pe.wait_ge(x_lo_done, b + 1)
                if e_before is not None:
                    pe.wait_ge(silu_done, b)
                project(gate_ps[:], GATE, e, gate_done)
                if e_before is not None:
                    transpose_h(b - 1)
                transpose_x(b + 1, 1 - half, (b + 1 - (1 - half)) // 2 if isinstance(b, int) else (b + half) // 2)
                project(up_ps[:], UP, e, up_done)
                if e_before is not None:
                    project_down(b - 1, e_before)

            def tail(b, half, e_before):
                transpose_h(b - 1)
                project_down(b - 1, e_before)

            transpose_x(0, 0, 0)
            each_step(pe, step, tail)


def combine_phase(nc, persist, rows, x1_dram, y_dram, out):
    f32, i32 = mybir.dt.float32, mybir.dt.int32
    ALU, ACT, AX = mybir.AluOpType, mybir.ActivationFunctionType, mybir.AxisListType
    ident, mod, paced = persist["ident"], persist["mod"], persist["paced"]
    m_all = (persist["m1_all"], persist["m2_all"])
    w_all, idx_all, row_base = (persist[n] for n in ("w_all", "idx_all", "row_base"))
    NBUF = 4

    ctx = ExitStack()
    with ctx:
        sb = lambda name, shape, dt=f32: ctx.enter_context(nc.sbuf_tensor(name, shape, dt))
        sem = lambda name: ctx.enter_context(nc.semaphore(name))
        bc = sb("bc2", [P, KD, P])
        g2_row = sb("g2_row", [P, D])
        ln_g = sb("ln2g", [P, D])
        ln_b = sb("ln2b", [P, D])
        prod = sb("prod", [P, NT, NE])
        y_idx = sb("y_idx", [P, 2, NT], i32)
        y_row = sb("y_row", [P, 2, NT])
        xa = [sb(f"xa{n}", [P, D]) for n in range(NBUF)]
        ya = [sb(f"ya{n}", [P, D]) for n in range(NBUF)]
        yb = [sb(f"yb{n}", [P, D]) for n in range(NBUF)]
        zo = [sb(f"zo{n}", [P, D]) for n in range(NBUF)]
        stats = sb("stats2", [P, 2, 6])
        mv = [sb(f"mv2{n}", [P, 2]) for n in range(2)]
        root = sb("root2", [P, 1])
        rstd = [sb(f"rstd2{n}", [P, 1]) for n in range(2)]
        eps_col = sb("eps2", [P, 1])
        row_ps = ctx.enter_context(nc.psum_tensor("row_ps", [P, D], f32))

        s_rows = sem("s_rows2")
        s_bc = sem("s_bc2")
        s_row = sem("s_row2")
        s_idx = sem("s_idx2")
        xa_in = [sem(f"xa_in{n}") for n in range(NBUF)]
        ya_in = [sem(f"ya_in{n}") for n in range(NBUF)]
        yb_in = [sem(f"yb_in{n}") for n in range(NBUF)]
        wa_done = sem("wa_done")
        f_done = sem("f_done")
        fg_done = sem("fg_done")
        z_done = sem("z_done2")
        stat_done = sem("stat_done2")
        root_done = sem("root_done2")
        rstd_done = sem("rstd_done2")
        n_norm = sem("n_norm")
        n_half = sem("n_half")
        n_done = sem("n_done")
        stored = [sem(f"stored{n}") for n in range(NBUF)]
        ch = persist["dve_chain"]
        block = ctx.enter_context(nc.Block())
        x1_t = x1_dram.rearrange("(t p) d -> t p d", p=P)
        out_t = out.rearrange("(t p) d -> t p d", p=P)

        @block.sync
        def _(sp):
            sp.dma_start(ln_g[:], rows[ROW_G2:ROW_G2 + 1, :].broadcast_to([P, D])).then_inc(s_rows, 16)
            sp.dma_start(ln_b[:], rows[ROW_B2:ROW_B2 + 1, :].broadcast_to([P, D])).then_inc(s_rows, 16)
            with sp.Fori(0, NT // NBUF) as r:
                for n in range(NBUF):
                    src = x1_t[bass.ds(r * NBUF + n, 1)].rearrange("a p d -> (a p) d")
                    sp.wait_ge(z_done, r * NBUF)
                    sp.dma_start(xa[n][:], src).then_inc(xa_in[n], 16)
            sp.wait_ge(s_rows, 32)

        def norm(pool, t):
            n = t % NBUF
            pool.wait_ge(rstd_done, t + 1)
            pool.sem_inc(paced, 1)
            nc.gpsimd.tensor_scalar(zo[n][:], zo[n][:], mv[t % 2][:, 0:1], rstd[t % 2][:, 0:1], ALU.subtract, ALU.mult).then_inc(n_norm, 1)
            pool.wait_ge(n_norm, t + 1)
            nc.gpsimd.tensor_tensor(out=zo[n][:], in0=zo[n][:], in1=ln_g[:], op=ALU.mult).then_inc(n_half, 1)
            pool.wait_ge(n_half, t + 1)
            nc.gpsimd.tensor_tensor(out=zo[n][:], in0=zo[n][:], in1=ln_b[:], op=ALU.add).then_inc(n_done, 1)

        @block.gpsimd
        def _(pool):
            pool.wait_ge(s_idx, 1)
            for t in range(NT):
                n = t % NBUF
                if t >= NBUF:
                    pool.wait_ge(f_done, t - NBUF + 1)
                for j, dst, s in ((0, ya[n], ya_in[n]), (1, yb[n], yb_in[n])):
                    nc.gpsimd.indirect_dma_start(out=dst[:], out_offset=None, in_=y_dram,
                                                 in_offset=bass.IndirectOffsetOnAxis(ap=y_idx[:, j, t:t + 1], axis=0)).then_inc(s, 16)
                if t >= 1:
                    norm(pool, t - 1)
            norm(pool, NT - 1)

        @block.scalar
        def _(act):
            act.wait_ge(s_idx, 1)
            for t in range(NT):
                n = t % NBUF
                act.wait_ge(ya_in[n], 16 * (t // NBUF + 1))
                nc.scalar.activation(ya[n][:], ya[n][:], ACT.Copy, scale=w_all[:, 0, t:t + 1]).then_inc(wa_done, 1)
                act.wait_ge(stat_done, t + 1)
                if t:
                    act.wait_ge(rstd_done, t)
                nc.scalar.activation(root[:], mv[t % 2][:, 1:2], ACT.Sqrt, bias=eps_col[:, 0:1]).then_inc(root_done, 1)
                if t:
                    act.wait_ge(n_done, t)
                    act.dma_start(out_t[t - 1], zo[(t - 1) % NBUF][:]).then_inc(stored[(t - 1) % NBUF], 16)
            act.wait_ge(n_done, NT)
            act.dma_start(out_t[NT - 1], zo[(NT - 1) % NBUF][:]).then_inc(stored[(NT - 1) % NBUF], 16)
            for n in range(NBUF):
                act.wait_ge(stored[n], 16 * NT // NBUF)

        @block.vector
        def _(dve):
            chained = [0]

            def link(ins):
                ins.then_inc(ch, 1)
                chained[0] += 1
                dve.wait_ge(ch, chained[0])

            link(nc.vector.memset(eps_col[:], EPS))
            for j in range(2):
                link(nc.vector.tensor_tensor(out=prod[:], in0=m_all[j][:], in1=row_base[:].rearrange("p (a e) -> p a e", a=1)
                                             .broadcast_to([P, NT, NE]), op=ALU.mult))
                link(nc.vector.tensor_reduce(out=y_row[:, j, :], in_=prod[:], axis=AX.X, op=ALU.add))
            link(nc.vector.tensor_tensor(out=y_row[:], in0=y_row[:], in1=idx_all[:], op=ALU.add))
            link(nc.vector.tensor_copy(y_idx[:], y_row[:]))
            dve.sem_inc(s_idx, 1)
            nc.vector.tensor_copy(bc[:], mod[:, GT2 * KD:(GT2 + 1) * KD].rearrange("p (k a) -> p k a", a=1)
                                  .broadcast_to([P, KD, P])).then_inc(s_bc, 1)
            dve.wait_ge(s_row, 1)
            link(nc.vector.tensor_copy(g2_row[:], row_ps[:]))
            dve.wait_ge(s_rows, 32)
            for t in range(NT):
                n = t % NBUF
                dve.wait_ge(wa_done, t + 1)
                dve.wait_ge(yb_in[n], 16 * (t // NBUF + 1))
                nc.vector.scalar_tensor_tensor(out=yb[n][:], in0=yb[n][:], scalar=w_all[:, 1, t:t + 1], in1=ya[n][:],
                                               op0=ALU.mult, op1=ALU.add).then_inc(fg_done, 1)
                dve.wait_ge(fg_done, 2 * t + 1)
                if t >= NBUF:
                    dve.wait_ge(stored[n], 16 * (t // NBUF))
                nc.vector.tensor_tensor(out=zo[n][:], in0=yb[n][:], in1=g2_row[:], op=ALU.mult).then_inc(fg_done, 1)
                dve.wait_ge(fg_done, 2 * t + 2)
                dve.sem_inc(f_done, 1)
                dve.wait_ge(xa_in[n], 16 * (t // NBUF + 1))
                nc.vector.tensor_tensor(out=zo[n][:], in0=zo[n][:], in1=xa[n][:], op=ALU.add).then_inc(z_done, 1)
                dve.wait_ge(z_done, t + 1)
                for part in range(2):
                    nc.vector.bn_stats(stats[:, part, :], zo[n][:, part * 512:(part + 1) * 512]).then_inc(ch, 1)
                chained[0] += 2
                dve.wait_ge(ch, chained[0])
                if t >= 2:
                    dve.wait_ge(n_done, t - 1)
                nc.vector.bn_aggr(mv[t % 2][:], stats[:]).then_inc(stat_done, 1)
                dve.wait_ge(root_done, t + 1)
                nc.vector.reciprocal(rstd[t % 2][:], root[:]).then_inc(rstd_done, 1)

        @block.tensor
        def _(pe):
            pe.wait_ge(s_bc, 1)
            for k in range(KD):
                ins = nc.tensor.matmul(row_ps[:, k * P:(k + 1) * P], bc[:, k, :], ident[:], start=True, stop=True)
            ins.then_inc(s_row, 1)


def hybrid_block(nc, x, xT, w_ada, cols, w_in, pool_w, w_out, rows, w_router, router_bias, w_exp, out):
    f32 = mybir.dt.float32
    scratch = lambda name, shape, dt=f32: nc.dram_tensor(name, shape, dt).ap()
    mix_spill = scratch("mix_spill", (NCH, P, KD * CH))
    x1_dram = scratch("x1_dram", (SEQ, D))
    u2_dram = scratch("u2_dram", (SEQ, D))
    y_dram = scratch("y_dram", (NB * P, D))
    list_dram = scratch("list_dram", (NE * SEQ, 1), mybir.dt.int32)
    ctx = ExitStack()
    with ctx:
        persist = {name: ctx.enter_context(nc.sbuf_tensor(name, shape, f32)) for name, shape in (
            ("ident", [P, P]), ("mod", [P, 6 * KD]))}
        persist["dve_chain"] = ctx.enter_context(nc.semaphore("dve_chain"))
        persist["paced"] = ctx.enter_context(nc.semaphore("paced"))
        with ExitStack() as front:
            col = front.enter_context(nc.sbuf_tensor("col", [P, NCOL], f32))
            w_hi, w_lo = (front.enter_context(nc.sbuf_tensor(name, [P, KD, NIN], mybir.dt.float32r)) for name in ("w_in_hi", "w_in_lo"))
            modulation_phase(nc, {**persist, "col": col}, w_hi, w_lo, w_ada, cols, w_in)
            conv_pool_phase(nc, {**persist, "col": col}, w_hi, w_lo, xT, pool_w, mix_spill)
        persist |= {name: ctx.enter_context(nc.sbuf_tensor(name, shape, f32)) for name, shape in (
            ("m1_all", [P, NT, NE]), ("m2_all", [P, NT, NE]), ("w_all", [P, 2, NT]), ("idx_all", [P, 2, NT]),
            ("run", [P, NE]), ("row_base", [P, NE]))}
        mix_router_phase(nc, persist, x, w_out, rows, w_router, router_bias, mix_spill, x1_dram, u2_dram, list_dram, y_dram)
        expert_phase(nc, persist, w_exp, u2_dram, list_dram, y_dram)
        combine_phase(nc, persist, rows, x1_dram, y_dram, out)


def lay_out(a):
    import numpy as np
    x = np.asarray(a["x"])[0]
    col = np.zeros((P, NCOL), np.float32)
    col[:, COL_BADA:COL_BIN] = np.asarray(a["b_ada"])[0].reshape(6 * KD, P).T
    order = [b for j in range(CG) for b in (CG + j, j)] + list(range(2 * CG, NM))
    col[:, COL_BIN:COL_CONVW] = np.asarray(a["b_in"])[0].reshape(NM, P)[order].T
    col[:, COL_CONVW:COL_CONVB] = np.asarray(a["conv_w"])[0].reshape(TAPS, CG, P).transpose(2, 1, 0).reshape(P, CG * TAPS)
    for at, name in ((COL_CONVB, "conv_b"), (COL_LNG, "conv_ln_g"), (COL_LNB, "conv_ln_b"), (COL_PSC, "pool_scale")):
        col[:, at:at + CG] = np.asarray(a[name])[0].reshape(CG, P).T
    col[:, COL_C:COL_FIX] = np.asarray(a["c"])[0].reshape(KD, P).T
    col[:, COL_FIX:] = np.concatenate([[w / min(t + 1, w) for t in range(PHALO)] for w in WINDOWS]).astype(np.float32)
    w_in = np.asarray(a["w_in"])[0].reshape(KD, P, NM, P)[:, :, order].transpose(1, 0, 2, 3)
    w_in = w_in.reshape(P, KD * NIN // PC, PC).transpose(1, 0, 2)
    gate, up = (np.asarray(a[n])[0].reshape(NE, KD, P, DE).transpose(0, 2, 1, 3).reshape(NE, P, 4, PC) for n in ("w_gate", "w_up"))
    down = np.asarray(a["w_down"])[0].reshape(NE, KE, P, D).transpose(0, 2, 1, 3)
    w_exp = np.empty((NE, NPIECE, P, PC), np.float32)
    for at, part in ((0, gate), (4, up), (8, down)):
        w_exp[:, at:at + 4] = part.transpose(0, 2, 1, 3)
    return {
        "x": x,
        "xT": x.reshape(NCH, CH, KD, P).transpose(0, 3, 2, 1).reshape(NCH, P, KD * CH),
        "w_ada": np.asarray(a["w_ada"])[0].reshape(KD, P, 6, PC).transpose(2, 0, 1, 3).reshape(6 * KD, P, PC),
        "cols": col,
        "w_in": w_in,
        "pool_w": np.asarray(a["pool_w"])[0].transpose(1, 0, 2).reshape(P, CG * P),
        "w_out": np.asarray(a["w_out"])[0].reshape(KD, P, D),
        "rows": np.stack([np.asarray(a[n])[0] for n in ("b_out", "ln1_g", "ln1_b", "ln2_g", "ln2_b")]),
        "w_router": np.asarray(a["w_router"]).reshape(KD, P, NE).transpose(1, 0, 2).reshape(P, KD * NE),
        "router_bias": np.asarray(a["router_bias"]).reshape(1, NE),
        "w_exp": w_exp,
    }


_INS = ("x", "xT", "w_ada", "cols", "w_in", "pool_w", "w_out", "rows", "w_router", "router_bias", "w_exp")


def kernel(**inputs):
    import numpy as np
    import concourse.bacc as bacc
    from concourse.bass_utils import run_bass_kernel_spmd
    laid = lay_out(inputs)
    nc = bacc.Bacc("TRN2", target_bir_lowering=False, num_devices=1)
    arrays, args = {}, []
    for name in _INS:
        a = np.ascontiguousarray(laid[name])
        arrays[f"in_{name}"] = a
        args.append(nc.dram_tensor(f"in_{name}", a.shape, mybir.dt.from_np(a.dtype), kind="ExternalInput").ap())
    out = nc.dram_tensor("out", (SEQ, D), mybir.dt.float32, kind="ExternalOutput").ap()
    hybrid_block(nc, *args, out)
    got = run_bass_kernel_spmd(nc, [arrays], core_ids=[0]).results[0]["out"]
    return got.reshape(1, SEQ, D)
```

```python
import concourse.bass as bass
from concourse import mybir
from contextlib import ExitStack

P = 128
D = 1024
SEQ = 2048
KD = D // P
CW = 512
CG = CW // P
NIN = 2 * CW + (D - CW)
NM = NIN // P
TAPS = 31
HALO = TAPS - 1
WINDOWS = (2, 4, 8, 16)
PHALO = 16
CH = 256
NCH = SEQ // CH
TPC = CH // P
NT = SEQ // P
NE = 32
NG = 4
EPG = NE // NG
DE = 512
KE = DE // P
EPS = 1e-5
ALPHA = 2.0 ** 0.25
NPIECE = 12
PC = 1024
NBMAX = SEQ * 2 // P + NE - 1
BIG = 1e30

COL_BADA = 0
COL_BIN = COL_BADA + 6 * KD
COL_CONVW = COL_BIN + NM
COL_CONVB = COL_CONVW + CG * TAPS
COL_LNG = COL_CONVB + CG
COL_LNB = COL_LNG + CG
COL_PSC = COL_LNB + CG
COL_C = COL_PSC + CG
COL_FIX = COL_C + KD
NCOL = COL_FIX + CG * PHALO
ROW_BOUT, ROW_G1, ROW_B1, ROW_G2, ROW_B2, NROW = 0, 1, 2, 3, 4, 5
SH1, SC1, GT1, SH2, SC2, GT2 = range(6)


def modulation_phase(nc, persist, w_hi, w_lo, w_ada, cols, w_in):
    f32 = mybir.dt.float32
    ALU, ACT = mybir.AluOpType, mybir.ActivationFunctionType
    ident, mod, col = persist["ident"], persist["mod"], persist["col"]
    NRING = 5
    N_WIN = KD * NIN // PC
    N_ADA = 2 * KD

    ctx = ExitStack()
    with ctx:
        sb = lambda name, shape, dt=f32: ctx.enter_context(nc.sbuf_tensor(name, shape, dt))
        sem = lambda name: ctx.enter_context(nc.semaphore(name))
        retire = lambda s: persist["retired"][0].append(s) or s
        ring = sb("ring", [P, NRING, PC])
        acc = sb("ada_acc", [P, 2, PC])
        cact, ones = persist["cact"], persist["ones"]
        mod_ps = ctx.enter_context(nc.psum_tensor("mod_ps", [P, 512], f32))
        s_col = retire(sem("s_col"))
        s_const = retire(sem("s_const"))
        s_cact = retire(sem("s_cact"))
        ring_in = [retire(sem(f"ring_in{n}")) for n in range(NRING)]
        ring_free = retire(sem("ring_free"))
        w_hi_ready = retire(sem("w_hi_ready"))
        mod_ps_ready = retire(sem("mod_ps_ready"))
        ident_ready = retire(sem("ident_ready"))
        chain = persist["dve_chain"]
        block = ctx.enter_context(nc.Block())
        hi_of = lambda q: w_hi[:].rearrange("p k n -> p (k n)")[:, q * PC:(q + 1) * PC]
        lo_of = lambda q: w_lo[:].rearrange("p k n -> p (k n)")[:, q * PC:(q + 1) * PC]

        @block.sync
        def _(sp):
            sp.dma_start(col[:], cols).then_inc(s_col, 16)
            for n in range(N_ADA + N_WIN):
                src = w_ada[n] if n < N_ADA else w_in[n - N_ADA]
                if n >= NRING:
                    sp.wait_ge(ring_free, n - NRING + 1)
                sp.dma_start(ring[:, n % NRING, :], src).then_inc(ring_in[n % NRING], 16)

        @block.scalar
        def _(act):
            act.wait_ge(s_col, 16)
            nc.scalar.activation(cact[:], col[:, COL_C:COL_C + KD], ACT.Silu).then_inc(s_cact, 1)
            for n in range(N_ADA, N_ADA + N_WIN):
                act.wait_ge(ring_in[n % NRING], 16 * (n // NRING + 1))
                nc.scalar.activation(hi_of(n - N_ADA), ring[:, n % NRING, :], ACT.Copy).then_inc(w_hi_ready, 1)

        @block.vector
        def _(dve):
            nc.vector.memset(ident[:], 1.0)
            nc.vector.memset(ones[:], 1.0).then_inc(s_const, 1)
            dve.wait_ge(s_cact, 1)
            for n in range(N_ADA + N_WIN):
                dve.wait_ge(ring_in[n % NRING], 16 * (n // NRING + 1))
                if n >= N_ADA:
                    dve.wait_ge(w_hi_ready, n - N_ADA + 1)
                    nc.vector.tensor_tensor(out=lo_of(n - N_ADA), in0=ring[:, n % NRING, :], in1=hi_of(n - N_ADA).bitcast(f32),
                                            op=ALU.subtract).then_inc(ring_free, 1)
                    continue
                which, k = divmod(n, KD)
                if k:
                    dve.wait_ge(ring_free, n)
                    nc.vector.scalar_tensor_tensor(out=acc[:, which, :], in0=ring[:, n % NRING, :], scalar=cact[:, k:k + 1],
                                                   in1=acc[:, which, :], op0=ALU.mult, op1=ALU.add).then_inc(ring_free, 1)
                else:
                    nc.vector.tensor_scalar(acc[:, which, :], ring[:, n % NRING, :], cact[:, 0:1], None, ALU.mult).then_inc(ring_free, 1)
            dve.wait_ge(mod_ps_ready, 2)
            nc.vector.tensor_tensor(out=mod[:, 0:2 * KD], in0=mod_ps[:, 0:2 * KD], in1=col[:, COL_BADA:COL_BADA + 2 * KD],
                                    op=ALU.add).then_inc(chain, 1)
            dve.wait_ge(chain, 1)
            part = mod[:, SC1 * KD:(SC1 + 1) * KD]
            nc.vector.tensor_scalar(part, part, 1.0, None, ALU.add).then_inc(chain, 1)
            dve.wait_ge(chain, 2)
            dve.sem_clear(chain)

        @block.gpsimd
        def _(pool):
            pool.wait_ge(s_const, 1)
            nc.gpsimd.affine_select(out=ident[:], in_=ident[:], compare_op=ALU.is_equal, fill=0.0, base=0,
                                    pattern=[[-1, P]], channel_multiplier=1).then_inc(ident_ready, 1)
            pool.wait_ge(ident_ready, 1)

        @block.tensor
        def _(pe):
            pe.wait_ge(s_const, 1)
            for which in (SH1, SC1):
                pe.wait_ge(ring_free, (which + 1) * KD)
                for j in range(KD):
                    ins = nc.tensor.matmul(mod_ps[:, which * KD + j:which * KD + j + 1], acc[:, which, j * P:(j + 1) * P],
                                           ones[:, 0:1], start=True, stop=True)
                ins.then_inc(mod_ps_ready, 1)


def conv_pool_phase(nc, persist, w_hi, w_lo, w_ada, xT, pool_w, mix_spill):
    f32, f32r = mybir.dt.float32, mybir.dt.float32r
    ALU, ACT = mybir.AluOpType, mybir.ActivationFunctionType
    mod, col, paced = persist["mod"], persist["col"], persist["paced"]
    SHARED = slice(CG // 2, CG)
    T_DVE = 7
    N_PROD = TAPS - T_DVE
    N_SUM = N_PROD - 1
    NPB = 6
    ctx = ExitStack()
    with ctx:
        sb = lambda name, shape, dt=f32: ctx.enter_context(nc.sbuf_tensor(name, shape, dt))
        ps = lambda name, shape: ctx.enter_context(nc.psum_tensor(name, shape, f32))
        retire = lambda s: persist["retired"][1].append(s) or s
        sem = lambda name: retire(ctx.enter_context(nc.semaphore(name)))

        mean_w = sb("mean_w", [P, P])
        poolw_sb = sb("poolw_sb", [P, CG, P])
        x_raw = sb("x_raw", [P, KD, CH])
        u_hi = [sb(f"u_hi{n}", [P, KD, CH], f32r) for n in range(2)]
        u_lo = [sb(f"u_lo{n}", [P, KD, CH], f32r) for n in range(2)]
        sig = sb("sig", [P, 2, CH])
        v = [sb(f"v{n}", [P, CG, HALO + CH]) for n in range(2)]
        pp = [sb(f"p{n}", [P, CG, PHALO + CH]) for n in range(2)]
        y = [sb(f"y{n}", [P, CG, CH]) for n in range(2)]
        rstd = sb("rstd", [P, CH])
        prod = sb("prod_c", [P, NPB, CG // 2, CH])
        yp = [sb(f"yp{n}", [P, CG // 2, CH]) for n in range(2)]
        eps_col = sb("eps_col", [P, 1])
        s_a = sb("s_a", [P, CG, PHALO + CH])
        s_b = sb("s_b", [P, CG, PHALO + CH])
        mixo = sb("mixo", [P, 2 * CG, CH])
        ysq = mixo[:, 0:CG, :]

        h_ps = [ps(f"h_ps{n}", [P, 512]) for n in range(4)]
        stat_ps = ps("stat_ps", [P, 2, CH])
        mod_ps = ps("mod_ps2", [P, 4 * KD])
        yb_ps = [ps(f"yb_ps{n}", [P, 512]) for n in range(2)]

        flat = lambda ap: ap.rearrange("p a n -> p (a n)")
        ring = [flat(mixo[:, 0:4, :]), flat(mixo[:, 4:8, :]), flat(y[1][:]), flat(prod[:, 0:2].rearrange("p a b n -> p (a b) n")),
                flat(prod[:, 2:4].rearrange("p a b n -> p (a b) n"))]
        acc = [flat(y[0][:]), flat(prod[:, 4:6].rearrange("p a b n -> p (a b) n"))]
        NRING = len(ring)
        cact, ones = persist["cact"], persist["ones"]
        pool_sum_w = sb("pool_sum_w", [P, CG, P])
        pool_p_w = sb("pool_p_w", [P, CG, P])

        s_poolw = sem("s_poolw")
        ring_in = [sem(f"ring2_in{n}") for n in range(NRING)]
        ring_free = sem("ring2_free")
        mod_ps_ready = sem("mod_ps2_ready")
        poolw_ready = sem("poolw_ready")
        s_const = sem("s_const2")
        x_in = sem("x_in")
        u_ready = sem("u_ready")
        hi_ready = sem("hi_ready")
        u_split = sem("u_split")
        h_ready = sem("h_ready")
        evac_act = sem("evac_act")
        evac_dve = sem("evac_dve")
        mean_ready = sem("mean_ready")
        centered = sem("centered")
        squared = sem("squared")
        var_ready = sem("var_ready")
        root_ready = sem("root_ready")
        normed = sem("normed")
        yb_ready = sem("yb_ready")
        mix_ready = sem("mix_ready")
        yb_taken = sem("yb_taken")
        mix_out = sem("mix_out")
        rstd_ready = sem("rstd_ready")
        p_halo = sem("p_halo")
        p_used = sem("p_used")
        prod_ready = sem("prod_ready")
        sums = sem("sums")
        yp_used = sem("yp_used")
        chain_p = sem("chain_p")
        chain_v = persist["dve_chain"]
        halo_done = sem("halo_done")

        block = ctx.enter_context(nc.Block())

        @block.sync
        def _(sp):
            def load_x(c):
                if c:
                    sp.wait_ge(u_split, c)
                sp.dma_start(x_raw[:], xT[c].rearrange("p (k n) -> p k n", k=KD)).then_inc(x_in, 16)

            load_x(0)
            sp.dma_start(poolw_sb[:], pool_w.rearrange("p (g n) -> p g n", g=CG)).then_inc(s_poolw, 16)
            for n in range(4 * KD):
                if n >= NRING:
                    sp.wait_ge(ring_free, n - NRING + 1)
                sp.dma_start(ring[n % NRING], w_ada[2 * KD + n]).then_inc(ring_in[n % NRING], 16)
                if n == NRING - 1:
                    load_x(1)
                if n == 2 * NRING:
                    load_x(2)
            with sp.Fori(3, NCH) as c:
                src = xT[bass.ds(c, 1)].rearrange("a p (k n) -> (a p) k n", k=KD)
                sp.wait_ge(u_split, c)
                sp.dma_start(x_raw[:], src).then_inc(x_in, 16)
            sp.wait_ge(x_in, 16 * NCH)

        @block.scalar
        def _(act):
            def modulate(c):
                act.wait_ge(x_in, c * 16 + 16)
                for k in range(KD):
                    ins = nc.scalar.activation(x_raw[:, k, :], x_raw[:, k, :], ACT.Identity,
                                               bias=mod[:, SH1 * KD + k:SH1 * KD + k + 1],
                                               scale=mod[:, SC1 * KD + k:SC1 * KD + k + 1])
                ins.then_inc(u_ready, 1)

            def gate(c, j, first):
                act.wait_ge(h_ready, c * NM + 2 * j + 1)
                if j >= 2:
                    act.wait_ge(evac_dve, c * CG + j - 1)
                elif not first:
                    act.wait_ge(evac_dve, c * CG + j - 1)
                nc.scalar.activation(sig[:, j % 2, :], h_ps[2 * j % 4][:, 0:CH], ACT.Sigmoid,
                                     bias=col[:, COL_BIN + 2 * j:COL_BIN + 2 * j + 1]).then_inc(evac_act, 1)

            def products(c, b, quarter, first):
                for i in range(N_PROD * quarter // 4, N_PROD * (quarter + 1) // 4):
                    if not (first and i < NPB):
                        act.wait_ge(sums, (c - 1) * N_SUM + (max(i - NPB, 1) if i >= NPB else i - NPB + 1))
                    for g in range(CG // 2, CG):
                        t = T_DVE + i
                        w = col[:, COL_CONVW + g * TAPS + t:COL_CONVW + g * TAPS + t + 1]
                        ins = nc.scalar.activation(prod[:, i % NPB, g - CG // 2, :], v[b][:, g, t:t + CH], ACT.Copy, scale=w)
                    ins.then_inc(prod_ready, 1)

            def step(c, half, project=True, conv=True, finish=True, more=True, first=False, store_before=True):
                first_prod = isinstance(c, int) and c == 1
                if project:
                    gate(c, 0, first)
                if conv:
                    act.wait_ge(evac_dve, c * CG)
                    if first_prod:
                        act.wait_ge(mod_ps_ready, 4)
                    products(c, 1 - half, 0, first_prod)
                if project:
                    gate(c, 1, first)
                if conv:
                    products(c, 1 - half, 1, first_prod)
                if finish:
                    act.wait_ge(centered, c - 1)
                    if store_before:
                        act.wait_ge(mix_out, (c - 2) * 16)
                    nc.scalar.activation(ysq, y[half][:], ACT.Square).then_inc(squared, 1)
                if finish:
                    for g in range(CG):
                        act.wait_ge(yb_ready, (c - 2) * CG + g + 1)
                        nc.scalar.activation(mixo[:, CG + g, :], yb_ps[g % 2][:, g // 2 * CH:(g // 2 + 1) * CH], ACT.Copy,
                                             scale=col[:, COL_PSC + g:COL_PSC + g + 1]).then_inc(yb_taken, 1)
                if project:
                    gate(c, 2, first)
                if conv:
                    products(c, 1 - half, 2, first_prod)
                if project:
                    gate(c, 3, first)
                if finish:
                    act.wait_ge(var_ready, c - 1)
                    nc.scalar.activation(rstd[:], stat_ps[:, 1, :], ACT.Sqrt, bias=eps_col[:, 0:1]).then_inc(root_ready, 1)
                if more:
                    modulate(c + 2)
                if conv:
                    products(c, 1 - half, 3, first_prod)
                if project:
                    if not first:
                        act.wait_ge(p_used, c - 1)
                        act.wait_ge(p_halo, c)
                    for j in range(CG):
                        m = 2 * CG + j
                        act.wait_ge(h_ready, c * NM + m + 1)
                        nc.scalar.activation(pp[half][:, j, PHALO:], h_ps[m % 4][:, 0:CH], ACT.Identity,
                                             bias=col[:, COL_BIN + m:COL_BIN + m + 1]).then_inc(evac_act, 1)
                if finish:
                    act.wait_ge(normed, c - 1)
                    for g in range(CG):
                        nc.scalar.activation(mixo[:, g, :], y[half][:, g, :], ACT.Silu,
                                             bias=col[:, COL_LNB + g:COL_LNB + g + 1],
                                             scale=col[:, COL_LNG + g:COL_LNG + g + 1]).then_inc(mix_ready, 1)
                    dst = mix_spill[bass.ds(c - 2, 1)].rearrange("a p (k n) -> (a p) k n", k=2 * CG)
                    act.wait_ge(mix_ready, (c - 1) * CG)
                    act.wait_ge(yb_taken, (c - 1) * CG)
                    act.dma_start(dst, mixo[:]).then_inc(mix_out, 16)

            act.wait_ge(s_const, 1)
            modulate(0)
            modulate(1)
            step(0, 0, conv=False, finish=False, first=True)
            step(1, 1, finish=False)
            step(2, 0, store_before=False)
            step(3, 1)
            with act.Fori(4, NCH - 2, 2) as c0:
                step(c0, 0)
                step(c0 + 1, 1)
            step(NCH - 2, 0, more=False)
            step(NCH - 1, 1, more=False)
            step(NCH, 0, project=False, more=False)
            step(NCH + 1, 1, project=False, conv=False, more=False)
            act.wait_ge(mix_out, 16 * NCH)

        @block.vector
        def _(dve):
            nc.vector.memset(mean_w[:], 1.0 / CW)
            nc.vector.memset(eps_col[:], EPS)
            for b in range(2):
                nc.vector.memset(v[b][:], 0.0)
                nc.vector.memset(pp[b][:], 0.0)
            nc.vector.memset(s_a[:], 0.0)
            nc.vector.memset(s_b[:], 0.0).then_inc(s_const, 1)

            def split(c, half):
                dve.wait_ge(u_ready, c + 1)
                nc.vector.tensor_copy(u_hi[half][:], x_raw[:]).then_inc(hi_ready, 1)
                dve.wait_ge(hi_ready, c + 1)
                nc.vector.tensor_tensor(out=u_lo[half][:], in0=x_raw[:], in1=u_hi[half][:].bitcast(f32),
                                        op=ALU.subtract).then_inc(u_split, 1)

            def evac(c, half, j):
                m = 2 * j + 1
                dve.wait_ge(h_ready, c * NM + m + 1)
                dve.wait_ge(evac_act, c * 2 * CG + j + 1)
                nc.vector.scalar_tensor_tensor(out=v[half][:, j, HALO:], in0=h_ps[m % 4][:, 0:CH],
                                               scalar=col[:, COL_BIN + m:COL_BIN + m + 1], in1=sig[:, j % 2, :],
                                               op0=ALU.add, op1=ALU.mult).then_inc(evac_dve, 1)

            order = [(t, g) for t in range(TAPS) for g in range(CG) if g < CG // 2 or t < T_DVE]

            def taps(b, quarter):
                for i in range(len(order) * quarter // 4, len(order) * (quarter + 1) // 4):
                    t, g = order[i]
                    w = col[:, COL_CONVW + g * TAPS + t:COL_CONVW + g * TAPS + t + 1]
                    if t == 0:
                        ins = nc.vector.tensor_scalar(y[b][:, g, :], v[b][:, g, 0:CH], w,
                                                      col[:, COL_CONVB + g:COL_CONVB + g + 1], ALU.mult, ALU.add)
                    else:
                        dve.wait_ge(chain_v, order.index((t - 1, g)) + 1)
                        ins = nc.vector.scalar_tensor_tensor(out=y[b][:, g, :], in0=v[b][:, g, t:t + CH], scalar=w,
                                                             in1=y[b][:, g, :], op0=ALU.mult, op1=ALU.add)
                    ins.then_inc(chain_v, 1)

            def ada(which):
                a = acc[which % 2]
                for k in range(KD):
                    n = which * KD + k
                    dve.wait_ge(ring_in[n % NRING], 16 * (n // NRING + 1))
                    if k:
                        dve.wait_ge(ring_free, n)
                        nc.vector.scalar_tensor_tensor(out=a, in0=ring[n % NRING], scalar=cact[:, k:k + 1], in1=a,
                                                       op0=ALU.mult, op1=ALU.add).then_inc(ring_free, 1)
                    else:
                        if which >= 2:
                            dve.wait_ge(mod_ps_ready, which - 1)
                        nc.vector.tensor_scalar(a, ring[n % NRING], cact[:, 0:1], None, ALU.mult).then_inc(ring_free, 1)

            def step(c, half, project=True, conv=True, finish=True, more=True, first=False, y_reused=True):
                if first:
                    ada(0)
                if more:
                    if not first:
                        dve.wait_ge(h_ready, c * NM)
                    split(c + 1, 1 - half)
                if finish:
                    dve.wait_ge(sums, (c - 1) * N_SUM)
                    nc.vector.tensor_tensor(out=y[half][:, SHARED, :], in0=y[half][:, SHARED, :], in1=yp[half][:],
                                            op=ALU.add).then_inc(yp_used, 1)
                if conv:
                    dve.wait_ge(evac_dve, c * CG)
                    if y_reused:
                        dve.wait_ge(mix_ready, (c - 2) * CG)
                for j in range(CG):
                    if project:
                        evac(c, half, j)
                    if first and j < CG - 1:
                        ada(j + 1)
                    if conv:
                        taps(1 - half, j)
                    if finish and j == 0:
                        dve.wait_ge(mean_ready, c - 1)
                        nc.vector.tensor_tensor(out=y[half][:], in0=y[half][:],
                                                in1=stat_ps[:, 0:1, :].broadcast_to([P, CG, CH]),
                                                op=ALU.subtract).then_inc(centered, 1)
                    if finish and j == 2:
                        dve.wait_ge(root_ready, c - 1)
                        nc.vector.reciprocal(rstd[:], rstd[:]).then_inc(rstd_ready, 1)
                    if finish and j == 3:
                        dve.wait_ge(rstd_ready, c - 1)
                        nc.vector.tensor_tensor(out=y[half][:], in0=y[half][:],
                                                in1=rstd[:].rearrange("p (a n) -> p a n", a=1).broadcast_to([P, CG, CH]),
                                                op=ALU.mult).then_inc(normed, 1)
                if conv:
                    dve.wait_ge(chain_v, len(order))
                    dve.sem_clear(chain_v)
                if more:
                    if not first:
                        dve.wait_ge(prod_ready, c * N_PROD)
                    dve.wait_ge(evac_dve, c * CG + CG)
                    nc.vector.tensor_copy(v[1 - half][:, :, 0:HALO], v[half][:, :, CH:CH + HALO]).then_inc(halo_done, 1)
                    dve.wait_ge(halo_done, c + 1)

            split(0, 0)
            step(0, 0, conv=False, finish=False, first=True)
            step(1, 1, finish=False, y_reused=False)
            step(2, 0, y_reused=False)
            step(3, 1)
            with dve.Fori(4, NCH - 2, 2) as c0:
                step(c0, 0)
                step(c0 + 1, 1)
            step(NCH - 2, 0)
            step(NCH - 1, 1, more=False)
            step(NCH, 0, project=False, more=False)
            step(NCH + 1, 1, project=False, conv=False, more=False)

            dve.wait_ge(mod_ps_ready, 4)
            nc.vector.tensor_tensor(out=mod[:, 2 * KD:], in0=mod_ps[:], in1=col[:, COL_BADA + 2 * KD:COL_BADA + 6 * KD],
                                    op=ALU.add).then_inc(chain_v, 1)
            dve.wait_ge(chain_v, 1)
            for which in (GT1, SC2, GT2):
                part = mod[:, which * KD:(which + 1) * KD]
                nc.vector.tensor_scalar(part, part, 1.0, None, ALU.add).then_inc(chain_v, 1)
            dve.wait_ge(chain_v, 4)
            dve.sem_clear(chain_v)

        @block.gpsimd
        def _(pool):
            pool.wait_ge(s_const, 1)

            for s in persist["retired"][0]:
                pool.sem_clear(s)
            pool.wait_ge(s_poolw, 16)
            for g in range(CG):
                nc.gpsimd.tensor_scalar(pool_sum_w[:, g, :], poolw_sb[:, g, :], 1.0 / WINDOWS[g], None, ALU.mult)
            nc.gpsimd.tensor_scalar(pool_p_w[:], poolw_sb[:], -1.0, None, ALU.mult).then_inc(poolw_ready, 1)

            def add(c, half, i, first):
                if i == 1 and not first:
                    pool.wait_ge(yp_used, c - 1)
                pool.wait_ge(prod_ready, c * N_PROD + i + 1)
                if i > 1:
                    pool.wait_ge(sums, c * N_SUM + i - 1)
                so_far = prod[:, 0] if i == 1 else yp[half][:]
                nc.gpsimd.tensor_tensor(out=yp[half][:], in0=so_far, in1=prod[:, i % NPB], op=ALU.add).then_inc(sums, 1)

            def step(c, half, first=False):
                p_now, at = pp[half], lambda g: s_b if g % 2 else s_a
                for i in range(1, 4):
                    add(c, half, i, isinstance(c, int) and c < 2)
                pool.wait_ge(evac_act, c * 2 * CG + 2 * CG)
                pool.sem_inc(paced, 1)
                nc.gpsimd.tensor_copy(pp[1 - half][:, :, 0:PHALO], p_now[:, :, CH:CH + PHALO]).then_inc(p_halo, 1)
                if not first:
                    pool.wait_ge(yb_ready, c * CG)
                done = 0
                for g in range(CG):
                    step_back, start = 1 << g, (1 << (g + 1)) - 1
                    prior = at(g - 1) if g else p_now
                    if g:
                        pool.wait_ge(chain_p, done)
                    nc.gpsimd.tensor_tensor(out=at(g)[:, g:, start:], in0=prior[:, g:, start:],
                                            in1=prior[:, g:, start - step_back:PHALO + CH - step_back],
                                            op=ALU.add).then_inc(chain_p, 1)
                    done += 1
                    for i in range(4 + 2 * g, 6 + 2 * g):
                        add(c, half, i, False)
                pool.wait_ge(chain_p, done)
                for g in range(CG):
                    s_g = at(g)[:, g, PHALO:2 * PHALO]
                    nc.gpsimd.tensor_tensor(out=s_g, in0=s_g, in1=col[:, COL_FIX + g * PHALO:COL_FIX + (g + 1) * PHALO],
                                            op=ALU.mult).then_inc(chain_p, 1)
                done += CG
                pool.wait_ge(chain_p, done)
                nc.gpsimd.memset(col[:, COL_FIX:COL_FIX + CG * PHALO], 1.0).then_inc(chain_p, 1)
                pool.wait_ge(chain_p, done + 1)
                pool.sem_clear(chain_p)
                pool.sem_inc(p_used, 1)
                for i in range(12, N_PROD):
                    add(c, half, i, False)

            step(0, 0, first=True)
            step(1, 1)
            with pool.Fori(2, NCH, 2) as c0:
                step(c0, 0)
                step(c0 + 1, 1)

        @block.tensor
        def _(pe):
            pe.wait_ge(s_const, 1)
            pe.wait_ge(poolw_ready, 1)

            def reduce_ada(which):
                pe.wait_ge(ring_free, (which + 1) * KD)
                for j in range(KD):
                    at = which * KD + j
                    ins = nc.tensor.matmul(mod_ps[:, at:at + 1], acc[which % 2][:, j * P:(j + 1) * P], ones[:, 0:1], start=True, stop=True)
                ins.then_inc(mod_ps_ready, 1)

            def step(c, half, project=True, finish=True, first=False, second=False, first_use=False):
                if finish:
                    pe.wait_ge(p_used, c - 1)
                    for g in range(CG):
                        if g == 0 and not first_use:
                            pe.wait_ge(yb_taken, (c - 2) * CG)
                        out = yb_ps[g % 2][:, g // 2 * CH:(g // 2 + 1) * CH]
                        nc.tensor.matmul(out, pool_sum_w[:, g, :], (s_b if g % 2 else s_a)[:, g, PHALO:], start=True, stop=False)
                        nc.tensor.matmul(out, pool_p_w[:, g, :], pp[half][:, g, PHALO:], start=False, stop=True).then_inc(yb_ready, 1)
                for m in range(NM):
                    if m == 2 and finish:
                        pe.wait_ge(yp_used, c - 1)
                        for g in range(CG):
                            ins = nc.tensor.matmul(stat_ps[:, 0, :], mean_w[:], y[half][:, g, :], start=(g == 0), stop=(g == CG - 1))
                        ins.then_inc(mean_ready, 1)
                    if m == 6 and finish:
                        pe.wait_ge(squared, c - 1)
                        for g in range(CG):
                            ins = nc.tensor.matmul(stat_ps[:, 1, :], mean_w[:], ysq[:, g, :], start=(g == 0), stop=(g == CG - 1))
                        ins.then_inc(var_ready, 1)
                    if not project:
                        continue
                    if m == 0:
                        pe.wait_ge(u_split, c + 1)
                    if m < 4:
                        if not first:
                            pe.wait_ge(evac_act, (c - 1) * 2 * CG + CG + m + 1)
                    elif m % 2:
                        pe.wait_ge(evac_dve, c * CG + (m - 4) // 2 + 1)
                    else:
                        pe.wait_ge(evac_act, c * 2 * CG + (m - 4) // 2 + 1)
                    out = h_ps[m % 4][:, 0:CH]
                    for k in range(KD):
                        w_h, w_l = w_hi[:, k, m * P:(m + 1) * P], w_lo[:, k, m * P:(m + 1) * P]
                        nc.tensor.matmul(out, w_h, u_hi[half][:, k, :], start=(k == 0), stop=False)
                        nc.tensor.matmul(out, w_h, u_lo[half][:, k, :], start=False, stop=False)
                        ins = nc.tensor.matmul(out, w_l, u_hi[half][:, k, :], start=False, stop=(k == KD - 1))
                    ins.then_inc(h_ready, 1)
                    if first and m in (3, 5, 8):
                        reduce_ada((3, 5, 8).index(m))
                    if second and m == 1:
                        reduce_ada(3)

            step(0, 0, finish=False, first=True)
            step(1, 1, finish=False, second=True)
            step(2, 0, first_use=True)
            step(3, 1)
            with pe.Fori(4, NCH, 2) as c0:
                step(c0, 0)
                step(c0 + 1, 1)
            step(NCH, 0, project=False)
            step(NCH + 1, 1, project=False)


def mix_router_phase(nc, persist, x, w_out, rows, w_router, router_bias, w_exp, mix_spill, x1_dram, u2_dram, list_dram, y_dram):
    f32, f32r, bf16, i32 = mybir.dt.float32, mybir.dt.float32r, mybir.dt.bfloat16, mybir.dt.int32
    ALU, ACT, AX = mybir.AluOpType, mybir.ActivationFunctionType, mybir.AxisListType
    ident, mod, paced = persist["ident"], persist["mod"], persist["paced"]
    m1_all, m2_all, w_all, idx_all, run = (persist[n] for n in ("m1_all", "m2_all", "w_all", "idx_all", "run"))

    ctx = ExitStack()
    with ctx:
        sb = lambda name, shape, dt=f32: ctx.enter_context(nc.sbuf_tensor(name, shape, dt))
        ps = lambda name, shape: ctx.enter_context(nc.psum_tensor(name, shape, f32))
        sem = lambda name: ctx.enter_context(nc.semaphore(name))

        stage, stage_in = persist["stage"], persist["stage_in"]
        wo_raw = stage[:, 0:KD, :]
        wo_hi = sb("wo_hi", [P, KD, D], f32r)
        wo_lo = sb("wo_lo", [P, KD, D], f32r)
        g_x1 = sb("g_x1", [P, D])
        b_x1 = sb("b_x1", [P, D])
        g_u2 = sb("g_u2", [P, D])
        b_u2 = sb("b_u2", [P, D])
        b_mix = sb("b_mix", [P, D])
        g1_row = stage[:, KD, :]
        bc = [stage[:, KD + 1 + n, :].rearrange("p (k n) -> p k n", k=KD) for n in range(3)]
        wr = sb("wr", [P, KD, NE])
        rbias = sb("rbias", [P, NE])
        mix_raw = [sb(f"mix_raw{n}", [P, KD, P]) for n in range(2)]
        mix_hi = [sb(f"mix_hi{n}", [P, KD, P], f32r) for n in range(2)]
        mix_lo = [sb(f"mix_lo{n}", [P, KD, P], f32r) for n in range(2)]
        xt = [sb(f"xt{n}", [P, D]) for n in range(2)]
        z = [sb(f"z{n}", [P, D]) for n in range(2)]
        x1 = [sb(f"x1{n}", [P, D]) for n in range(2)]
        u2 = [sb(f"u2{n}", [P, D]) for n in range(2)]
        u2T = sb("u2T", [P, KD, P])
        stats = sb("stats", [P, 2, 6])
        mv = [sb(f"mv{n}", [P, 2]) for n in range(2)]
        root = sb("root", [P, 1])
        rstd = [sb(f"rstd1{n}", [P, 1]) for n in range(2)]
        nmr = [sb(f"nmr{n}", [P, 1]) for n in range(2)]
        eps_col = sb("eps_col1", [P, 1])
        sc = sb("sc", [P, 2, NE])
        score = sb("score", [P, 2, NE])
        sel = sb("sel", [P, 2, NE])
        key = sb("key", [P, 2, NE])
        o1 = sb("o1", [P, 2, NE])
        o2 = sb("o2", [P, 2, NE])
        mb = sb("mb", [P, 2, NE], bf16)
        kd = sb("kd", [P, EPG])
        top1 = sb("top1", [P, 2 * NG])
        top2 = sb("top2", [P, 2 * NG])
        kmax = sb("kmax", [P, 2 * NG])
        gsum = sb("gsum", [P, 2, NG])
        gmax = sb("gmax", [P, 2])
        picked = sb("picked", [P, 2, 2])
        den = sb("den", [P, 2])
        pose = sb("pose", [P, 2, NE])
        idx_i = sb("idx_i", [P, 2, 2], i32)
        tok_f = sb("tok_f", [P, 2])
        tok_i = sb("tok_i", [P, 2], i32)
        tri = sb("tri", [P, P], bf16)
        ones_b = sb("ones_b", [P, P], bf16)
        zero_i = sb("zero_i", [P, NE * SEQ // P], i32)

        mm_ps = [ps(f"mm_ps{n}", [P, D]) for n in range(2)]
        tr_ps = ps("tr_ps", [P, D])
        rt_ps = ps("rt_ps", [P, 512])
        pos_ps = ps("pos_ps", [P, 3, NE])

        s_wo = [sem(f"s_wo{n}") for n in range(KD // 2)]
        s_rows = sem("s_rows")
        s_cst = sem("s_cst")
        s_clear = sem("s_clear")
        s_tri = sem("s_tri")
        s_zero = sem("s_zero")
        s_fill = sem("s_fill")
        bc_ready = sem("bc_ready")
        row_ps = sem("row_ps")
        row_taken = sem("row_taken")
        wo_scaled = sem("wo_scaled")
        wo_scaled_pool = sem("wo_scaled_pool")
        alpha_rows = sem("alpha_rows")
        b_mix_done = sem("b_mix_done")
        wo_h = sem("wo_h")
        wo_done = sem("wo_done")
        mix_in = [sem(f"mix_in{n}") for n in range(2)]
        xt_in = [sem(f"xt_in{n}") for n in range(2)]
        hi_done = sem("hi_done")
        lo_done = sem("lo_done")
        xb_done = sem("xb_done")
        mm_done = sem("mm_done")
        z_done = sem("z_done")
        stat_done = sem("stat_done")
        root_done = sem("root_done")
        rstd_done = sem("rstd_done")
        xa_done = sem("xa_done")
        x1_norm = sem("x1_norm")
        x1_half = sem("x1_half")
        x1_done = sem("x1_done")
        x1_out = [sem(f"x1_out{n}") for n in range(2)]
        nmr_done = sem("nmr_done")
        u2_half = sem("u2_half")
        u2_done = sem("u2_done")
        u2_out = [sem(f"u2_out{n}") for n in range(2)]
        tr_done = sem("tr_done")
        u2T_done = sem("u2T_done")
        logit_done = sem("logit_done")
        sc_done = sem("sc_done")
        sc_taken = sem("sc_taken")
        m_done = sem("m_done")
        pos_done = sem("pos_done")
        idx_done = sem("idx_done")
        scatter = sem("scatter")
        ch = persist["dve_chain"]
        chp = sem("chp")

        block = ctx.enter_context(nc.Block())
        mix_t = mix_spill.rearrange("c p (k h n) -> c h p k n", k=KD, h=TPC)
        x_t = x.rearrange("(t p) d -> t p d", p=P)
        x1_t = x1_dram.rearrange("(t p) d -> t p d", p=P)
        u2_t = u2_dram.rearrange("(t p) d -> t p d", p=P)

        @block.sync
        def _(sp):
            for k in range(KD):
                sp.dma_start(wo_raw[:, k, :], w_out[k]).then_inc(s_wo[k // 2], 16)
            for n, row in enumerate((g_x1, b_x1, b_mix)):
                src = rows[{0: ROW_G1, 1: ROW_B1, 2: ROW_BOUT}[n]:{0: ROW_G1, 1: ROW_B1, 2: ROW_BOUT}[n] + 1, :]
                sp.dma_start(row[:], src.broadcast_to([P, D])).then_inc(s_rows, 16)
            sp.dma_start(rbias[:], router_bias.broadcast_to([P, NE])).then_inc(s_rows, 16)
            sp.dma_start(wr[:], w_router.rearrange("p (k n) -> p k n", k=KD)).then_inc(s_rows, 16)
            for t in range(2):
                sp.dma_start(mix_raw[t][:], mix_t[0, t]).then_inc(mix_in[t], 16)
                sp.dma_start(xt[t][:], x_t[t]).then_inc(xt_in[t], 16)
            sp.wait_ge(s_clear, 1)
            sp.dma_start(list_dram.rearrange("(p n) a -> p (n a)", p=P), zero_i[:]).then_inc(s_zero, 16)

            zeros = zero_i[:].bitcast(f32).rearrange("p (a n) -> p a n", a=1)
            fill = y_dram[NE * P:, :].rearrange("(r p a) (b n) -> r p (a b) n", p=P, r=NT // 2, n=zeros.shape[2])
            sp.dma_start(fill[0], zeros.broadcast_to([P, fill.shape[2], fill.shape[3]])).then_inc(s_fill, 16)
            with sp.Fori(1, NT // 2) as q:
                t0 = q * 2
                for half in range(2):
                    t = t0 + half
                    src_m = mix_t[bass.ds(q, 1), half].rearrange("a p k n -> (a p) k n")
                    src_x = x_t[bass.ds(t, 1)].rearrange("a p d -> (a p) d")
                    sp.wait_ge(lo_done, t - 1)
                    sp.dma_start(mix_raw[half][:], src_m).then_inc(mix_in[half], 16)
                    sp.wait_ge(z_done, t - 1)
                    sp.dma_start(xt[half][:], src_x).then_inc(xt_in[half], 16)
                sp.dma_start(fill[bass.ds(q, 1)].rearrange("r p a n -> (r p) a n"),
                             zeros.broadcast_to([P, fill.shape[2], fill.shape[3]])).then_inc(s_fill, 16)
            sp.wait_ge(wo_done, KD // 2)
            for i in range(NPIECE):
                sp.dma_start(stage[:, i, :], w_exp[0, i]).then_inc(stage_in[i], 16)
            sp.wait_ge(s_zero, 16)
            sp.wait_ge(s_fill, 16 * (NT // 2))

        @block.scalar
        def _(act):
            act.wait_ge(s_cst, 1)
            for n in range(KD // 2):
                act.wait_ge(wo_scaled, n + 1) if n < KD // 2 - 1 else act.wait_ge(wo_scaled_pool, 1)
                nc.scalar.activation(wo_hi[:, 2 * n:2 * n + 2, :], wo_raw[:, 2 * n:2 * n + 2, :], ACT.Copy).then_inc(wo_h, 1)

            def hi(t, half):
                act.wait_ge(mix_in[half], (t // 2) * 16 + 16)
                nc.scalar.activation(mix_hi[half][:], mix_raw[half][:], ACT.Copy).then_inc(hi_done, 1)

            def scale_x(t, half):
                act.wait_ge(xt_in[half], (t // 2) * 16 + 16)
                nc.scalar.activation(xt[half][:], xt[half][:], ACT.Copy, scale=ALPHA).then_inc(xa_done, 1)

            def normalise(t, half, first):
                act.wait_ge(nmr_done, t + 1)
                if not first:
                    act.wait_ge(x1_out[half], (t // 2) * 16)
                nc.scalar.activation(x1[half][:], z[half][:], ACT.Identity, scale=rstd[half][:, 0:1],
                                     bias=nmr[half][:, 0:1]).then_inc(x1_norm, 1)

            def copy_u2T(t, first=False):
                act.wait_ge(tr_done, t + 1)
                if not first:
                    act.wait_ge(logit_done, t)
                nc.scalar.activation(u2T[:], tr_ps[:].rearrange("p (k n) -> p k n", k=KD), ACT.Copy).then_inc(u2T_done, 1)

            def scores(t, half, first=False):
                act.wait_ge(logit_done, t + 1)
                if half == 0 and not first:
                    act.wait_ge(sc_taken, (t // 2))
                nc.scalar.activation(sc[:, half, :], rt_ps[:, 0:NE], ACT.Sigmoid).then_inc(sc_done, 1)

            def step(t, half, more=True):
                first = isinstance(t, int)
                if more:
                    if not (first and t == 0):
                        act.wait_ge(mm_done, t)
                    hi(t + 1, 1 - half)
                    scale_x(t + 1, 1 - half)
                if not (first and t < 2):
                    scores(t - 2, half, first=first and t == 2)
                if not (first and t < 1):
                    copy_u2T(t - 1, first=first and t == 1)
                act.wait_ge(stat_done, t + 1)
                nc.scalar.activation(root[:], mv[half][:, 1:2], ACT.Sqrt, bias=eps_col[:, 0:1]).then_inc(root_done, 1)
                normalise(t, half, first and t < 2)

            hi(0, 0)
            scale_x(0, 0)
            act.wait_ge(row_taken, 2)
            for row in (g_x1, b_x1):
                nc.scalar.activation(row[:], row[:], ACT.Copy, scale=ALPHA).then_inc(alpha_rows, 1)
            for t in range(4):
                step(t, t % 2)
            with act.Fori(2, NT // 2 - 1) as q:
                t0 = q * 2
                step(t0, 0)
                step(t0 + 1, 1)
            step(NT - 2, 0)
            step(NT - 1, 1, more=False)
            scores(NT - 2, 0)
            copy_u2T(NT - 1)
            scores(NT - 1, 1)

        @block.vector
        def _(dve):
            chained = [0]

            def link(ins):
                ins.then_inc(ch, 1)
                chained[0] += 1

            def settle():
                dve.wait_ge(ch, chained[0])

            def reset():
                settle()
                dve.sem_clear(ch)
                chained[0] = 0

            nc.vector.memset(eps_col[:], EPS)
            for n in range(EPG):
                nc.vector.memset(kd[:, n:n + 1], float(EPG - n))
            nc.vector.memset(root[:], 0.0).then_inc(s_cst, 1)
            for n, which in enumerate((GT1, SC2, SH2)):
                nc.vector.tensor_copy(bc[n], mod[:, which * KD:(which + 1) * KD].rearrange("p (k a) -> p k a", a=1)
                                      .broadcast_to([P, KD, P])).then_inc(bc_ready, 1)

            def lo(t, half):
                dve.wait_ge(hi_done, t + 1)
                nc.vector.tensor_tensor(out=mix_lo[half][:], in0=mix_raw[half][:], in1=mix_hi[half][:].bitcast(f32),
                                        op=ALU.subtract).then_inc(lo_done, 1)

            def low_part(n):
                pair = slice(2 * n, 2 * n + 2)
                dve.wait_ge(wo_h, n + 1)
                nc.vector.tensor_tensor(out=wo_lo[:, pair, :], in0=wo_raw[:, pair, :], in1=wo_hi[:, pair, :].bitcast(f32),
                                        op=ALU.subtract).then_inc(wo_done, 1)

            dve.wait_ge(row_ps, 1)
            nc.vector.tensor_copy(g1_row[:], tr_ps[:]).then_inc(row_taken, 1)
            dve.wait_ge(row_taken, 1)
            for n in range(KD // 2):
                pair = slice(2 * n, 2 * n + 2)
                if n < KD // 2 - 1:
                    dve.wait_ge(s_wo[n], 32)
                    nc.vector.tensor_tensor(out=wo_raw[:, pair, :], in0=wo_raw[:, pair, :],
                                            in1=g1_row[:].rearrange("p (a n) -> p a n", a=1).broadcast_to([P, 2, D]),
                                            op=ALU.mult).then_inc(wo_scaled, 1)
                if n:
                    low_part(n - 1)
            low_part(KD // 2 - 1)
            lo(0, 0)
            dve.wait_ge(s_rows, 16 * 5)
            dve.wait_ge(row_ps, 3)
            link(nc.vector.tensor_tensor(out=g_u2[:], in0=mm_ps[1][:], in1=g_x1[:], op=ALU.mult))
            link(nc.vector.tensor_tensor(out=b_u2[:], in0=mm_ps[1][:], in1=b_x1[:], op=ALU.mult))
            settle()
            dve.sem_inc(row_taken, 1)
            link(nc.vector.tensor_tensor(out=b_u2[:], in0=tr_ps[:], in1=b_u2[:], op=ALU.add))
            settle()
            dve.sem_inc(row_taken, 1)
            reset()

            def grouped(ap):
                return ap.rearrange("p a (g e) -> p (a g) e", g=NG)

            def spread_to(ap, n):
                return ap.rearrange("p (a b) -> p a b", b=1).broadcast_to([P, ap.shape[1], n])

            def best(values, top, out):
                link(nc.vector.tensor_reduce(out=top[:], in_=grouped(values[:]), axis=AX.X, op=ALU.max))
                settle()
                link(nc.vector.tensor_tensor(out=grouped(key[:]), in0=grouped(values[:]), in1=spread_to(top[:], EPG), op=ALU.is_ge))
                settle()
                link(nc.vector.tensor_tensor(out=grouped(key[:]), in0=grouped(key[:]),
                                             in1=kd[:].rearrange("p (a e) -> p a e", a=1).broadcast_to([P, 2 * NG, EPG]), op=ALU.mult))
                settle()
                link(nc.vector.tensor_reduce(out=kmax[:], in_=grouped(key[:]), axis=AX.X, op=ALU.max))
                settle()
                link(nc.vector.tensor_tensor(out=grouped(out[:]), in0=grouped(key[:]), in1=spread_to(kmax[:], EPG), op=ALU.is_equal))
                settle()

            def choose(pair):
                dve.wait_ge(sc_done, 2 * pair + 2)
                link(nc.vector.tensor_copy(score[:], sc[:]))
                settle()
                dve.sem_inc(sc_taken, 1)
                link(nc.vector.tensor_tensor(out=sel[:], in0=score[:], in1=rbias[:].rearrange("p (a e) -> p a e", a=1)
                                             .broadcast_to([P, 2, NE]), op=ALU.add))
                settle()
                best(sel, top1, o1)
                link(nc.vector.scalar_tensor_tensor(out=sel[:], in0=o1[:], scalar=-BIG, in1=sel[:], op0=ALU.mult, op1=ALU.add))
                settle()
                best(sel, top2, o2)
                gs = gsum[:].rearrange("p a g -> p (a g)")
                link(nc.vector.tensor_tensor(out=gs, in0=top1[:], in1=top2[:], op=ALU.add))
                settle()
                link(nc.vector.tensor_reduce(out=gmax[:], in_=gsum[:], axis=AX.X, op=ALU.max))
                settle()
                link(nc.vector.tensor_tensor(out=gsum[:], in0=gsum[:], in1=spread_to(gmax[:], NG), op=ALU.is_ge))
                settle()
                link(nc.vector.tensor_tensor(out=gsum[:], in0=gsum[:], in1=kd[:, 0:NG].rearrange("p (a e) -> p a e", a=1)
                                             .broadcast_to([P, 2, NG]), op=ALU.mult))
                settle()
                link(nc.vector.tensor_reduce(out=gmax[:], in_=gsum[:], axis=AX.X, op=ALU.max))
                settle()
                link(nc.vector.tensor_tensor(out=gsum[:], in0=gsum[:], in1=spread_to(gmax[:], NG), op=ALU.is_equal))
                settle()
                link(nc.vector.tensor_tensor(out=grouped(o1[:]), in0=grouped(o1[:]), in1=spread_to(gs, EPG), op=ALU.mult))
                link(nc.vector.tensor_tensor(out=grouped(o2[:]), in0=grouped(o2[:]), in1=spread_to(gs, EPG), op=ALU.mult))
                settle()
                link(nc.vector.tensor_tensor(out=mb[:], in0=o1[:], in1=o2[:], op=ALU.add))
                settle()
                dve.sem_inc(m_done, 1)
                for n, o in enumerate((o1, o2)):
                    link(nc.vector.tensor_tensor(out=key[:], in0=score[:], in1=o[:], op=ALU.mult))
                    settle()
                    link(nc.vector.tensor_reduce(out=picked[:, n, :], in_=key[:], axis=AX.X, op=ALU.add))
                    settle()
                link(nc.vector.tensor_tensor(out=den[:], in0=picked[:, 0, :], in1=picked[:, 1, :], op=ALU.add))
                settle()
                link(nc.vector.reciprocal(den[:], den[:]))
                settle()
                for n in range(2):
                    link(nc.vector.tensor_tensor(out=w_all[:, n, bass.ds(pair * 2, 2)], in0=picked[:, n, :], in1=den[:], op=ALU.mult))

            def place(pair, first=False):
                dve.wait_ge(pos_done, pair + 1)
                link(nc.vector.tensor_tensor(out=pose[:], in0=pos_ps[:, 0:2, :], in1=run[:].rearrange("p (a e) -> p a e", a=1)
                                             .broadcast_to([P, 2, NE]), op=ALU.add))
                settle()
                link(nc.vector.tensor_tensor(out=run[:], in0=run[:], in1=pos_ps[:, 2, :], op=ALU.add))
                if not first:
                    dve.wait_ge(scatter, pair * 64)
                for n, (o, keep) in enumerate(((o1, m1_all), (o2, m2_all))):
                    link(nc.vector.tensor_copy(keep[:, bass.ds(pair * 2, 2), :], o[:]))
                    link(nc.vector.tensor_tensor(out=key[:], in0=pose[:], in1=o[:], op=ALU.mult))
                    settle()
                    link(nc.vector.tensor_reduce(out=picked[:, n, :], in_=key[:], axis=AX.X, op=ALU.add))
                    settle()
                link(nc.vector.tensor_copy(idx_all[:, :, bass.ds(pair * 2, 2)], picked[:]))
                link(nc.vector.tensor_copy(idx_i[:], picked[:]))
                link(nc.vector.tensor_copy(tok_i[:], tok_f[:]))
                settle()
                link(nc.vector.tensor_scalar(tok_f[:], tok_f[:], float(2 * P), None, ALU.add))
                settle()
                dve.sem_inc(idx_done, 1)

            def step(t, half, more=True, first=False, reused=True, choose_pair=None, place_pair=None):
                if more and place_pair is None:
                    if not first:
                        dve.wait_ge(mm_done, t)
                    lo(t + 1, 1 - half)
                dve.wait_ge(xb_done, t + 1)
                dve.wait_ge(mm_done, t + 1)
                if reused:
                    dve.wait_ge(x1_norm, t - 1)
                nc.vector.tensor_tensor(out=z[half][:], in0=mm_ps[half][:], in1=xt[half][:], op=ALU.add).then_inc(z_done, 1)
                dve.wait_ge(z_done, t + 1)
                for n in range(2):
                    link(nc.vector.bn_stats(stats[:, n, :], z[half][:, n * 512:(n + 1) * 512]))
                settle()
                nc.vector.bn_aggr(mv[half][:], stats[:]).then_inc(stat_done, 1)
                dve.wait_ge(stat_done, t + 1)
                if reused:
                    dve.wait_ge(u2_out[half], (t // 2) * 16)
                    dve.wait_ge(tr_done, t - 1)
                nc.vector.scalar_tensor_tensor(out=u2[half][:], in0=z[half][:], scalar=mv[half][:, 0:1], in1=g_u2[:],
                                               op0=ALU.subtract, op1=ALU.mult).then_inc(u2_half, 1)
                dve.wait_ge(root_done, t + 1)
                nc.vector.reciprocal(rstd[half][:], root[:]).then_inc(rstd_done, 1)
                dve.wait_ge(rstd_done, t + 1)
                nc.vector.tensor_scalar(nmr[half][:], mv[half][:, 0:1], rstd[half][:, 0:1], -1.0, ALU.mult, ALU.mult).then_inc(nmr_done, 1)
                dve.wait_ge(u2_half, t + 1)
                nc.vector.scalar_tensor_tensor(out=u2[half][:], in0=u2[half][:], scalar=rstd[half][:, 0:1], in1=b_u2[:],
                                               op0=ALU.mult, op1=ALU.add).then_inc(u2_done, 1)
                if place_pair is not None:
                    place(place_pair, first=isinstance(place_pair, int) and place_pair == 0)
                if choose_pair is not None:
                    if more:
                        lo(t + 2, half)
                    settle()
                    choose(choose_pair)
                reset()

            dve.wait_ge(s_tri, 2)
            step(0, 0, first=True, reused=False)
            step(1, 1, reused=False)
            step(2, 0)
            step(3, 1, choose_pair=0)
            step(4, 0, place_pair=0)
            step(5, 1, choose_pair=1)
            with dve.Fori(3, NT // 2 - 1) as q:
                t0 = q * 2
                step(t0, 0, place_pair=q - 2)
                step(t0 + 1, 1, choose_pair=q - 1)
            step(NT - 2, 0, place_pair=NT // 2 - 3)
            step(NT - 1, 1, more=False, choose_pair=NT // 2 - 2)
            place(NT // 2 - 2)
            settle()
            choose(NT // 2 - 1)
            place(NT // 2 - 1)
            reset()

        @block.gpsimd
        def _(pool):
            for s in persist["retired"][1]:
                pool.sem_clear(s)
            nc.gpsimd.memset(zero_i[:], 0)
            nc.gpsimd.memset(ones_b[:], 1.0)
            nc.gpsimd.memset(tri[:], 1.0)
            for e in range(NE):
                nc.gpsimd.memset(run[:, e:e + 1], float(e * SEQ))
            nc.gpsimd.memset(tok_f[:], 0.0).then_inc(s_clear, 1)
            pool.wait_ge(s_clear, 1)
            nc.gpsimd.affine_select(out=tri[:], in_=tri[:], compare_op=ALU.is_ge, fill=0.0, base=-1,
                                    pattern=[[1, P]], channel_multiplier=-1).then_inc(s_tri, 1)
            nc.gpsimd.iota(tok_i[:], pattern=[[P, 2]], base=0, channel_multiplier=1).then_inc(chp, 1)
            pool.wait_ge(chp, 1)
            nc.gpsimd.tensor_copy(tok_f[:], tok_i[:]).then_inc(s_tri, 1)
            pool.wait_ge(row_taken, 1)
            pool.wait_ge(s_wo[KD // 2 - 1], 32)
            nc.gpsimd.tensor_tensor(out=wo_raw[:, KD - 2:, :], in0=wo_raw[:, KD - 2:, :],
                                    in1=g1_row[:].rearrange("p (a n) -> p a n", a=1).broadcast_to([P, 2, D]),
                                    op=ALU.mult).then_inc(wo_scaled_pool, 1)
            pool.wait_ge(s_rows, 16 * 5)
            nc.gpsimd.tensor_tensor(out=b_mix[:], in0=b_mix[:], in1=g1_row[:], op=ALU.mult).then_inc(b_mix_done, 1)
            pool.wait_ge(b_mix_done, 1)
            pool.wait_ge(s_zero, 16)

            def xb(t, half):
                pool.wait_ge(xa_done, t + 1)
                nc.gpsimd.tensor_tensor(out=xt[half][:], in0=xt[half][:], in1=b_mix[:], op=ALU.add).then_inc(xb_done, 1)

            def send(pair):
                pool.wait_ge(idx_done, pair + 1)
                pool.sem_inc(paced, 1)
                for n in range(2):
                    for half in range(2):
                        nc.gpsimd.indirect_dma_start(out=list_dram, out_offset=bass.IndirectOffsetOnAxis(ap=idx_i[:, n, half:half + 1], axis=0),
                                                     in_=tok_i[:, half:half + 1], in_offset=None).then_inc(scatter, 16)

            def step(t, half, more=True, first=False, route=None):
                if more:
                    xb(t + 1, 1 - half)
                pool.wait_ge(x1_norm, t + 1)
                nc.gpsimd.tensor_tensor(out=x1[half][:], in0=x1[half][:], in1=g_x1[:], op=ALU.mult).then_inc(x1_half, 1)
                pool.wait_ge(x1_half, t + 1)
                nc.gpsimd.tensor_tensor(out=x1[half][:], in0=x1[half][:], in1=b_x1[:], op=ALU.add).then_inc(x1_done, 1)
                dst_x = x1_t[bass.ds(t, 1)].rearrange("a p d -> (a p) d")
                dst_u = u2_t[bass.ds(t, 1)].rearrange("a p d -> (a p) d")
                pool.wait_ge(u2_done, t + 1)
                pool.wait_ge(x1_done, t + 1)
                pool.sem_inc(paced, 1)
                pool.dma_start(dst_u, u2[half][:]).then_inc(u2_out[half], 16)
                pool.dma_start(dst_x, x1[half][:]).then_inc(x1_out[half], 16)
                if route is not None:
                    send(route)

            pool.wait_ge(alpha_rows, 2)
            xb(0, 0)
            step(0, 0, first=True)
            step(1, 1)
            step(2, 0)
            step(3, 1)
            with pool.Fori(2, NT // 2 - 1) as q:
                t0 = q * 2
                step(t0, 0, route=q - 2)
                step(t0 + 1, 1)
            step(NT - 2, 0, route=NT // 2 - 3)
            step(NT - 1, 1, more=False)
            send(NT // 2 - 2)
            send(NT // 2 - 1)
            pool.wait_ge(scatter, 64 * (NT // 2))
            for half in range(2):
                pool.wait_ge(u2_out[half], 16 * NT // 2)
                pool.wait_ge(x1_out[half], 16 * NT // 2)

        @block.tensor
        def _(pe):
            for n, out in enumerate((tr_ps, mm_ps[1], tr_ps)):
                pe.wait_ge(bc_ready, n + 1)
                if n == 2:
                    pe.wait_ge(row_taken, 1)
                for k in range(KD):
                    ins = nc.tensor.matmul(out[:, k * P:(k + 1) * P], bc[n][:, k, :], ident[:], start=True, stop=True)
                ins.then_inc(row_ps, 1)
            pe.wait_ge(wo_done, KD // 2)
            pe.wait_ge(s_tri, 2)

            def product(t, half, part):
                cols = slice(part * 512, (part + 1) * 512)
                out = mm_ps[half][:, cols]
                for k in range(KD):
                    h, l = mix_hi[half][:, k, :], mix_lo[half][:, k, :]
                    nc.tensor.matmul(out, h, wo_hi[:, k, cols], start=(k == 0), stop=False)
                    nc.tensor.matmul(out, h, wo_lo[:, k, cols], start=False, stop=False)
                    ins = nc.tensor.matmul(out, l, wo_hi[:, k, cols], start=False, stop=(k == KD - 1))
                if part:
                    ins.then_inc(mm_done, 1)

            def logits(t, first=False):
                pe.wait_ge(u2T_done, t + 1)
                if not first:
                    pe.wait_ge(sc_done, t)
                for k in range(KD):
                    ins = nc.tensor.matmul(rt_ps[:, 0:NE], u2T[:, k, :], wr[:, k, :], start=(k == 0), stop=(k == KD - 1))
                ins.then_inc(logit_done, 1)

            def transpose(t, half):
                pe.wait_ge(u2_done, t + 1)
                for k in range(KD):
                    ins = nc.tensor.transpose(tr_ps[:, k * P:(k + 1) * P], u2[half][:, k * P:(k + 1) * P], ident[:])
                ins.then_inc(tr_done, 1)

            def step(t, half):
                known = isinstance(t, int)
                pe.wait_ge(lo_done, t + 1)
                if not (known and t < 2):
                    pe.wait_ge(z_done, t - 1)
                product(t, half, 0)
                if not (known and t < 2):
                    logits(t - 2, first=known and t == 2)
                product(t, half, 1)
                if not (known and t < 1):
                    transpose(t - 1, 1 - half)

            def places(pair):
                pe.wait_ge(m_done, pair + 1)
                nc.tensor.matmul(pos_ps[:, 0, :], tri[:], mb[:, 0, :], start=True, stop=True)
                nc.tensor.matmul(pos_ps[:, 1, :], tri[:], mb[:, 1, :], start=True, stop=False)
                nc.tensor.matmul(pos_ps[:, 1, :], ones_b[:], mb[:, 0, :], start=False, stop=True)
                nc.tensor.matmul(pos_ps[:, 2, :], ones_b[:], mb[:, 0, :], start=True, stop=False)
                nc.tensor.matmul(pos_ps[:, 2, :], ones_b[:], mb[:, 1, :], start=False, stop=True).then_inc(pos_done, 1)

            step(0, 0)
            pe.wait_ge(row_taken, 3)
            for t in range(1, 4):
                step(t, t % 2)
            with pe.Fori(2, NT // 2) as q:
                t0 = q * 2
                step(t0, 0)
                places(q - 2)
                step(t0 + 1, 1)
            logits(NT - 2)
            transpose(NT - 1, 1)
            logits(NT - 1)
            places(NT // 2 - 2)
            places(NT // 2 - 1)


NB = NBMAX + 1
UNROLL = 4
NSTEP = -(-NBMAX // UNROLL) * UNROLL + 1
NBUF = 4


def expert_phase(nc, persist, w_exp, rows, x1_dram, u2_dram, list_dram, y_dram):
    f32, f32r, i32 = mybir.dt.float32, mybir.dt.float32r, mybir.dt.int32
    ALU, ACT, AX = mybir.AluOpType, mybir.ActivationFunctionType, mybir.AxisListType
    ident, run, row_base, paced = (persist[n] for n in ("ident", "run", "row_base", "paced"))
    m_all, idx_all = (persist["m1_all"], persist["m2_all"]), persist["idx_all"]
    y_idx, ln_g, ln_b, s_rows, xa, xa_in = (persist[n] for n in ("y_idx", "ln_g", "ln_b", "s_rows", "xa", "xa_in"))

    NTAB = NSTEP + 1

    ctx = ExitStack()
    with ctx:
        sb = lambda name, shape, dt=f32: ctx.enter_context(nc.sbuf_tensor(name, shape, dt))
        ps = lambda name, shape: ctx.enter_context(nc.psum_tensor(name, shape, f32))
        sem = lambda name: ctx.enter_context(nc.semaphore(name))

        stage, stage_in = persist["stage"], persist["stage_in"]
        w_hi = sb("wx_hi", [P, NPIECE, PC], f32r)
        w_lo = sb("wx_lo", [P, NPIECE, PC], f32r)
        xg = [sb(f"xg{n}", [P, D]) for n in range(2)]
        x_hi = sb("xe_hi", [P, KD, P], f32r)
        x_lo = sb("xe_lo", [P, KD, P], f32r)
        sg = sb("sg", [P, DE])
        h = sb("h", [P, DE])
        h_hi = sb("h_hi", [P, KE, P], f32r)
        h_lo = sb("h_lo", [P, KE, P], f32r)
        yo = [sb(f"yo{n}", [P, D]) for n in range(2)]
        warm = sb("warm", [P, 1])
        ids = [sb(f"ids{n}", [P, 1], i32) for n in range(2)]
        iota_i = sb("iota_i", [P, NE], i32)
        iota_e = sb("iota_e", [P, NE])
        slot_i = sb("slot_i", [P, 3], i32)
        slot = sb("slot", [P, 3])
        y_row = sb("y_row", [P, 2, NT])
        cnt, nb, begun, *nb_end = (yo[0][:, n * NE:(n + 1) * NE] for n in range(5))
        cmp = yo[0][:, 5 * NE:8 * NE].rearrange("p (n e) -> p n e", n=3)
        nb_start = sb("nb_start", [P, NE])
        thr = sb("thr", [P, SEQ // P])
        passed = h[:].rearrange("p (e j) -> p e j", e=NE)
        e3 = sb("e3", [P, 3])
        flag = sb("flag", [P, 1])
        cols4 = sb("cols4", [P, 4])
        tab = sb("tab", [1, 4, NTAB], i32)
        tab_mode, tab_e, tab_off, tab_go = (tab[:, n, :] for n in range(4))

        gate_ps = ps("gate_ps", [P, DE])
        up_ps = ps("up_ps", [P, DE])
        hT_ps = ps("hT_ps", [P, KE, P])
        xT_ps = ps("xT_ps", [P, D])
        y_ps = ps("y_ps", [P, D])
        tab_ps = up_ps[0:1, 0:4 * NTAB].rearrange("p (n b) -> p n b", n=4)

        s_iota = sem("s_iota")
        s_warm = sem("s_warm")
        cols_done = sem("cols_done")
        tab_ps_done = sem("tab_ps_done")
        tables = sem("tables")
        hi_done = [sem(f"w_hi_{m}") for m in ("gate", "up", "down")]
        lo_done = [sem(f"w_lo_{m}") for m in ("gate", "up", "down")]
        ids_in = sem("ids_in")
        xg_in = [sem(f"xg_in{n}") for n in range(2)]
        xT_done = sem("xT_done")
        x_hi_done = sem("x_hi_done")
        x_lo_done = sem("x_lo_done")
        gate_done = sem("gate_done")
        silu_done = sem("silu_done")
        up_done = sem("up_done")
        h_done = sem("h_done")
        hT_done = sem("hT_done")
        h_hi_done = sem("h_hi_done")
        h_lo_done = sem("h_lo_done")
        y_done = sem("y_done")
        yo_done = sem("yo_done")
        y_out = [sem(f"y_out{n}") for n in range(2)]
        ch = persist["dve_chain"]

        block = ctx.enter_context(nc.Block())
        y_t = y_dram.rearrange("(b p) d -> b p d", p=P)
        GATE, UP, DOWN = range(3)
        NPM = NPIECE // 3

        def choose(eng, condition, then, otherwise=None):
            with eng.If(condition):
                then()
            with eng.Else():
                otherwise() if otherwise else eng.nop()

        def each_step(eng, step, tail, idle=None, first_step=None, with_modes=True):
            at = lambda b: slice(b, b + 1) if isinstance(b, int) else bass.ds(b, 1)
            mode_of = lambda b: eng.value_load(tab_mode[0:1, at(b)], min_val=0, max_val=3)
            e_of = lambda b: eng.value_load(tab_e[0:1, at(b)], min_val=0, max_val=NE)

            def full(b, half, mode, before):
                last_before = mode_of(before) > 1 if with_modes else None
                step(b, half, e_of(b), mode > 1 if with_modes else None, e_of(before), last_before)
                eng.nop()

            def steps(q, n):
                b, before, half = q * UNROLL + (n + 1), q * UNROLL + n, (n + 1) % 2
                mode = mode_of(b)
                with eng.If(mode > 0):
                    choose(eng, mode < 3, lambda: full(b, half, mode, before), lambda: tail(b, half, e_of(before)))
                    if n + 1 < UNROLL:
                        steps(q, n + 1)
                    eng.nop()
                with eng.Else():
                    if idle:
                        for m in range(n, UNROLL):
                            idle(m % 2)
                    else:
                        eng.nop()

            if first_step:
                first_step()
            eng.wait_ge(tables, 1)
            if not first_step:
                step(0, 0, 0, mode_of(0) > 1, None, None)
            with eng.Fori(0, (NSTEP - 1) // UNROLL) as q:
                steps(q, 0)

        @block.sync
        def _(sp):
            def load(e, matrix, known=False):
                for i in range(matrix * NPM, (matrix + 1) * NPM):
                    src = w_exp[e, i] if known else w_exp[bass.ds(e, 1), i].rearrange("a p n -> (a p) n")
                    sp.wait_ge(lo_done[matrix], (e - 1) * NPM + i % NPM + 1)
                    sp.dma_start(stage[:, i, :], src).then_inc(stage_in[i], 16)

            load(1, GATE, known=True)
            load(1, UP, known=True)
            with sp.Fori(2, NE) as e:
                load(e, GATE)
                load(e, UP)
                load(e - 1, DOWN)
            load(NE - 1, DOWN, known=True)
            for dst, row in ((ln_g, ROW_G2), (ln_b, ROW_B2)):
                sp.dma_start(dst[:], rows[row:row + 1, :].broadcast_to([P, D])).then_inc(s_rows, 16)
            for n in range(NBUF):
                sp.dma_start(xa[n][:], x1_dram.rearrange("(t p) d -> t p d", p=P)[n]).then_inc(xa_in[n], 16)

        @block.gpsimd
        def _(pool):
            nc.gpsimd.iota(iota_i[:], pattern=[[1, NE]], base=0, channel_multiplier=0).then_inc(s_iota, 1)
            for n, base in enumerate((0, 1, -1)):
                nc.gpsimd.iota(slot_i[:, n:n + 1], pattern=[[0, 1]], base=base, channel_multiplier=1).then_inc(s_iota, 1)

            def fetch(b, q, half, at, first=False):
                src = list_dram[0:P, :] if isinstance(at, int) else list_dram[bass.ds(at, P), :]
                if not first:
                    pool.wait_ge(xT_done, b - 1)
                pool.sem_inc(paced, 1)
                pool.dma_start(ids[half][:], src).then_inc(ids_in, 16)
                pool.wait_ge(ids_in, b * 16 + 16)
                pool.sem_inc(paced, 1)
                nc.gpsimd.indirect_dma_start(out=xg[half][:], out_offset=None, in_=u2_dram,
                                             in_offset=bass.IndirectOffsetOnAxis(ap=ids[half][:, 0:1], axis=0)).then_inc(xg_in[half], 16)

            fetch(0, 0, 0, 0, first=True)
            pool.wait_ge(tables, 1)
            fetch(1, 0, 1, pool.value_load(tab_off[0:1, 1:2], min_val=0, max_val=NE * SEQ - P), first=True)
            with pool.Fori(1, NB // 2) as q:
                for half in range(2):
                    b = q * 2 + half
                    go = pool.value_load(tab_go[0:1, bass.ds(b, 1)], min_val=0, max_val=1)
                    choose(pool, go > 0, lambda: fetch(b, q, half, pool.value_load(tab_off[0:1, bass.ds(b, 1)], min_val=0,
                                                                                   max_val=NE * SEQ - P)))

        @block.scalar
        def _(act):
            def split_hi(e, matrix):
                for i in range(matrix * NPM, (matrix + 1) * NPM):
                    act.wait_ge(stage_in[i], e * 16 + 16)
                    nc.scalar.activation(w_hi[:, i, :], stage[:, i, :], ACT.Copy).then_inc(hi_done[matrix], 1)

            def x_high(b):
                act.wait_ge(xT_done, b + 1)
                nc.scalar.activation(x_hi[:], xT_ps[:].rearrange("p (k n) -> p k n", k=KD), ACT.Copy).then_inc(x_hi_done, 1)

            def h_high(b):
                act.wait_ge(hT_done, b + 1)
                nc.scalar.activation(h_hi[:], hT_ps[:], ACT.Copy).then_inc(h_hi_done, 1)

            def store(b, half):
                dst = y_t[bass.ds(b, 1)].rearrange("a p d -> (a p) d")
                act.wait_ge(y_done, b + 1)
                act.wait_ge(y_out[half], (b - half) * 8 + 16)
                nc.scalar.activation(yo[half][:], y_ps[:], ACT.Copy).then_inc(yo_done, 1)
                act.wait_ge(yo_done, b + 2)
                act.dma_start(dst, yo[half][:]).then_inc(y_out[half], 16)

            def step(b, half, e, last, e_before, last_before):
                act.wait_ge(gate_done, b + 1)
                if last_before is not None:
                    act.wait_ge(h_done, b)
                nc.scalar.activation(sg[:], gate_ps[:], ACT.Silu).then_inc(silu_done, 1)
                if last_before is not None:
                    h_high(b - 1)
                choose(act, last, lambda: split_hi(e + 1, GATE))
                act.wait_ge(up_done, b + 1)
                x_high(b + 1)
                choose(act, last, lambda: split_hi(e + 1, UP))
                if last_before is not None:
                    store(b - 1, 1 - half)
                    choose(act, last_before, lambda: split_hi(e, DOWN))

            def tail(b, half, e_before):
                h_high(b - 1)
                store(b - 1, 1 - half)

            act.wait_ge(s_warm, 1)
            nc.scalar.activation(warm[:], warm[:], ACT.Silu).then_inc(s_warm, 1)
            act.sem_inc(yo_done, 1)
            for half in range(2):
                act.sem_inc(y_out[half], 16)
            split_hi(0, GATE)
            x_high(0)
            split_hi(0, UP)
            split_hi(0, DOWN)
            each_step(act, step, tail, lambda half: act.sem_inc(y_out[half], 16))
            for half in range(2):
                act.wait_ge(y_out[half], 16 * ((NSTEP - 1) // 2 + 1))

        @block.vector
        def _(dve):
            chained = [0]

            def link(ins):
                ins.then_inc(ch, 1)
                chained[0] += 1
                dve.wait_ge(ch, chained[0])

            def split_lo(e, matrix):
                for i in range(matrix * NPM, (matrix + 1) * NPM):
                    dve.wait_ge(hi_done[matrix], e * NPM + i % NPM + 1)
                    nc.vector.tensor_tensor(out=w_lo[:, i, :], in0=stage[:, i, :], in1=w_hi[:, i, :].bitcast(f32),
                                            op=ALU.subtract).then_inc(lo_done[matrix], 1)

            def x_low(b):
                dve.wait_ge(x_hi_done, b + 1)
                nc.vector.tensor_tensor(out=x_lo[:], in0=xT_ps[:].rearrange("p (k n) -> p k n", k=KD), in1=x_hi[:].bitcast(f32),
                                        op=ALU.subtract).then_inc(x_lo_done, 1)

            def h_low(b):
                dve.wait_ge(h_hi_done, b + 1)
                nc.vector.tensor_tensor(out=h_lo[:], in0=hT_ps[:], in1=h_hi[:].bitcast(f32), op=ALU.subtract).then_inc(h_lo_done, 1)

            nc.vector.memset(warm[:], 0.0).then_inc(s_warm, 1)
            split_lo(0, GATE)
            x_low(0)
            for j in range(SEQ // P):
                ins = nc.vector.memset(thr[:, j:j + 1], float(P * (j + 1)))
            link(ins)
            dve.wait_ge(s_iota, 4)
            nc.vector.tensor_copy(slot[:], slot_i[:]).then_inc(ch, 1)
            chained[0] += 1
            link(nc.vector.tensor_copy(iota_e[:], iota_i[:]))
            link(nc.vector.scalar_tensor_tensor(out=cnt, in0=iota_e[:], scalar=-float(SEQ), in1=run[:], op0=ALU.mult, op1=ALU.add))
            link(nc.vector.tensor_tensor(out=passed, in0=cnt.rearrange("p (e a) -> p e a", a=1).broadcast_to([P, NE, SEQ // P]),
                                         in1=thr[:].rearrange("p (a j) -> p a j", a=1).broadcast_to([P, NE, SEQ // P]), op=ALU.is_gt))
            link(nc.vector.tensor_reduce(out=nb, in_=passed, axis=AX.X, op=ALU.add))
            link(nc.vector.tensor_scalar(nb, nb, 1.0, None, ALU.add))
            src = nb
            for lvl in range(5):
                dst, s = nb_end[lvl % 2], 1 << lvl
                link(nc.vector.tensor_copy(dst[:, 0:s], src[:, 0:s]))
                link(nc.vector.tensor_tensor(out=dst[:, s:], in0=src[:, s:], in1=src[:, 0:NE - s], op=ALU.add))
                src = dst
            end = src
            link(nc.vector.tensor_tensor(out=nb_start[:], in0=end, in1=nb, op=ALU.subtract))
            link(nc.vector.tensor_tensor(out=cmp, in0=end.rearrange("p (a e) -> p a e", a=1).broadcast_to([P, 3, NE]),
                                         in1=slot[:].rearrange("p (a b) -> p a b", b=1).broadcast_to([P, 3, NE]), op=ALU.is_le))
            link(nc.vector.tensor_reduce(out=e3[:], in_=cmp, axis=AX.X, op=ALU.add))
            mode, e_of, off, go = (cols4[:, n:n + 1] for n in range(4))
            link(nc.vector.tensor_copy(e_of, e3[:, 0:1]))
            link(nc.vector.tensor_tensor(out=begun, in0=nb_start[:], in1=slot[:, 0:1].broadcast_to([P, NE]), op=ALU.is_le))
            link(nc.vector.tensor_tensor(out=begun, in0=begun, in1=nb_start[:], op=ALU.mult))
            link(nc.vector.tensor_reduce(out=off, in_=begun, axis=AX.X, op=ALU.max))
            link(nc.vector.tensor_tensor(out=off, in0=slot[:, 0:1], in1=off, op=ALU.subtract))
            link(nc.vector.tensor_scalar(off, off, float(P), None, ALU.mult))
            link(nc.vector.scalar_tensor_tensor(out=off, in0=e_of, scalar=float(SEQ), in1=off, op0=ALU.mult, op1=ALU.add))
            link(nc.vector.tensor_scalar(flag[:], e_of, float(NE - 1), None, ALU.is_le))
            link(nc.vector.tensor_tensor(out=off, in0=off, in1=flag[:], op=ALU.mult))
            link(nc.vector.tensor_tensor(out=mode, in0=e3[:, 1:2], in1=e_of, op=ALU.is_gt))
            link(nc.vector.scalar_tensor_tensor(out=mode, in0=e_of, scalar=float(NE - 2), in1=mode, op0=ALU.is_le, op1=ALU.mult))
            link(nc.vector.tensor_tensor(out=mode, in0=mode, in1=flag[:], op=ALU.add))
            link(nc.vector.tensor_scalar(go, e3[:, 2:3], float(NE - 1), None, ALU.is_le))
            link(nc.vector.tensor_tensor(out=flag[:], in0=go, in1=flag[:], op=ALU.subtract))
            link(nc.vector.scalar_tensor_tensor(out=mode, in0=flag[:], scalar=3.0, in1=mode, op0=ALU.mult, op1=ALU.add))
            dve.sem_inc(cols_done, 1)
            dve.wait_ge(tab_ps_done, 1)
            link(nc.vector.tensor_copy(tab[:], tab_ps))
            dve.sem_inc(tables, 1)
            link(nc.vector.tensor_scalar(row_base[:], nb_start[:], float(P), None, ALU.mult))
            link(nc.vector.scalar_tensor_tensor(out=row_base[:], in0=iota_e[:], scalar=-float(SEQ), in1=row_base[:],
                                                op0=ALU.mult, op1=ALU.add))
            dve.sem_clear(ch)

            def step(b, half, e, last, e_before, last_before):
                if last_before is not None:
                    h_low(b - 1)
                choose(dve, last, lambda: split_lo(e + 1, GATE))
                dve.wait_ge(silu_done, b + 1)
                dve.wait_ge(up_done, b + 1)
                if last_before is not None:
                    dve.wait_ge(hT_done, b)
                nc.vector.tensor_tensor(out=h[:], in0=up_ps[:], in1=sg[:], op=ALU.mult).then_inc(h_done, 1)
                x_low(b + 1)
                choose(dve, last, lambda: split_lo(e + 1, UP))
                if last_before is not None:
                    choose(dve, last_before, lambda: split_lo(e, DOWN))

            split_lo(0, UP)
            split_lo(0, DOWN)
            each_step(dve, step, lambda b, half, e_before: h_low(b - 1))

            chained[0] = 0
            prod = h[:].rearrange("p (t e) -> p t e", t=NT)
            for j in range(2):
                link(nc.vector.tensor_tensor(out=prod, in0=m_all[j][:], in1=row_base[:].rearrange("p (a e) -> p a e", a=1)
                                             .broadcast_to([P, NT, NE]), op=ALU.mult))
                link(nc.vector.tensor_reduce(out=y_row[:, j, :], in_=prod, axis=AX.X, op=ALU.add))
            link(nc.vector.tensor_tensor(out=y_row[:], in0=y_row[:], in1=idx_all[:], op=ALU.add))
            link(nc.vector.tensor_copy(y_idx[:], y_row[:]))
            dve.sem_clear(ch)

        @block.tensor
        def _(pe):
            def transpose_x(b, half, q):
                pe.wait_ge(xg_in[half], q * 16 + 16)
                for k in range(KD):
                    ins = nc.tensor.transpose(xT_ps[:, k * P:(k + 1) * P], xg[half][:, k * P:(k + 1) * P], ident[:])
                ins.then_inc(xT_done, 1)

            def transpose_h(b):
                pe.wait_ge(h_done, b + 1)
                for k in range(KE):
                    ins = nc.tensor.transpose(hT_ps[:, k, :], h[:, k * P:(k + 1) * P], ident[:])
                ins.then_inc(hT_done, 1)

            def project(out, matrix, e, done):
                for k in range(KD):
                    if k % 2 == 0:
                        pe.wait_ge(lo_done[matrix], e * NPM + k // 2 + 1)
                    i, at = matrix * NPM + k // 2, slice(k % 2 * DE, (k % 2 + 1) * DE)
                    nc.tensor.matmul(out, x_hi[:, k, :], w_hi[:, i, at], start=(k == 0), stop=False)
                    nc.tensor.matmul(out, x_hi[:, k, :], w_lo[:, i, at], start=False, stop=False)
                    ins = nc.tensor.matmul(out, x_lo[:, k, :], w_hi[:, i, at], start=False, stop=(k == KD - 1))
                ins.then_inc(done, 1)

            def project_down(b, e):
                pe.wait_ge(h_lo_done, b + 1)
                pe.wait_ge(yo_done, b + 1)
                for k in range(KE):
                    pe.wait_ge(lo_done[DOWN], e * NPM + k + 1)
                    for part in range(2):
                        at = slice(part * 512, (part + 1) * 512)
                        nc.tensor.matmul(y_ps[:, at], h_hi[:, k, :], w_hi[:, 2 * NPM + k, at], start=(k == 0), stop=False)
                        nc.tensor.matmul(y_ps[:, at], h_hi[:, k, :], w_lo[:, 2 * NPM + k, at], start=False, stop=False)
                        ins = nc.tensor.matmul(y_ps[:, at], h_lo[:, k, :], w_hi[:, 2 * NPM + k, at], start=False, stop=(k == KE - 1))
                ins.then_inc(y_done, 1)

            def step(b, half, e, last, e_before, last_before):
                pe.wait_ge(x_lo_done, b + 1)
                pe.wait_ge(silu_done, b)
                project(gate_ps[:], GATE, e, gate_done)
                transpose_h(b - 1)
                transpose_x(b + 1, 1 - half, (b + half) // 2)
                project(up_ps[:], UP, e, up_done)
                project_down(b - 1, e_before)

            def tail(b, half, e_before):
                transpose_h(b - 1)
                project_down(b - 1, e_before)

            def first_step():
                pe.wait_ge(x_lo_done, 1)
                project(gate_ps[:], GATE, 0, gate_done)
                pe.wait_ge(cols_done, 1)
                for n in range(4):
                    ins = nc.tensor.matmul(tab_ps[:, n, :], cols4[0:NTAB, n:n + 1], ident[0:NTAB, 0:NTAB], start=True, stop=True)
                ins.then_inc(tab_ps_done, 1)
                pe.wait_ge(tables, 1)
                project(up_ps[:], UP, 0, up_done)
                transpose_x(1, 1, 0)

            transpose_x(0, 0, 0)
            each_step(pe, step, tail, first_step=first_step, with_modes=False)


def combine_phase(nc, persist, x1_dram, y_dram, out):
    f32, i32 = mybir.dt.float32, mybir.dt.int32
    ALU, ACT, AX = mybir.AluOpType, mybir.ActivationFunctionType, mybir.AxisListType
    ident, mod, paced = persist["ident"], persist["mod"], persist["paced"]
    w_all, y_idx, ln_g, ln_b, s_rows, xa, xa_in = (persist[n] for n in ("w_all", "y_idx", "ln_g", "ln_b", "s_rows", "xa", "xa_in"))

    ctx = ExitStack()
    with ctx:
        sb = lambda name, shape, dt=f32: ctx.enter_context(nc.sbuf_tensor(name, shape, dt))
        sem = lambda name: ctx.enter_context(nc.semaphore(name))
        bc = sb("bc2", [P, KD, P])
        g2_row = sb("g2_row", [P, D])
        ya = [sb(f"ya{n}", [P, D]) for n in range(NBUF)]
        yb = [sb(f"yb{n}", [P, D]) for n in range(NBUF)]
        zo = [sb(f"zo{n}", [P, D]) for n in range(NBUF)]
        stats = sb("stats2", [P, 2, 6])
        mv = [sb(f"mv2{n}", [P, 2]) for n in range(2)]
        root = sb("root2", [P, 1])
        rstd = [sb(f"rstd2{n}", [P, 1]) for n in range(2)]
        nmr = [sb(f"nmr2{n}", [P, 1]) for n in range(2)]
        eps_col = sb("eps2", [P, 1])
        diag = [[sb(f"diag{n}{j}", [P, P]) for j in range(2)] for n in range(NBUF)]
        row_ps = ctx.enter_context(nc.psum_tensor("row_ps", [P, D], f32))
        f_ps = [ctx.enter_context(nc.psum_tensor(f"f_ps{n}", [P, D], f32)) for n in range(2)]

        s_bc = sem("s_bc2")
        s_row = sem("s_row2")
        ya_in = [sem(f"ya_in{n}") for n in range(NBUF)]
        yb_in = [sem(f"yb_in{n}") for n in range(NBUF)]
        diag_done = sem("diag_done")
        f_done = sem("f_done")
        fg_done = sem("fg_done")
        z_done = sem("z_done2")
        stat_done = sem("stat_done2")
        root_done = sem("root_done2")
        rstd_done = sem("rstd_done2")
        n_norm = sem("n_norm")
        nmr_done = sem("nmr_done2")
        n_half = sem("n_half")
        n_done = sem("n_done")
        stored = [sem(f"stored{n}") for n in range(NBUF)]
        ch = persist["dve_chain"]
        block = ctx.enter_context(nc.Block())
        x1_t = x1_dram.rearrange("(t p) d -> t p d", p=P)
        out_t = out.rearrange("(t p) d -> t p d", p=P)

        @block.sync
        def _(sp):
            with sp.Fori(1, NT // NBUF) as r:
                for n in range(NBUF):
                    src = x1_t[bass.ds(r * NBUF + n, 1)].rearrange("a p d -> (a p) d")
                    sp.wait_ge(z_done, (r - 1) * NBUF + n + 1)
                    sp.dma_start(xa[n][:], src).then_inc(xa_in[n], 16)

        def gain(pool, t):
            n = t % NBUF
            pool.wait_ge(n_norm, t + 1)
            nc.gpsimd.tensor_tensor(out=zo[n][:], in0=zo[n][:], in1=ln_g[:], op=ALU.mult).then_inc(n_half, 1)

        @block.gpsimd
        def _(pool):
            def gather(t):
                n = t % NBUF
                if t >= NBUF:
                    pool.wait_ge(f_done, t - NBUF + 1)
                for j, dst, s in ((0, ya[n], ya_in[n]), (1, yb[n], yb_in[n])):
                    nc.gpsimd.indirect_dma_start(out=dst[:], out_offset=None, in_=y_dram,
                                                 in_offset=bass.IndirectOffsetOnAxis(ap=y_idx[:, j, t:t + 1], axis=0)).then_inc(s, 16)

            for t in range(NBUF):
                gather(t)
            for t in range(NT):
                if t + NBUF < NT:
                    gather(t + NBUF)
                gain(pool, t)

        @block.scalar
        def _(act):
            def weights(t):
                if t >= NBUF:
                    act.wait_ge(f_done, t - NBUF + 1)
                for j in range(2):
                    ins = nc.scalar.activation(diag[t % NBUF][j][:], ident[:], ACT.Copy, scale=w_all[:, j, t:t + 1])
                ins.then_inc(diag_done, 1)

            for t in range(NBUF - 1):
                weights(t)
            for t in range(NT):
                n = t % NBUF
                if t + NBUF - 1 < NT:
                    weights(t + NBUF - 1)
                act.wait_ge(stat_done, t + 1)
                if t:
                    act.wait_ge(rstd_done, t)
                nc.scalar.activation(root[:], mv[t % 2][:, 1:2], ACT.Sqrt, bias=eps_col[:, 0:1]).then_inc(root_done, 1)
                act.wait_ge(nmr_done, t + 1)
                nc.scalar.activation(zo[n][:], zo[n][:], ACT.Identity, scale=rstd[t % 2][:, 0:1],
                                     bias=nmr[t % 2][:, 0:1]).then_inc(n_norm, 1)
                if t:
                    act.wait_ge(n_done, t)
                    act.dma_start(out_t[t - 1], zo[(t - 1) % NBUF][:]).then_inc(stored[(t - 1) % NBUF], 16)
            act.wait_ge(n_done, NT)
            act.dma_start(out_t[NT - 1], zo[(NT - 1) % NBUF][:]).then_inc(stored[(NT - 1) % NBUF], 16)
            for n in range(NBUF):
                act.wait_ge(stored[n], 16 * NT // NBUF)

        @block.vector
        def _(dve):
            chained = [0]

            def link(ins):
                ins.then_inc(ch, 1)
                chained[0] += 1
                dve.wait_ge(ch, chained[0])

            link(nc.vector.memset(eps_col[:], EPS))
            nc.vector.tensor_copy(bc[:], mod[:, GT2 * KD:(GT2 + 1) * KD].rearrange("p (k a) -> p k a", a=1)
                                  .broadcast_to([P, KD, P])).then_inc(s_bc, 1)
            dve.wait_ge(s_row, 1)
            link(nc.vector.tensor_copy(g2_row[:], row_ps[:]))
            dve.wait_ge(s_rows, 32)

            def bias(t):
                n = t % NBUF
                dve.wait_ge(n_half, t + 1)
                nc.vector.tensor_tensor(out=zo[n][:], in0=zo[n][:], in1=ln_b[:], op=ALU.add).then_inc(n_done, 1)

            for t in range(NT):
                n = t % NBUF
                dve.wait_ge(f_done, t + 1)
                if t >= NBUF:
                    dve.wait_ge(stored[n], 16 * (t // NBUF))
                nc.vector.tensor_tensor(out=zo[n][:], in0=f_ps[t % 2][:], in1=g2_row[:], op=ALU.mult).then_inc(fg_done, 1)
                dve.wait_ge(fg_done, t + 1)
                dve.wait_ge(xa_in[n], 16 * (t // NBUF + 1))
                nc.vector.tensor_tensor(out=zo[n][:], in0=zo[n][:], in1=xa[n][:], op=ALU.add).then_inc(z_done, 1)
                dve.wait_ge(z_done, t + 1)
                for part in range(2):
                    nc.vector.bn_stats(stats[:, part, :], zo[n][:, part * 512:(part + 1) * 512]).then_inc(ch, 1)
                chained[0] += 2
                dve.wait_ge(ch, chained[0])
                if t >= 2:
                    dve.wait_ge(n_norm, t - 1)
                nc.vector.bn_aggr(mv[t % 2][:], stats[:]).then_inc(stat_done, 1)
                dve.wait_ge(root_done, t + 1)
                nc.vector.reciprocal(rstd[t % 2][:], root[:]).then_inc(rstd_done, 1)
                dve.wait_ge(rstd_done, t + 1)
                nc.vector.tensor_scalar(nmr[t % 2][:], mv[t % 2][:, 0:1], rstd[t % 2][:, 0:1], -1.0, ALU.mult, ALU.mult).then_inc(nmr_done, 1)
                if t:
                    bias(t - 1)
            bias(NT - 1)

        @block.tensor
        def _(pe):
            pe.wait_ge(s_bc, 1)
            for k in range(KD):
                ins = nc.tensor.matmul(row_ps[:, k * P:(k + 1) * P], bc[:, k, :], ident[:], start=True, stop=True)
            ins.then_inc(s_row, 1)
            for t in range(NT):
                n = t % NBUF
                pe.wait_ge(diag_done, t + 1)
                pe.wait_ge(ya_in[n], 16 * (t // NBUF + 1))
                pe.wait_ge(yb_in[n], 16 * (t // NBUF + 1))
                if t >= 2:
                    pe.wait_ge(fg_done, t - 1)
                for part in range(2):
                    at = slice(part * 512, (part + 1) * 512)
                    nc.tensor.matmul(f_ps[t % 2][:, at], diag[n][0][:], ya[n][:, at], start=True, stop=False)
                    ins = nc.tensor.matmul(f_ps[t % 2][:, at], diag[n][1][:], yb[n][:, at], start=False, stop=True)
                ins.then_inc(f_done, 1)


def hybrid_block(nc, x, xT, w_ada, cols, w_in, pool_w, w_out, rows, w_router, router_bias, w_exp, out):
    f32 = mybir.dt.float32
    scratch = lambda name, shape, dt=f32: nc.dram_tensor(name, shape, dt).ap()
    mix_spill = scratch("mix_spill", (NCH, P, KD * CH))
    x1_dram = scratch("x1_dram", (SEQ, D))
    u2_dram = scratch("u2_dram", (SEQ, D))
    y_dram = scratch("y_dram", (NB * P, D))
    list_dram = scratch("list_dram", (NE * SEQ, 1), mybir.dt.int32)
    ctx = ExitStack()
    with ctx:
        persist = {name: ctx.enter_context(nc.sbuf_tensor(name, shape, f32)) for name, shape in (
            ("ident", [P, P]), ("mod", [P, 6 * KD]))}
        persist["retired"] = [], []
        persist["dve_chain"] = ctx.enter_context(nc.semaphore("dve_chain"))
        persist["paced"] = ctx.enter_context(nc.semaphore("paced"))
        with ExitStack() as front:
            col = front.enter_context(nc.sbuf_tensor("col", [P, NCOL], f32))
            w_hi, w_lo = (front.enter_context(nc.sbuf_tensor(name, [P, KD, NIN], mybir.dt.float32r)) for name in ("w_in_hi", "w_in_lo"))
            cact = front.enter_context(nc.sbuf_tensor("cact", [P, KD], f32))
            ones = front.enter_context(nc.sbuf_tensor("ones", [P, 1], f32))
            persist_front = {**persist, "col": col, "cact": cact, "ones": ones}
            modulation_phase(nc, persist_front, w_hi, w_lo, w_ada, cols, w_in)
            conv_pool_phase(nc, persist_front, w_hi, w_lo, w_ada, xT, pool_w, mix_spill)
        persist |= {name: ctx.enter_context(nc.sbuf_tensor(name, shape, f32)) for name, shape in (
            ("m1_all", [P, NT, NE]), ("m2_all", [P, NT, NE]), ("w_all", [P, 2, NT]), ("idx_all", [P, 2, NT]),
            ("run", [P, NE]), ("row_base", [P, NE]), ("stage", [P, NPIECE, PC]))}
        persist["stage_in"] = [ctx.enter_context(nc.semaphore(f"stage_in{n}")) for n in range(NPIECE)]
        mix_router_phase(nc, persist, x, w_out, rows, w_router, router_bias, w_exp, mix_spill, x1_dram, u2_dram, list_dram, y_dram)
        persist |= {name: ctx.enter_context(nc.sbuf_tensor(name, shape, dt)) for name, shape, dt in (
            ("y_idx", [P, 2, NT], mybir.dt.int32), ("ln_g", [P, D], f32), ("ln_b", [P, D], f32))}
        persist["xa"] = [ctx.enter_context(nc.sbuf_tensor(f"xa{n}", [P, D], f32)) for n in range(NBUF)]
        persist["s_rows"] = ctx.enter_context(nc.semaphore("s_rows2"))
        persist["xa_in"] = [ctx.enter_context(nc.semaphore(f"xa_in{n}")) for n in range(NBUF)]
        expert_phase(nc, persist, w_exp, rows, x1_dram, u2_dram, list_dram, y_dram)
        combine_phase(nc, persist, x1_dram, y_dram, out)


def lay_out(a):
    import numpy as np
    x = np.asarray(a["x"])[0]
    col = np.zeros((P, NCOL), np.float32)
    col[:, COL_BADA:COL_BIN] = np.asarray(a["b_ada"])[0].reshape(6 * KD, P).T
    order = [b for j in range(CG) for b in (CG + j, j)] + list(range(2 * CG, NM))
    col[:, COL_BIN:COL_CONVW] = np.asarray(a["b_in"])[0].reshape(NM, P)[order].T
    col[:, COL_CONVW:COL_CONVB] = np.asarray(a["conv_w"])[0].reshape(TAPS, CG, P).transpose(2, 1, 0).reshape(P, CG * TAPS)
    for at, name in ((COL_CONVB, "conv_b"), (COL_LNG, "conv_ln_g"), (COL_LNB, "conv_ln_b"), (COL_PSC, "pool_scale")):
        col[:, at:at + CG] = np.asarray(a[name])[0].reshape(CG, P).T
    col[:, COL_C:COL_FIX] = np.asarray(a["c"])[0].reshape(KD, P).T
    col[:, COL_FIX:] = np.concatenate([[w / min(t + 1, w) for t in range(PHALO)] for w in WINDOWS]).astype(np.float32)
    w_in = np.asarray(a["w_in"])[0].reshape(KD, P, NM, P)[:, :, order].transpose(1, 0, 2, 3)
    w_in = w_in.reshape(P, KD * NIN // PC, PC).transpose(1, 0, 2)
    gate, up = (np.asarray(a[n])[0].reshape(NE, KD, P, DE).transpose(0, 2, 1, 3).reshape(NE, P, 4, PC) for n in ("w_gate", "w_up"))
    down = np.asarray(a["w_down"])[0].reshape(NE, KE, P, D).transpose(0, 2, 1, 3)
    w_exp = np.empty((NE, NPIECE, P, PC), np.float32)
    for at, part in ((0, gate), (4, up), (8, down)):
        w_exp[:, at:at + 4] = part.transpose(0, 2, 1, 3)
    return {
        "x": x,
        "xT": x.reshape(NCH, CH, KD, P).transpose(0, 3, 2, 1).reshape(NCH, P, KD * CH),
        "w_ada": np.asarray(a["w_ada"])[0].reshape(KD, P, 6, PC).transpose(2, 0, 1, 3).reshape(6 * KD, P, PC),
        "cols": col,
        "w_in": w_in,
        "pool_w": np.asarray(a["pool_w"])[0].transpose(1, 0, 2).reshape(P, CG * P),
        "w_out": np.asarray(a["w_out"])[0].reshape(KD, P, D),
        "rows": np.stack([np.asarray(a[n])[0] for n in ("b_out", "ln1_g", "ln1_b", "ln2_g", "ln2_b")]),
        "w_router": np.asarray(a["w_router"]).reshape(KD, P, NE).transpose(1, 0, 2).reshape(P, KD * NE),
        "router_bias": np.asarray(a["router_bias"]).reshape(1, NE),
        "w_exp": w_exp,
    }


_INS = ("x", "xT", "w_ada", "cols", "w_in", "pool_w", "w_out", "rows", "w_router", "router_bias", "w_exp")


def kernel(**inputs):
    import numpy as np
    import concourse.bacc as bacc
    from concourse.bass_utils import run_bass_kernel_spmd
    laid = lay_out(inputs)
    nc = bacc.Bacc("TRN2", target_bir_lowering=False, num_devices=1)
    arrays, args = {}, []
    for name in _INS:
        a = np.ascontiguousarray(laid[name])
        arrays[f"in_{name}"] = a
        args.append(nc.dram_tensor(f"in_{name}", a.shape, mybir.dt.from_np(a.dtype), kind="ExternalInput").ap())
    out = nc.dram_tensor("out", (SEQ, D), mybir.dt.float32, kind="ExternalOutput").ap()
    hybrid_block(nc, *args, out)
    got = run_bass_kernel_spmd(nc, [arrays], core_ids=[0]).results[0]["out"]
    return got.reshape(1, SEQ, D)
```
